# Optimizing a Trainium2 kernel written in Bass

```python
import jax, jax.numpy as jnp
from jax import lax
import numpy as np
import math

D_MODEL = 1024
BATCH = 1
SEQ = 512
DEPTH = 1

D_MIX = D_MODEL
HEAD_DIM = 64
ATTN_WIDTH = D_MIX // 2
CONV_WIDTH = D_MIX - ATTN_WIDTH
N_HEADS = ATTN_WIDTH // HEAD_DIM
N_KV_HEADS = 2
GQA_GROUP = N_HEADS // N_KV_HEADS
KV_WIDTH = N_KV_HEADS * HEAD_DIM
N_CONV_GROUPS = CONV_WIDTH // HEAD_DIM
WINDOW = 128
CONV_K = 3
IN_WIDTH = ATTN_WIDTH + 2 * KV_WIDTH + 3 * CONV_WIDTH
N_KEYS = 128
N_EXPERTS = N_KEYS * N_KEYS
PEER_HEADS = 8
PEER_TOPK = 16
D_KEY = 256
D_HALF = D_KEY // 2
PEER_CHUNK = 128
EPS = 1e-6
NEG = -1e30


def rms_norm(x, g):
    x32 = x.astype(jnp.float32)
    y = x32 * lax.rsqrt(jnp.mean(x32 * x32, axis=-1, keepdims=True) + EPS)
    return (y * g.astype(jnp.float32)).astype(x.dtype)

def head_rms_norm(x, g, n_groups):
    shp = x.shape
    xh = x.reshape(shp[:-1] + (n_groups, HEAD_DIM))
    y = rms_norm(xh, g.reshape(n_groups, HEAD_DIM))
    return y.reshape(shp)

def modulate(h, shift, scale):
    return h * (1 + scale[:, None, :]) + shift[:, None, :]

def sliding_window_sink_attention(q, k, v, sinks):
    bsz, s_len = q.shape[0], q.shape[1]
    nb = s_len // WINDOW
    qb = q.reshape(bsz, nb, WINDOW, N_KV_HEADS, GQA_GROUP, HEAD_DIM)
    kb = k.reshape(bsz, nb, WINDOW, N_KV_HEADS, HEAD_DIM)
    vb = v.reshape(bsz, nb, WINDOW, N_KV_HEADS, HEAD_DIM)

    def with_prev(t):
        prev = jnp.pad(t[:, :-1], ((0, 0), (1, 0), (0, 0), (0, 0), (0, 0)))
        return jnp.concatenate([prev, t], axis=2)

    kk, vv = with_prev(kb), with_prev(vb)
    s = jnp.einsum('bnqkgd,bnjkd->bnkgqj', qb, kk).astype(jnp.float32) * (HEAD_DIM ** -0.5)
    qi = jnp.arange(WINDOW)[:, None]
    kj = jnp.arange(2 * WINDOW)[None, :]
    diff = qi + WINDOW - kj
    rel_ok = (diff >= 0) & (diff < WINDOW)
    blk = jnp.arange(nb)[:, None, None]
    valid = rel_ok[None] & ((blk > 0) | (kj[None] >= WINDOW))
    s = jnp.where(valid[None, :, None, None], s, NEG)
    sink = sinks.astype(jnp.float32).reshape(N_KV_HEADS, GQA_GROUP)[None, None, :, :, None, None]
    m = jnp.maximum(jnp.max(s, axis=-1, keepdims=True), sink)
    e = jnp.exp(s - m)
    p = e / (jnp.sum(e, axis=-1, keepdims=True) + jnp.exp(sink - m))
    o = jnp.einsum('bnkgqj,bnjkd->bnqkgd', p.astype(v.dtype), vv)
    return o.reshape(bsz, s_len, ATTN_WIDTH)

def short_gated_conv(b_gate, c_gate, u, conv_w):
    z = c_gate * u
    zp = jnp.pad(z, ((0, 0), (CONV_K - 1, 0), (0, 0)))
    s_len = z.shape[1]
    conv = zp[:, 0:s_len] * conv_w[0] + zp[:, 1:s_len + 1] * conv_w[1] + zp[:, 2:s_len + 2] * conv_w[2]
    return b_gate * conv

def peer_layer(h, w_query, peer_keys1, peer_keys2, peer_u, peer_v):
    bsz, s_len, d = h.shape
    t = bsz * s_len
    hf = h.reshape(t, d)
    q = (hf @ w_query).reshape(t, PEER_HEADS, D_KEY)
    s1 = jnp.einsum('thd,hnd->thn', q[..., :D_HALF], peer_keys1).astype(jnp.float32)
    s2 = jnp.einsum('thd,hnd->thn', q[..., D_HALF:], peer_keys2).astype(jnp.float32)
    v1, i1 = lax.top_k(s1, PEER_TOPK)
    v2, i2 = lax.top_k(s2, PEER_TOPK)
    cand = (v1[..., :, None] + v2[..., None, :]).reshape(t, PEER_HEADS, PEER_TOPK * PEER_TOPK)
    sc, ci = lax.top_k(cand, PEER_TOPK)
    e1 = jnp.take_along_axis(i1, ci // PEER_TOPK, axis=-1)
    e2 = jnp.take_along_axis(i2, ci % PEER_TOPK, axis=-1)
    idx = e1 * N_KEYS + e2
    gates = jax.nn.softmax(sc, axis=-1).astype(h.dtype)

    nchunk = t // PEER_CHUNK
    hc = hf.reshape(nchunk, PEER_CHUNK, d)
    ic = idx.reshape(nchunk, PEER_CHUNK, PEER_HEADS, PEER_TOPK)
    gc = gates.reshape(nchunk, PEER_CHUNK, PEER_HEADS, PEER_TOPK)

    def chunk_fn(args):
        hx, ix, gx = args
        u = peer_u[ix]
        a = jax.nn.gelu(jnp.einsum('td,thkd->thk', hx, u), approximate=False)
        vsel = peer_v[ix]
        return jnp.einsum('thk,thkd->td', gx * a, vsel)

    out = lax.map(chunk_fn, (hc, ic, gc))
    return out.reshape(bsz, s_len, d)

def first_inputs(seed: int = 0) -> dict:
    key = jax.random.key(seed)
    ks = jax.random.split(key, 20)
    D = D_MODEL
    f32 = jnp.float32
    return {
        "x": jax.random.normal(ks[0], (BATCH, SEQ, D), f32),
        "c": jax.random.normal(ks[1], (BATCH, D), f32),
        "w_ada": jax.random.normal(ks[2], (D, 6 * D), f32) * D ** -0.5,
        "b_ada": jax.random.normal(ks[3], (6 * D,), f32) * 0.02,
        "norm1_g": 1.0 + 0.02 * jax.random.normal(ks[4], (D,), f32),
        "w_in": jax.random.normal(ks[5], (D, IN_WIDTH), f32) * D ** -0.5,
        "b_in": jax.random.normal(ks[6], (IN_WIDTH,), f32) * 0.02,
        "attn_sinks": jax.random.normal(ks[7], (N_HEADS,), f32) * 0.5,
        "conv_w": jax.random.normal(ks[8], (CONV_K, CONV_WIDTH), f32) * CONV_K ** -0.5,
        "attn_out_g": 1.0 + 0.02 * jax.random.normal(ks[9], (ATTN_WIDTH,), f32),
        "conv_out_g": 1.0 + 0.02 * jax.random.normal(ks[10], (CONV_WIDTH,), f32),
        "w_out": jax.random.normal(ks[11], (D_MIX, D), f32) * D_MIX ** -0.5,
        "b_out": jax.random.normal(ks[12], (D,), f32) * 0.02,
        "norm2_g": 1.0 + 0.02 * jax.random.normal(ks[13], (D,), f32),
        "w_query": jax.random.normal(ks[14], (D, PEER_HEADS * D_KEY), f32) * D ** -0.5,
        "peer_keys1": jax.random.normal(ks[15], (PEER_HEADS, N_KEYS, D_HALF), f32) * D_HALF ** -0.5,
        "peer_keys2": jax.random.normal(ks[16], (PEER_HEADS, N_KEYS, D_HALF), f32) * D_HALF ** -0.5,
        "peer_u": jax.random.normal(ks[17], (N_EXPERTS, D), f32) * D ** -0.5,
        "peer_v": jax.random.normal(ks[18], (N_EXPERTS, D), f32) * PEER_HEADS ** -0.5,
        "final_g": 1.0 + 0.02 * jax.random.normal(ks[19], (D,), f32),
    }

def first_block(x, c, w_ada, b_ada, norm1_g, w_in, b_in, attn_sinks, conv_w, attn_out_g,
              conv_out_g, w_out, b_out, norm2_g, w_query, peer_keys1, peer_keys2,
              peer_u, peer_v, final_g):
    bsz, s_len, _ = x.shape
    for _layer in range(DEPTH):
        ada = jax.nn.silu(c) @ w_ada + b_ada
        shift1, scale1, gate1, shift2, scale2, gate2 = jnp.split(ada, 6, axis=-1)

        h = modulate(rms_norm(x, norm1_g), shift1, scale1)
        proj = h @ w_in + b_in
        o1 = ATTN_WIDTH
        o2 = o1 + KV_WIDTH
        o3 = o2 + KV_WIDTH
        o4 = o3 + CONV_WIDTH
        o5 = o4 + CONV_WIDTH
        q = proj[..., :o1].reshape(bsz, s_len, N_HEADS, HEAD_DIM)
        k = proj[..., o1:o2].reshape(bsz, s_len, N_KV_HEADS, HEAD_DIM)
        v = proj[..., o2:o3].reshape(bsz, s_len, N_KV_HEADS, HEAD_DIM)
        b_gate = proj[..., o3:o4]
        c_gate = proj[..., o4:o5]
        u_conv = proj[..., o5:]
        attn = head_rms_norm(sliding_window_sink_attention(q, k, v, attn_sinks), attn_out_g, N_HEADS)
        conv = head_rms_norm(short_gated_conv(b_gate, c_gate, u_conv, conv_w), conv_out_g, N_CONV_GROUPS)
        mix = jnp.concatenate([attn, conv], axis=-1) @ w_out + b_out
        x = x + gate1[:, None, :] * mix

        h2 = modulate(rms_norm(x, norm2_g), shift2, scale2)
        x = x + gate2[:, None, :] * peer_layer(h2, w_query, peer_keys1, peer_keys2, peer_u, peer_v)
    return rms_norm(x, final_g)


DEPTH_2 = 2

CHUNK = 64
LEFT_CHUNKS = 8
BAND = LEFT_CHUNKS + 1
ATTN_HEAD_DIM = 64
ATTN_HEADS = D_MODEL // ATTN_HEAD_DIM
MAX_REL = 256
DN_HEAD_DIM = 128
DN_HEADS = D_MODEL // DN_HEAD_DIM
DN_WIDTH = DN_HEADS * DN_HEAD_DIM
CONV_K_2 = 4
D_FF = 4 * D_MODEL
N_MIXERS = 2
N_ATTN_LAYERS = (DEPTH_2 + 1) // 2
N_DN_LAYERS = DEPTH_2 // 2


def rmsnorm(x, w):
    xf = x.astype(jnp.float32)
    y = xf * lax.rsqrt(jnp.mean(xf * xf, axis=-1, keepdims=True) + EPS)
    return (y * w.astype(jnp.float32)).astype(x.dtype)

def l2norm(x):
    xf = x.astype(jnp.float32)
    return xf * lax.rsqrt(jnp.sum(xf * xf, axis=-1, keepdims=True) + EPS)

def chunked_rel_attention(h, w_qkv, rel_bias, w_o):
    B, S, _ = h.shape
    nc = S // CHUNK
    qkv = h @ w_qkv
    q, k, v = jnp.split(qkv, 3, axis=-1)
    q = q.reshape(B, S, ATTN_HEADS, ATTN_HEAD_DIM)
    k = k.reshape(B, S, ATTN_HEADS, ATTN_HEAD_DIM)
    v = v.reshape(B, S, ATTN_HEADS, ATTN_HEAD_DIM)
    pad = ((0, 0), (LEFT_CHUNKS * CHUNK, 0), (0, 0), (0, 0))
    kpad = jnp.pad(k, pad)
    vpad = jnp.pad(v, pad)
    q_off = jnp.arange(CHUNK)[:, None]
    k_off = jnp.arange(BAND * CHUNK)[None, :] - LEFT_CHUNKS * CHUNK
    dist = jnp.clip(q_off - k_off, -MAX_REL, MAX_REL) + MAX_REL
    bias = rel_bias[:, dist].astype(jnp.float32)
    scale = ATTN_HEAD_DIM ** -0.5

    def one_chunk(c):
        start = c * CHUNK
        q_c = lax.dynamic_slice_in_dim(q, start, CHUNK, axis=1)
        k_b = lax.dynamic_slice_in_dim(kpad, start, BAND * CHUNK, axis=1)
        v_b = lax.dynamic_slice_in_dim(vpad, start, BAND * CHUNK, axis=1)
        s = jnp.einsum('bqhd,bkhd->bhqk', q_c, k_b,
                       preferred_element_type=jnp.float32) * scale + bias[None]
        k_abs = start - LEFT_CHUNKS * CHUNK + jnp.arange(BAND * CHUNK)
        s = jnp.where((k_abs >= 0)[None, None, None, :], s, -jnp.inf)
        p = jax.nn.softmax(s, axis=-1).astype(v.dtype)
        return jnp.einsum('bhqk,bkhd->bqhd', p, v_b)

    o = lax.map(one_chunk, jnp.arange(nc))
    o = jnp.moveaxis(o, 0, 1).reshape(B, S, D_MODEL)
    return o @ w_o

def causal_conv(x, w):
    S = x.shape[1]
    xp = jnp.pad(x, ((0, 0), (CONV_K_2 - 1, 0), (0, 0)))
    y = xp[:, 0:S] * w[0]
    for j in range(1, CONV_K_2):
        y = y + xp[:, j:j + S] * w[j]
    return y

def chunk_gated_delta_rule(q, k, v, g, beta):
    B, S, H, dk = q.shape
    dv = v.shape[-1]
    nc = S // CHUNK

    def to_chunks(t):
        t = t.astype(jnp.float32).reshape((B, nc, CHUNK, H) + t.shape[3:])
        return jnp.moveaxis(t, 3, 1)

    q, k, v, g, beta = map(to_chunks, (q, k, v, g, beta))
    gc = jnp.cumsum(g, axis=-1)
    idx = jnp.arange(CHUNK)
    incl = idx[:, None] >= idx[None, :]
    strict = idx[:, None] > idx[None, :]
    decay = jnp.exp(jnp.where(incl, gc[..., :, None] - gc[..., None, :], -jnp.inf))
    kb = k * beta[..., None]
    vb = v * beta[..., None]
    L = jnp.where(strict, jnp.einsum('bhnid,bhnjd->bhnij', kb, k) * decay, 0.0)
    M = L + jnp.eye(CHUNK, dtype=jnp.float32)
    rhs = jnp.concatenate([vb, kb * jnp.exp(gc)[..., None]], axis=-1)
    sol = lax.linalg.triangular_solve(M, rhs, left_side=True, lower=True,
                                      unit_diagonal=True)
    u, w = sol[..., :dv], sol[..., dv:]
    qk = jnp.einsum('bhnid,bhnjd->bhnij', q, k) * decay
    q_dec = q * jnp.exp(gc)[..., None]
    k_dec = k * jnp.exp(gc[..., -1:] - gc)[..., None]
    g_last = jnp.exp(gc[..., -1])
    xs = tuple(jnp.moveaxis(t, 2, 0) for t in (u, w, qk, q_dec, k_dec, g_last))

    def step(state, inp):
        u_c, w_c, qk_c, qd_c, kd_c, gl_c = inp
        v_new = u_c - jnp.einsum('bhck,bhkv->bhcv', w_c, state)
        o_c = jnp.einsum('bhck,bhkv->bhcv', qd_c, state) + jnp.einsum('bhij,bhjv->bhiv', qk_c, v_new)
        state = state * gl_c[..., None, None] + jnp.einsum('bhck,bhcv->bhkv', kd_c, v_new)
        return state, o_c

    s0 = jnp.zeros((B, H, dk, dv), jnp.float32)
    _, o = lax.scan(step, s0, xs)
    o = jnp.transpose(o, (1, 0, 3, 2, 4))
    return o.reshape(B, S, H, dv)

def gated_deltanet(h, w_in, conv_w, a_log, dt_bias, head_norm, w_o):
    B, S, _ = h.shape
    proj = h @ w_in
    qkv = proj[..., :3 * DN_WIDTH]
    z = proj[..., 3 * DN_WIDTH:4 * DN_WIDTH]
    a = proj[..., 4 * DN_WIDTH:4 * DN_WIDTH + DN_HEADS]
    b = proj[..., 4 * DN_WIDTH + DN_HEADS:]
    qkv = jax.nn.silu(causal_conv(qkv, conv_w))
    q, k, v = jnp.split(qkv, 3, axis=-1)
    q = l2norm(q.reshape(B, S, DN_HEADS, DN_HEAD_DIM)) * (DN_HEAD_DIM ** -0.5)
    k = l2norm(k.reshape(B, S, DN_HEADS, DN_HEAD_DIM))
    v = v.reshape(B, S, DN_HEADS, DN_HEAD_DIM)
    beta = jax.nn.sigmoid(b.astype(jnp.float32))
    g = -jnp.exp(a_log.astype(jnp.float32)) * jax.nn.softplus(
        a.astype(jnp.float32) + dt_bias.astype(jnp.float32))
    o = chunk_gated_delta_rule(q, k, v, g, beta)
    o = rmsnorm(o, head_norm) * jax.nn.silu(
        z.astype(jnp.float32).reshape(B, S, DN_HEADS, DN_HEAD_DIM))
    return o.reshape(B, S, DN_WIDTH).astype(h.dtype) @ w_o

def squared_relu_mlp(h, w_up, w_down):
    return jnp.square(jax.nn.relu(h @ w_up)) @ w_down

def second_inputs(seed: int = 0) -> dict:
    key = jax.random.key(seed)
    ks = jax.random.split(key, 18)
    f32 = jnp.float32

    def nrm(k, shape, fan_in, gain=1.0):
        return jax.random.normal(k, shape, f32) * (gain * fan_in ** -0.5)

    def gains(k, shape):
        return 1.0 + 0.02 * jax.random.normal(k, shape, f32)

    NA, NB = N_ATTN_LAYERS, N_DN_LAYERS
    x = jax.random.normal(ks[0], (BATCH, SEQ, D_MODEL), f32)
    attn_norm = gains(ks[1], (NA, D_MODEL))
    attn_w_qkv = nrm(ks[2], (NA, D_MODEL, 3 * D_MODEL), D_MODEL)
    attn_rel_bias = 0.1 * jax.random.normal(ks[3], (NA, ATTN_HEADS, 2 * MAX_REL + 1), f32)
    attn_w_o = nrm(ks[4], (NA, D_MODEL, D_MODEL), D_MODEL)
    dn_norm = gains(ks[5], (NB, D_MODEL))
    dn_w_in = nrm(ks[6], (NB, D_MODEL, 4 * DN_WIDTH + 2 * DN_HEADS), D_MODEL)
    dn_conv_w = nrm(ks[7], (NB, CONV_K_2, 3 * DN_WIDTH), CONV_K_2)
    dn_a_log = jnp.log(jax.random.uniform(ks[8], (NB, DN_HEADS), f32, 1.0, 16.0))
    dt = jnp.exp(jax.random.uniform(ks[9], (NB, DN_HEADS), f32,
                                    math.log(1e-3), math.log(1e-1)))
    dn_dt_bias = dt + jnp.log(-jnp.expm1(-dt))
    dn_head_norm = gains(ks[10], (NB, DN_HEAD_DIM))
    dn_w_o = nrm(ks[11], (NB, DN_WIDTH, D_MODEL), DN_WIDTH)
    mlp_norm = gains(ks[12], (DEPTH_2, D_MODEL))
    mlp_w_up = nrm(ks[13], (DEPTH_2, D_MODEL, D_FF), D_MODEL)
    mlp_w_down = nrm(ks[14], (DEPTH_2, D_FF, D_MODEL), D_FF, gain=0.5)
    final_norm = gains(ks[15], (D_MODEL,))
    return {"x": x, "attn_norm": attn_norm, "attn_w_qkv": attn_w_qkv,
            "attn_rel_bias": attn_rel_bias, "attn_w_o": attn_w_o,
            "dn_norm": dn_norm, "dn_w_in": dn_w_in, "dn_conv_w": dn_conv_w,
            "dn_a_log": dn_a_log, "dn_dt_bias": dn_dt_bias, "dn_head_norm": dn_head_norm,
            "dn_w_o": dn_w_o, "mlp_norm": mlp_norm, "mlp_w_up": mlp_w_up,
            "mlp_w_down": mlp_w_down, "final_norm": final_norm}

def second_block(x, attn_norm, attn_w_qkv, attn_rel_bias, attn_w_o,
              dn_norm, dn_w_in, dn_conv_w, dn_a_log, dn_dt_bias, dn_head_norm, dn_w_o,
              mlp_norm, mlp_w_up, mlp_w_down, final_norm):
    for i in range(DEPTH_2):
        j = i // N_MIXERS
        if i % N_MIXERS == 0:
            x = x + chunked_rel_attention(rmsnorm(x, attn_norm[j]), attn_w_qkv[j],
                                          attn_rel_bias[j], attn_w_o[j])
        else:
            x = x + gated_deltanet(rmsnorm(x, dn_norm[j]), dn_w_in[j], dn_conv_w[j],
                                   dn_a_log[j], dn_dt_bias[j], dn_head_norm[j], dn_w_o[j])
        x = x + squared_relu_mlp(rmsnorm(x, mlp_norm[i]), mlp_w_up[i], mlp_w_down[i])
    return rmsnorm(x, final_norm)


def setup_inputs(seed=0):
    out = dict(first_inputs(seed))
    for name, value in second_inputs(seed + 1).items():
        if name != "x":
            out[name + "_2"] = value
    return out


def reference(
    x, c, w_ada, b_ada, norm1_g, w_in, b_in, attn_sinks, conv_w, attn_out_g, conv_out_g, w_out,
    b_out, norm2_g, w_query, peer_keys1, peer_keys2, peer_u, peer_v, final_g, attn_norm_2,
    attn_w_qkv_2, attn_rel_bias_2, attn_w_o_2, dn_norm_2, dn_w_in_2, dn_conv_w_2, dn_a_log_2,
    dn_dt_bias_2, dn_head_norm_2, dn_w_o_2, mlp_norm_2, mlp_w_up_2, mlp_w_down_2, final_norm_2,
):
    x = first_block(
        x, c, w_ada, b_ada, norm1_g, w_in, b_in, attn_sinks, conv_w, attn_out_g, conv_out_g,
        w_out, b_out, norm2_g, w_query, peer_keys1, peer_keys2, peer_u, peer_v, final_g,
    )
    return second_block(
        x, attn_norm_2, attn_w_qkv_2, attn_rel_bias_2, attn_w_o_2, dn_norm_2, dn_w_in_2,
        dn_conv_w_2, dn_a_log_2, dn_dt_bias_2, dn_head_norm_2, dn_w_o_2, mlp_norm_2, mlp_w_up_2,
        mlp_w_down_2, final_norm_2,
    )


_drawn_inputs = setup_inputs


def setup_inputs(seed=0):
    import zlib

    import numpy as np

    out = dict(_drawn_inputs(seed))
    spreads = {}
    factors = {'attn_sinks': 64.0,
     'attn_out_g': 3.286,
     'conv_out_g': 3.781,
     'norm2_g': 2.86,
     'attn_norm_2': 6.99,
     'attn_rel_bias_2': 4.607,
     'dn_norm_2': 3.717,
     'dn_head_norm_2': 19.297,
     'mlp_norm_2': 3.195,
     'final_norm_2': 8.107}
    for name, (base, spread) in spreads.items():
        noise = np.random.default_rng([zlib.crc32(name.encode()), seed]).standard_normal(out[name].shape)
        drawn = base * np.exp(spread * noise) if base else spread * noise
        out[name] = __import__('jax').numpy.asarray(drawn.astype(out[name].dtype))
    for name, factor in factors.items():
        out[name] = (out[name] * factor).astype(out[name].dtype)
    return out
```

```python
from contextlib import ExitStack

import numpy as np
import concourse.bass as bass
from concourse import mybir

F32 = mybir.dt.float32
U32 = mybir.dt.uint32
ALU = mybir.AluOpType
ACT = mybir.ActivationFunctionType
AX = mybir.AxisListType.X

P = 128
D = 1024
S = 512
T = S // P
KC = D // P
N = 512
EPS = 1e-6
NEG = -1e30
LOWEST = -3.4e38

HEAD = 64
HEADS1 = 8
AW = HEADS1 * HEAD
CW = D - AW
TAPS1 = 3
KEYS = 128
EXPERTS = KEYS * KEYS
PH = 8
TOPK = 16
HEADS2 = 16
MAX_REL = 256
CHUNK = 64
DH = 128
DNH = D // DH
TAPS2 = 4
FF = 4 * D
FC = FF // P

SLAB = KC * N
RING = 4
E2C = SLAB // D
ECH = KEYS // E2C
GT = 64
NG = S // GT

COLS = {}
_at = 0
for _name, _n in (("c", KC), ("b_ada", 6 * KC), ("norm1_g", KC), ("b_in", 18), ("conv_w", TAPS1 * 4),
                  ("conv_out_g", 4), ("norm2_g", KC), ("attn_norm", KC), ("mlp_norm0", KC), ("mlp_norm1", KC),
                  ("dn_norm", KC), ("dn_conv_w", TAPS2 * 24), ("dn_ab", KC * 2 * DNH)):
    COLS[_name] = (_at, _n)
    _at += _n
NCOL = _at
ROWS = {}
_at = 0
for _name, _n in (("b_v", P), ("attn_out_g", AW), ("sinks", HEADS1), ("head_norm", DH), ("dt_bias", DNH),
                  ("a_log", DNH)):
    ROWS[_name] = (_at, _n)
    _at += _n
NROW = _at
BIGROWS = ("b_gate1", "b_gate2", "b_out", "final_g", "final_norm")

ARENA = 23568
ADA_SLABS = 12
NSLABS = ADA_SLABS + 5 + 2 + 5 + 2 * ECH + 6 + 2 + 16 + 8 + 2 + 16


def program(nc, A, out):
    ctx = ExitStack()
    with ctx:
        def sb(name, shape, dt=F32):
            return ctx.enter_context(nc.sbuf_tensor(name, shape, dt))

        def sem(name):
            return ctx.enter_context(nc.semaphore(name))

        ps = ctx.enter_context(nc.psum_tensor("ps", [P, 8, N], F32))
        x = sb("x_res", [P, T, D])
        hT = sb("hT", [P, KC, S])
        ring = sb("ring", [P, RING, SLAB])
        cols = sb("cols_sb", [P, NCOL])
        rows = sb("rows_sb", [P, NROW])
        gates = sb("gates", [P, 2, D])
        gate1, gate2 = gates[:, 0, :], gates[:, 1, :]
        ada = sb("ada", [P, 6 * KC])
        mod1 = sb("mod1", [P, KC])
        mod2 = sb("mod2", [P, KC])
        ident = sb("ident", [P, P])
        ones = sb("ones", [P, P])
        group64 = sb("group64", [P, P])
        iota = sb("iota", [P, P])
        LEVELS = 6
        blk_id, blk_tri, blk_strict, blk_incl, blk_low0 = (
            sb("blk_" + n, [P, CHUNK]) for n in ("id", "tri", "strict", "incl", "low0"))
        blk_low = sb("blk_low", [P, LEVELS, CHUNK])
        small = sb("small", [P, 512])
        arena = sb("arena", [P, ARENA])

        def col(name, i=0, n=None):
            at, m = COLS[name]
            return cols[:, at + i:at + i + (n if n is not None else m - i)]

        def row(name):
            at, m = ROWS[name]
            return rows[:, at:at + m]

        def area(at, *shape):
            n = int(np.prod(shape))
            v = arena[:, at:at + n]
            if len(shape) == 2:
                v = v.rearrange("p (a b) -> p a b", b=shape[1])
            if len(shape) == 3:
                v = v.rearrange("p (a b c) -> p a b c", b=shape[1], c=shape[2])
            return v, at + n

        def bc(ap, *shape):
            return ap.broadcast_to([ap.shape[0], *shape])

        slab_in = [sem(f"slab_in{i}") for i in range(RING)]
        slab_used = sem("slab_used")
        stage_done = sem("stage_done")
        loaded = sem("loaded")
        consts = sem("consts")
        stored = sem("stored")

        gates_dram = nc.dram_tensor("gates_dram", [ECH, P, NG, E2C * GT], F32, kind="Internal").ap()
        by_name, calls = {}, {}

        def shared(name):
            if name not in by_name:
                by_name[name] = sem(name)
            return by_name[name]

        def call(kind):
            calls[kind] = calls.get(kind, -1) + 1
            return calls[kind]

        stages = []
        taken = [0]

        def stage(**parts):
            stages.append(parts)

        def slabs(n):
            at = taken[0]
            taken[0] += n
            return at

        def slab(i):
            return ring[:, i % RING, :]

        def slab_k(i, width=N):
            return ring[:, i % RING, 0:KC * width].rearrange("p (k n) -> p k n", n=width)

        def await_slab(eng, i):
            eng.wait_ge(slab_in[i % RING], 16 * (i // RING + 1))

        class Chain:
            def __init__(self, eng, name):
                self.eng, self.sem, self.n = eng, sem(name), 0

            def __call__(self, ins):
                self.n += 1
                ins.then_inc(self.sem, 1)
                self.eng.wait_ge(self.sem, self.n)

        chains = {}

        def chain(eng, name):
            if name not in chains:
                chains[name] = Chain(eng, name)
            return chains[name]

        def ada_stage():
            s0 = slabs(ADA_SLABS)
            sc, at = area(0, KC)
            scb, at = area(at, KC, P)
            bits, at = area(at, 6, CHUNK)
            bitf, at = area(at, 6, CHUNK)
            I32 = mybir.dt.int32
            act_silu = sem("act_silu")
            wide = sem("silu_wide")
            cols_done = sem("ada_cols_done")
            gates_done = sem("ada_gates_done")

            def act(e):
                e.dma_start(cols[:], A["cols"]).then_inc(loaded, 16)
                e.dma_start(rows[:], A["rows"].partition_broadcast(P)).then_inc(loaded, 16)
                e.dma_start(gate1, A["b_gate1"].partition_broadcast(P)).then_inc(loaded, 16)
                e.dma_start(gate2, A["b_gate2"].partition_broadcast(P)).then_inc(loaded, 16)
                e.dma_start(x[:], A["x"]).then_inc(loaded, 16)
                e.wait_ge(loaded, 80)
                e.activation(sc, col("c"), ACT.Silu).then_inc(act_silu, 1)

            def pool(e):
                e.memset(ident[:], 0.0).then_inc(consts, 1)
                e.memset(ones[:], 1.0).then_inc(consts, 1)
                e.memset(group64[:], 0.0).then_inc(consts, 1)
                e.iota(iota[:], [[1, P]], base=0, channel_multiplier=0,
                       allow_small_or_imprecise_dtypes=True).then_inc(consts, 1)
                e.wait_ge(consts, 4)
                e.affine_select(out=ident[:], in_=ident[:], compare_op=ALU.not_equal, fill=1.0, base=0,
                                pattern=[[-1, P]], channel_multiplier=1).then_inc(consts, 1)
                e.wait_ge(consts, 5)
                e.memset(group64[0:64, 0:64], 1.0).then_inc(consts, 1)
                e.wait_ge(consts, 6)
                e.memset(group64[64:128, 64:128], 1.0).then_inc(consts, 1)
                e.wait_ge(consts, 7)
                for r0 in (0, 64):
                    e.iota(bits[r0:r0 + 64, 0, :].bitcast(I32), [[0, CHUNK]], base=0, channel_multiplier=1
                           ).then_inc(consts, 1)
                e.wait_ge(consts, 9)
                e.iota(bits[:, 1, :].bitcast(I32), [[1, CHUNK]], base=0, channel_multiplier=0).then_inc(consts, 1)
                e.wait_ge(consts, 10)

            def pe(e):
                e.wait_ge(act_silu, 1)
                e.wait_ge(wide, 1)
                for i in range(ADA_SLABS):
                    part = i // 2
                    await_slab(e, s0 + i)
                    w = slab_k(s0 + i)
                    if part in (2, 5):
                        bank = 1 + (part == 5) * 2 + i % 2
                        for k in range(KC):
                            mm = e.matmul(ps[:, bank, :], scb[:, k, :], w[:, k, :], start=k == 0, stop=k == KC - 1)
                    else:
                        for j in range(N // P):
                            for k in range(KC):
                                c = i * (N // P) + j
                                mm = e.matmul(ps[:, 0, c:c + 1], w[:, k, j * P:(j + 1) * P], sc[:, k:k + 1],
                                              start=k == 0, stop=k == KC - 1)
                    mm.then_inc(slab_used, 1)

            def dve(e):
                link = chain(e, "dve_chain")
                e.wait_ge(consts, 2)
                e.wait_ge(act_silu, 1)
                for k in range(KC):
                    last = e.tensor_scalar(scb[:, k, :], ones[:], sc[:, k:k + 1], None, ALU.mult)
                last.then_inc(wide, 1)
                e.wait_ge(consts, 10)
                link(e.tensor_copy(bitf[:, 0:2, :], bits[:, 0:2, :].bitcast(I32)))
                rf, cf = bitf[:, 0, :], bitf[:, 1, :]
                for m, op in ((blk_id, ALU.is_equal), (blk_tri, ALU.is_le), (blk_strict, ALU.is_gt),
                              (blk_incl, ALU.is_ge)):
                    e.tensor_tensor(m[:], rf, cf, op)
                for s in range(LEVELS):
                    link(e.tensor_scalar(bits[:, 2:4, :].bitcast(I32), bits[:, 0:2, :].bitcast(I32), s, None,
                                         ALU.arith_shift_right))
                    link(e.tensor_tensor(bits[:, 4, :].bitcast(I32), bits[:, 2, :].bitcast(I32),
                                         bits[:, 3, :].bitcast(I32), ALU.bitwise_xor))
                    link(e.tensor_scalar(bits[:, 2:4, :].bitcast(I32), bits[:, 2:4, :].bitcast(I32), 1, None,
                                         ALU.bitwise_and))
                    link(e.tensor_copy(bitf[:, 2:5, :], bits[:, 2:5, :].bitcast(I32)))
                    link(e.scalar_tensor_tensor(blk_low[:, s, :], bitf[:, 4, :], 1.0, bitf[:, 2, :], ALU.is_equal,
                                                ALU.mult))
                    if s == 0:
                        link(e.scalar_tensor_tensor(blk_low0[:], bitf[:, 4, :], 1.0, bitf[:, 3, :], ALU.is_equal,
                                                    ALU.mult))
                e.wait_ge(slab_used, s0 + ADA_SLABS)
                e.wait_ge(loaded, 80)
                link(e.memset(ada[:], 0.0))
                for a, b in ((0, 2), (3, 5)):
                    link(e.tensor_tensor(ada[:, a * KC:b * KC], ps[:, 0, a * KC:b * KC],
                                         col("b_ada", a * KC, (b - a) * KC), ALU.add))
                for mod, g, a in ((mod1, "norm1_g", 1), (mod2, "norm2_g", 4)):
                    link(e.scalar_tensor_tensor(mod[:], ada[:, a * KC:(a + 1) * KC], 1.0, col(g), ALU.add, ALU.mult))
                for g, bank in ((gate1, 1), (gate2, 3)):
                    for n in range(2):
                        link(e.tensor_tensor(g[:, n * N:(n + 1) * N], ps[:, bank + n, :], g[:, n * N:(n + 1) * N],
                                             ALU.add))
            stage(pe=pe, act=act, dve=dve, pool=pool)

        def rms_scale(e_dve, link, e_act_sem, dst, ss, width):
            link(e_dve.tensor_scalar(dst, ss, 1.0 / width, EPS, ALU.mult, ALU.add))

        def norm_stage(tag, g, b=None, at=0):
            xn, _ = area(at, T, D)
            ss, rs = small[:, 0:T], small[:, T:2 * T]
            r = call("norm")
            squared, inverse, rooted, normed, turned = (
                shared("norm_" + n) for n in ("squared", "inverse", "rooted", "normed", "turned"))

            def act(e):
                for t in range(T):
                    e.activation(xn[:, t, :], x[:, t, :], ACT.Square, accum_out=ss[:, t:t + 1]).then_inc(squared, 1)
                e.wait_ge(inverse, r + 1)
                e.activation(rs, rs, ACT.Sqrt).then_inc(rooted, 1)
                for c in range(0, KC, 2):
                    e.wait_ge(turned, r * KC + c + 1)
                    e.activation(hT[:, c, :], ps[:, c, :], ACT.Identity, scale=g[:, c:c + 1],
                                 bias=b[:, c:c + 1] if b is not None else 0.0)

            def dve(e):
                link = chain(e, "dve_chain")
                e.wait_ge(squared, (r + 1) * T)
                link(e.tensor_scalar(rs, ss, 1.0 / D, EPS, ALU.mult, ALU.add))
                e.reciprocal(rs, rs).then_inc(inverse, 1)
                e.wait_ge(rooted, r + 1)
                for t in range(T):
                    e.tensor_scalar(xn[:, t, :], x[:, t, :], rs[:, t:t + 1], None, ALU.mult).then_inc(normed, 1)
                for c in range(1, KC, 2):
                    e.wait_ge(turned, r * KC + c + 1)
                    if b is None:
                        e.tensor_scalar(hT[:, c, :], ps[:, c, :], g[:, c:c + 1], None, ALU.mult)
                    else:
                        e.tensor_scalar(hT[:, c, :], ps[:, c, :], g[:, c:c + 1], b[:, c:c + 1], ALU.mult, ALU.add)

            def pe(e):
                for c in range(KC):
                    for t in range(T):
                        if c == 0:
                            e.wait_ge(normed, r * T + t + 1)
                        mm = e.transpose(ps[:, c, t * P:(t + 1) * P], xn[:, t, c * P:(c + 1) * P], ident[:])
                    mm.then_inc(turned, 1)
            stage(pe=pe, act=act, dve=dve)

        def slab_channels(e, i, outs, width=N, src=None, first=0, done=None, wait=None):
            src = hT if src is None else src
            w = slab_k(i, width)
            await_slab(e, i)
            for j in outs:
                if wait:
                    wait(j)
                for k in range(KC):
                    mm = e.matmul(ps[:, (first + j) % 8, :], w[:, k, j * P:(j + 1) * P], src[:, k, :],
                                  start=k == 0, stop=k == KC - 1)
                mm.then_inc(done, 1)
            return mm

        def in_stage():
            s0 = slabs(5)
            qT, at = area(0, 4, S)
            kT, at = area(at, S)
            v, at = area(at, T, P)
            bcu, at = area(at, 12, S)
            done, freed = sem("in_done"), sem("in_freed")

            def pe(e):
                def wait(g):
                    if g >= 8:
                        e.wait_ge(freed, g - 7)
                for i in range(5):
                    await_slab(e, s0 + i)
                    w = slab_k(s0 + i, 256 if i == 1 else N)
                    for j in range(2 if i == 1 else 4):
                        g = (0, 4, 6, 10, 14)[i] + j
                        wait(g)
                        if i == 1 and j == 1:
                            for t in range(T):
                                for k in range(KC):
                                    mm = e.matmul(ps[:, g % 8, t * P:(t + 1) * P], hT[:, k, t * P:(t + 1) * P],
                                                  w[:, k, P:2 * P], start=k == 0, stop=k == KC - 1)
                        else:
                            for k in range(KC):
                                mm = e.matmul(ps[:, g % 8, :], w[:, k, j * P:(j + 1) * P], hT[:, k, :],
                                              start=k == 0, stop=k == KC - 1)
                        mm.then_inc(done, 1)
                    e.wait_ge(done, g + 1)
                    e.sem_inc(slab_used, 1)

            def dve(e):
                for g in range(18):
                    e.wait_ge(done, g + 1)
                    if g == 5:
                        ins = e.tensor_tensor(v, ps[:, g % 8, :].rearrange("p (t c) -> p t c", c=P),
                                              bc(row("b_v").unsqueeze(1), T, P), ALU.add)
                    else:
                        dst = qT[:, g, :] if g < 4 else kT if g == 4 else bcu[:, g - 6, :]
                        ins = e.tensor_scalar(dst, ps[:, g % 8, :], col("b_in", g, 1), None, ALU.add)
                    ins.then_inc(freed, 1)
            stage(pe=pe, dve=dve)
            return qT, kT, v, bcu, at

        def mix_stage(qT, kT, v, bcu, at):
            z, at = area(at, 4, S + TAPS1 - 1)
            y, at = area(at, 4, S)
            sc, at = area(at, HEADS1, 2 * P)
            mask, at = area(at, 2 * P)
            pt, at = area(at, 4, 4, P)
            ao, at = area(at, AW)
            sq, at = area(at, AW)
            tmp = bcu
            mx, es, den, rd = (small[:, 16 + 8 * i:24 + 8 * i] for i in range(4))
            hs, hr = small[:, 48:56], small[:, 56:64]
            masked, squares, sums, inverse, rooted = (sem("mix_" + n) for n in ("mask", "sq", "sum", "inv", "root"))
            scored, read, prob, expd = (sem("mix_" + n) for n in ("scored", "read", "prob", "exp"))
            turned, copied, valued, hinv, hroot, normed, oT, oC = (
                sem("mix_" + n) for n in ("turned", "copied", "valued", "hinv", "hroot", "normed", "oT", "oC"))

            def pool(e):
                e.memset(mask, 0.0).then_inc(masked, 1)
                e.wait_ge(masked, 1)
                e.affine_select(out=mask[:, 0:P], in_=mask[:, 0:P], compare_op=ALU.is_gt, fill=NEG, base=0,
                                pattern=[[1, P]], channel_multiplier=-1).then_inc(masked, 1)
                e.affine_select(out=mask[:, P:], in_=mask[:, P:], compare_op=ALU.is_ge, fill=NEG, base=0,
                                pattern=[[-1, P]], channel_multiplier=1).then_inc(masked, 1)

            def lo(t):
                return P if t == 0 else 0

            def pe(e):
                e.wait_ge(squares, 1)
                for c in range(4):
                    mm = e.matmul(ps[:, c, :], group64[:], tmp[:, c, :], start=True, stop=True)
                mm.then_inc(sums, 1)
                e.wait_ge(inverse, 1)

                def turn_out(t):
                    e.wait_ge(normed, t + 1)
                    if t:
                        e.wait_ge(oC, t)
                    for c in range(4):
                        mm = e.transpose(ps[:, 7, c * P:(c + 1) * P], ao[:, c * P:(c + 1) * P], ident[:])
                    mm.then_inc(oT, 1)

                for t in range(T):
                    if t:
                        e.wait_ge(read, t)
                    for h in range(HEADS1):
                        b = 64 * (h // 4)
                        mm = e.matmul(ps[:, h // 2, (h % 2) * 2 * P + lo(t):(h % 2 + 1) * 2 * P],
                                      qT[b:b + 64, h % 4, t * P:(t + 1) * P],
                                      kT[b:b + 64, (t - 1) * P + lo(t):(t + 1) * P], start=True, stop=True)
                    mm.then_inc(scored, 1)
                    if t:
                        turn_out(t - 1)
                    e.wait_ge(prob, t + 1)
                    for pair in range(4):
                        n = 4 * t + pair
                        if n >= 2:
                            e.wait_ge(copied, n - 1)
                        blocks = [(h, half) for h in (2 * pair, 2 * pair + 1) for half in (0, 1) if t or half]
                        for h, half in blocks:
                            mm = e.transpose(ps[:, 4 + n % 2, (2 * (h % 2) + half) * P:(2 * (h % 2) + half + 1) * P],
                                             sc[:, h, half * P:(half + 1) * P], ident[:])
                        mm.then_inc(turned, 1)
                        if pair:
                            values(e, t, pair - 1)
                    values(e, t, 3)
                turn_out(T - 1)

            def values(e, t, pair):
                n = 4 * t + pair
                e.wait_ge(copied, n + 1)
                if pair == 0 and t:
                    e.wait_ge(hinv, t)
                for h in (2 * pair, 2 * pair + 1):
                    kv = h // 4
                    for half in range(t == 0, 2):
                        mm = e.matmul(ps[:, 6, h * HEAD:(h + 1) * HEAD], pt[:, n % 4, 2 * (h % 2) + half, :],
                                      v[:, t - 1 + half, kv * HEAD:(kv + 1) * HEAD],
                                      start=half == (t == 0), stop=half == 1)
                mm.then_inc(valued, 1)

            def dve(e):
                link = chain(e, "dve_chain")
                link(e.memset(z[:, :, 0:TAPS1 - 1], 0.0))
                link(e.tensor_tensor(z[:, :, TAPS1 - 1:], bcu[:, 4:8, :], bcu[:, 8:12, :], ALU.mult))
                for c in range(4):
                    e.tensor_scalar(y[:, c, :], z[:, c, 0:S], col("conv_w", c, 1), None, ALU.mult)
                for tap in (1, 2):
                    link(e.engine_nop())
                    for c in range(4):
                        last = e.scalar_tensor_tensor(y[:, c, :], z[:, c, tap:tap + S], col("conv_w", 4 * tap + c, 1),
                                                      y[:, c, :], ALU.mult, ALU.add)
                link(last)
                link(e.tensor_tensor(y, y, bcu[:, 0:4, :], ALU.mult))
                e.tensor_tensor(tmp[:, 0:4, :], y, y, ALU.mult).then_inc(squares, 1)
                e.wait_ge(sums, 1)
                link(e.tensor_scalar(z[:, :, 0:S], ps[:, 0:4, :], 1.0 / HEAD, EPS, ALU.mult, ALU.add))
                e.reciprocal(z[:, :, 0:S], z[:, :, 0:S]).then_inc(inverse, 1)
                e.wait_ge(masked, 3)

                def finish(t):
                    e.wait_ge(valued, 4 * t + 4)
                    a3 = ao.rearrange("p (h d) -> p h d", d=HEAD)
                    s3 = sq.rearrange("p (h d) -> p h d", d=HEAD)
                    if t:
                        e.wait_ge(oT, t)
                    link(e.tensor_tensor(a3, ps[:, 6, :].rearrange("p (h d) -> p h d", d=HEAD),
                                         bc(rd.unsqueeze(2), HEADS1, HEAD), ALU.mult))
                    link(e.tensor_tensor(sq, ao, ao, ALU.mult))
                    link(e.tensor_reduce(hs, s3, AX, ALU.add))
                    link(e.tensor_scalar(hr, hs, 1.0 / HEAD, EPS, ALU.mult, ALU.add))
                    e.reciprocal(hr, hr).then_inc(hinv, 1)
                    e.wait_ge(hroot, t + 1)
                    link(e.tensor_tensor(a3, a3, bc(hr.unsqueeze(2), HEADS1, HEAD), ALU.mult))
                    e.tensor_tensor(ao, ao, row("attn_out_g"), ALU.mult).then_inc(normed, 1)

                for t in range(T):
                    e.wait_ge(scored, t + 1)
                    if t:
                        e.wait_ge(turned, 4 * t)
                    w = 2 * P - lo(t)
                    s3 = sc[:, :, lo(t):]
                    e.scalar_tensor_tensor(
                        s3, ps[:, 0:4, :].rearrange("p b (h k) -> p (b h) k", k=2 * P)[:, :, lo(t):], HEAD ** -0.5,
                        bc(mask[:, lo(t):].unsqueeze(1), HEADS1, w), ALU.mult, ALU.add).then_inc(read, 1)
                    e.wait_ge(read, t + 1)
                    link(e.tensor_reduce(mx, s3, AX, ALU.max))
                    link(e.tensor_tensor(mx, mx, row("sinks"), ALU.max))
                    link(e.tensor_tensor(es, row("sinks"), mx, ALU.subtract))
                    e.tensor_scalar(mx, mx, -1.0, None, ALU.mult).then_inc(expd, 1)
                    e.wait_ge(prob, t + 1)
                    link(e.tensor_tensor(den, den, es, ALU.add))
                    link(e.reciprocal(rd, den))
                    finish(t)
                e.wait_ge(rooted, 1)
                link(e.tensor_tensor(y, y, z[:, :, 0:S], ALU.mult))
                for c in range(4):
                    e.tensor_scalar(hT[:, 4 + c, :], y[:, c, :], col("conv_out_g", c, 1), None, ALU.mult)

            def act(e):
                e.wait_ge(inverse, 1)
                e.activation(z[:, :, 0:S], z[:, :, 0:S], ACT.Sqrt).then_inc(rooted, 1)

                def out_copy(t):
                    e.wait_ge(oT, t + 1)
                    e.activation(hT[:, 0:4, t * P:(t + 1) * P], ps[:, 7, :].rearrange("p (c q) -> p c q", q=P),
                                 ACT.Copy).then_inc(oC, 1)

                for t in range(T):
                    e.wait_ge(expd, t + 1)
                    e.activation(es, es, ACT.Exp)
                    for h in range(HEADS1):
                        last = e.activation(sc[:, h, lo(t):], sc[:, h, lo(t):], ACT.Exp, bias=mx[:, h:h + 1],
                                            accum_out=den[:, h:h + 1])
                    last.then_inc(prob, 1)
                    if t:
                        out_copy(t - 1)
                    for pair in range(4):
                        n = 4 * t + pair
                        e.wait_ge(turned, n + 1)
                        if n >= 4:
                            e.wait_ge(valued, n - 3)
                        src = ps[:, 4 + n % 2, :].rearrange("p (b q) -> p b q", q=P)
                        if t:
                            e.activation(pt[:, n % 4, :, :], src, ACT.Copy).then_inc(copied, 1)
                        else:
                            e.activation(pt[:, n % 4, 1::2, :], src[:, 1::2, :], ACT.Copy).then_inc(copied, 1)
                    e.wait_ge(hinv, t + 1)
                    e.activation(hr, hr, ACT.Sqrt).then_inc(hroot, 1)
                out_copy(T - 1)
            stage(pe=pe, act=act, dve=dve, pool=pool)

        def residual_stage(tag, gate=None, bias=None, src=None):
            s0 = slabs(2)
            src = hT if src is None else src
            brow, at = area(0, D)
            tmp, at = area(at, 2, N)
            r = call("residual")
            done = shared("residual_done")

            def act(e):
                if bias is not None:
                    e.dma_start(brow, bias.partition_broadcast(P)).then_inc(loaded, 16)

            def pe(e):
                for n in range(2):
                    await_slab(e, s0 + n)
                    w = slab_k(s0 + n)
                    for t in range(T):
                        for k in range(KC):
                            mm = e.matmul(ps[:, 4 * n + t, :], src[:, k, t * P:(t + 1) * P], w[:, k, :],
                                          start=k == 0, stop=k == KC - 1)
                        mm.then_inc(done, 1)
                    e.wait_ge(done, 8 * r + 4 * n + 4)
                    e.sem_inc(slab_used, 1)

            def dve(e):
                link = chain(e, "dve_chain")
                if bias is not None:
                    e.wait_ge(loaded, 96)
                for n in range(2):
                    cs = slice(n * N, (n + 1) * N)
                    for t in range(T):
                        e.wait_ge(done, 8 * r + 4 * n + t + 1)
                        src_ = ps[:, 4 * n + t, :]
                        if bias is not None:
                            link(e.tensor_tensor(tmp[:, 0, :], src_, brow[:, cs], ALU.add))
                            src_ = tmp[:, 0, :]
                        if gate is not None:
                            link(e.tensor_tensor(tmp[:, 1, :], src_, gate[:, cs], ALU.mult))
                            src_ = tmp[:, 1, :]
                        link(e.tensor_tensor(x[:, t, cs], x[:, t, cs], src_, ALU.add))
            stage(pe=pe, act=act, dve=dve)

        def route_stage():
            s0 = slabs(5)
            qT, at = area(0, 16, S)
            s1, at = area(at, 16, KEYS)
            s2, at = area(at, 16, KEYS)
            cand, at = area(at, PH, TOPK * TOPK)
            cand2 = s2.rearrange("p a b -> p (a b)").rearrange("p (h c) -> p h c", c=TOPK * TOPK)
            vals, at = area(at, 16, TOPK)
            idx, at = area(at, 16, TOPK)
            fidx, at = area(at, 16, TOPK)
            top, at = area(at, PH, TOPK)
            ci, at = area(at, PH, TOPK)
            cab, at = area(at, 2, PH * TOPK)
            fab, at = area(at, 2, PH * TOPK)
            eg, at = area(at, 3, PH * TOPK)
            gsum, at = area(at, PH)
            assert at <= 2 * KEYS * GT
            egT, at = area(2 * KEYS * GT, 3, S)
            done, freed = sem("rt_done"), sem("rt_freed")
            scored, read, expd, gated, ready, turned = (
                sem("rt_" + n) for n in ("scored", "read", "exp", "gated", "ready", "turned"))

            def pe(e):
                for i in range(4):
                    await_slab(e, s0 + i)
                    w = slab_k(s0 + i)
                    for j in range(4):
                        g = 4 * i + j
                        if g >= 8:
                            e.wait_ge(freed, g - 7)
                        for k in range(KC):
                            mm = e.matmul(ps[:, g % 8, :], w[:, k, j * P:(j + 1) * P], hT[:, k, :],
                                          start=k == 0, stop=k == KC - 1)
                        mm.then_inc(done, 1)
                    e.wait_ge(done, 4 * i + 4)
                    e.sem_inc(slab_used, 1)
                await_slab(e, s0 + 4)
                keys = slab(s0 + 4)
                e.wait_ge(freed, 16)

                def turn(t):
                    e.wait_ge(ready, t + 1)
                    for i in range(3):
                        mm = e.transpose(ps[:, 7, i * P:(i + 1) * P], eg[:, i, :], ident[:])
                    mm.then_inc(turned, 1)

                for t in range(T):
                    if t:
                        e.wait_ge(read, t)
                    for c in range(16):
                        mm = e.matmul(ps[:, c // 4, (c % 4) * P:(c % 4 + 1) * P], qT[:, c, t * P:(t + 1) * P],
                                      keys[:, c * KEYS:(c + 1) * KEYS], start=True, stop=True)
                    mm.then_inc(scored, 1)
                    if t:
                        turn(t - 1)
                e.wait_ge(scored, T)
                e.sem_inc(slab_used, 1)
                turn(T - 1)

            def act(e):
                for g in range(16):
                    e.wait_ge(done, g + 1)
                    e.activation(qT[:, g, :], ps[:, g % 8, :], ACT.Copy).then_inc(freed, 1)
                for t in range(T):
                    e.wait_ge(expd, t + 1)
                    e.activation(top, top, ACT.Exp).then_inc(gated, 1)

            def dve(e):
                link = chain(e, "dve_chain")
                for t in range(T):
                    e.wait_ge(scored, t + 1)
                    e.tensor_copy(s1, ps[:, 0:4, :].rearrange("p b (c k) -> p (b c) k", k=KEYS)).then_inc(read, 1)
                    e.wait_ge(read, t + 1)

                    def top16(n, src, spare, v, i):
                        for c in range(n):
                            last = e.max(v[:, c, 0:8], src[:, c, :])
                        link(last)
                        for c in range(n):
                            e.max_index(i[:, c, 0:8].bitcast(U32), v[:, c, 0:8], src[:, c, :])
                            last = e.match_replace(spare[:, c, :], v[:, c, 0:8], src[:, c, :], LOWEST)
                        link(last)
                        for c in range(n):
                            last = e.max(v[:, c, 8:16], spare[:, c, :])
                        link(last)
                        for c in range(n):
                            last = e.max_index(i[:, c, 8:16].bitcast(U32), v[:, c, 8:16], spare[:, c, :])
                        link(last)

                    top16(16, s1, s2, vals, idx)
                    link(e.tensor_copy(fidx, idx.bitcast(U32)))
                    v4 = vals.rearrange("p (h a) k -> p h a k", a=2)
                    for h in range(PH):
                        last = e.tensor_tensor(cand[:, h, :].rearrange("p (a b) -> p a b", b=TOPK),
                                               bc(v4[:, h, 0, :].unsqueeze(2), TOPK, TOPK),
                                               bc(v4[:, h, 1, :].unsqueeze(1), TOPK, TOPK), ALU.add)
                    link(last)
                    top16(PH, cand, cand2, top, ci)
                    ciu = ci.bitcast(U32).rearrange("p h k -> p (h k)")
                    e.tensor_scalar(cab[:, 0, :].bitcast(U32), ciu, 4, None, ALU.logical_shift_right)
                    link(e.tensor_scalar(cab[:, 1, :].bitcast(U32), ciu, 15, None, ALU.bitwise_and))
                    link(e.tensor_copy(fab, cab.bitcast(U32)))
                    link(e.tensor_copy(gsum, top[:, :, 0]))
                    e.tensor_tensor(top, top, bc(gsum.unsqueeze(2), PH, TOPK), ALU.subtract).then_inc(expd, 1)
                    if t:
                        e.wait_ge(turned, t)
                    f4 = fidx.rearrange("p (h a) k -> p h a k", a=2)
                    for a in range(2):
                        for h in range(PH):
                            last = e.tensor_tensor(cand[:, h, :].rearrange("p (k j) -> p k j", j=TOPK),
                                                   bc(fab[:, a, h * TOPK:(h + 1) * TOPK].unsqueeze(2), TOPK, TOPK),
                                                   bc(iota[:, 0:TOPK].unsqueeze(1), TOPK, TOPK), ALU.is_equal)
                        link(last)
                        for h in range(PH):
                            last = e.tensor_tensor(cand2[:, h, :].rearrange("p (k j) -> p k j", j=TOPK),
                                                   cand[:, h, :].rearrange("p (k j) -> p k j", j=TOPK),
                                                   bc(f4[:, h, a, :].unsqueeze(1), TOPK, TOPK), ALU.mult)
                        link(last)
                        link(e.tensor_reduce(eg[:, a, :], cand2.rearrange("p h (k j) -> p (h k) j", j=TOPK), AX,
                                             ALU.add))
                    e.wait_ge(gated, t + 1)
                    link(e.tensor_reduce(gsum, top, AX, ALU.add))
                    link(e.reciprocal(gsum, gsum))
                    e.tensor_tensor(eg[:, 2, :].rearrange("p (h k) -> p h k", k=TOPK), top,
                                    bc(gsum.unsqueeze(2), PH, TOPK), ALU.mult).then_inc(ready, 1)
                    e.wait_ge(turned, t + 1)
                    e.tensor_copy(egT[:, :, t * P:(t + 1) * P], ps[:, 7, 0:3 * P].rearrange("p (a q) -> p a q", q=P))
            stage(pe=pe, act=act, dve=dve)
            return egT

        GB = 8
        NB = GT // GB

        def gate_stage(egT):
            stg, at = area(0, 2, KEYS, GT)
            oh, at = area(at + 3 * S, 2 * GB, 2, KEYS)
            one_hot, oh_used, copied = (sem("gm_" + n) for n in ("oh", "ohused", "copy"))
            written = [sem(f"gm_written{i}") for i in range(2)]

            def dve(e):
                with e.Fori(0, S // (2 * GB)) as i:
                    for j in range(2 * GB):
                        tok = i * (2 * GB) + j
                        e.wait_ge(oh_used, tok + 1)
                        e.tensor_scalar(oh[:, j, 0, :], iota[:], egT[:, 0, bass.ds(tok, 1)], None, ALU.is_equal)
                        e.tensor_scalar(oh[:, j, 1, :], iota[:], egT[:, 1, bass.ds(tok, 1)],
                                        egT[:, 2, bass.ds(tok, 1)], ALU.is_equal, ALU.mult).then_inc(one_hot, 1)

            def pe(e):
                e.sem_inc(oh_used, 2 * GB)
                with e.Fori(0, S // (2 * GB)) as i:
                    for j in range(2 * GB):
                        if j % 4 == 0:
                            e.wait_ge(copied, i * 4 + j // 4 + 1)
                        e.wait_ge(one_hot, i * (2 * GB) + j + 1)
                        mm = e.matmul(ps[:, j // 4, (j % 4) * P:(j % 4 + 1) * P], oh[:, j, 0, :], oh[:, j, 1, :],
                                      start=True, stop=True)
                        mm.then_inc(oh_used, 1)

            def act(e):
                e.sem_inc(copied, 4)
                for b in range(2):
                    e.sem_inc(written[b], 16)
                quads = GT // 4
                with e.Fori(0, NG // 2) as i:
                    for b in range(2):
                        e.wait_ge(written[b], i * 16 + 16)
                        for q in range(quads):
                            e.wait_ge(oh_used, i * (2 * GT) + (b * GT + 4 * q + 4 + 2 * GB))
                            e.activation(stg[:, b, :, 4 * q:4 * q + 4],
                                         ps[:, q % 4, :].rearrange("p (t k) -> p k t", k=KEYS),
                                         ACT.Copy).then_inc(copied, 1)
                        e.wait_ge(copied, i * (2 * quads) + ((b + 1) * quads + 4))
                        e.dma_start(gates_dram[:, :, bass.ds(i * 2 + b, 1), :].rearrange("c p g n -> p (c g) n"),
                                    stg[:, b, :, :].rearrange("p (c k) t -> p c (k t)", k=E2C)
                                    ).then_inc(written[b], 16)
                for b in range(2):
                    e.wait_ge(written[b], 16 + 16 * (NG // 2))
            stage(pe=pe, act=act, dve=dve)

        def expert_stage():
            s0 = slabs(2 * ECH)
            g, at = area(0, 2, NG, E2C * GT)
            w, at = area(at, 2, E2C, S)
            acc, at = area(at, T, D)
            scored, acted, weighted, summed, added = (
                sem("ex_" + n) for n in ("scored", "acted", "weighted", "summed", "added"))
            g_in = [sem(f"ex_g{i}") for i in range(2)]

            def pe(e):
                def wait_slab(q, m=0):
                    i = s0 + q
                    e.wait_ge(slab_in[i % RING], m * 16 + 16 * (i // RING + 1))

                def score(q, c, first=False, m=0, c0=0, release=None):
                    u = slab(s0 + q).rearrange("p (k j n) -> p k j n", k=KC, j=E2C)
                    wait_slab(q, m)
                    for j in range(E2C):
                        if not first:
                            e.wait_ge(acted, m * E2C * 2 + E2C * (c - 1) + j + 1)
                        for k in range(KC):
                            mm = e.matmul(ps[:, j, :], u[:, k, j, :], hT[:, k, :], start=k == 0, stop=k == KC - 1)
                        mm.then_inc(scored, 1)
                        if j == 0 and release:
                            release()

                def gather(q, c, m=0, release=None):
                    v = slab(s0 + q).rearrange("p (j n) -> p j n", j=E2C)
                    wait_slab(q, m)
                    e.wait_ge(weighted, m * E2C * 2 + E2C * (c + 1))
                    for n in range(2):
                        for t in range(T):
                            i = n * T + t
                            if 8 * c + i >= 4:
                                e.wait_ge(added, m * 16 + 8 * c + i - 3)
                            for j in range(E2C):
                                mm = e.matmul(ps[:, 4 + t, :], w[:, c % 2, j, t * P:(t + 1) * P],
                                              v[:, j, n * N:(n + 1) * N], start=j == 0, stop=j == E2C - 1)
                            mm.then_inc(summed, 1)
                            if i == 0 and release:
                                release()

                def release(sem_, n):
                    def f():
                        e.wait_ge(sem_, n)
                        e.sem_inc(slab_used, 1)
                    return f

                score(0, 0, first=True)
                score(1, 1, release=release(scored, E2C))
                gather(2, 0, release=release(scored, 2 * E2C))
                with e.Fori(0, (ECH - 2) // 2) as m:
                    for a in range(2):
                        c, q = 2 + a, 3 + 2 * a
                        score(q, c, m=m, release=release(summed, m * 16 + 8 * (c - 1)))
                        gather(q + 1, c - 1, m=m, release=release(scored, m * E2C * 2 + E2C * (c + 1)))
                gather(2 * ECH - 1, ECH - 1, release=release(summed, 8 * (ECH - 1)))
                e.wait_ge(summed, 8 * ECH)
                e.sem_inc(slab_used, 1)

            def act(e):
                def gelu(c, j, m=0):
                    e.wait_ge(scored, m * E2C * 2 + E2C * c + j + 1)
                    e.activation(w[:, c % 2, j, :], ps[:, j, :], ACT.Gelu).then_inc(acted, 1)
                for c in range(2):
                    for j in range(E2C):
                        gelu(c, j)
                with e.Fori(0, (ECH - 2) // 2) as m:
                    for c in (2, 3):
                        e.wait_ge(summed, m * 16 + 8 * (c - 1))
                        for j in range(E2C):
                            gelu(c, j, m)

            def pool(e):
                for b in range(2):
                    e.dma_start(g[:, b, :, :], gates_dram[b]).then_inc(g_in[b], 16)
                with e.Fori(0, (ECH - 2) // 2) as m:
                    for b in range(2):
                        e.wait_ge(weighted, m * E2C * 2 + E2C * (b + 1))
                        e.dma_start(g[:, b, :, :], gates_dram[m * 2 + (b + 2)]).then_inc(g_in[b], 16)

            def dve(e):
                def weigh(c, m=0):
                    e.wait_ge(g_in[c % 2], m * 16 + 16 * (c // 2 + 1))
                    for j in range(E2C):
                        e.wait_ge(acted, m * E2C * 2 + E2C * c + j + 1)
                        wj = w[:, c % 2, j, :].rearrange("p (g t) -> p g t", t=GT)
                        e.tensor_tensor(wj, wj, g[:, c % 2, :, j * GT:(j + 1) * GT], ALU.mult).then_inc(weighted, 1)

                def add(c, m=0, first=False):
                    for n in range(2):
                        for t in range(T):
                            e.wait_ge(summed, m * 16 + 8 * c + n * T + t + 1)
                            dst = acc[:, t, n * N:(n + 1) * N]
                            if first:
                                e.tensor_copy(dst, ps[:, 4 + t, :]).then_inc(added, 1)
                            else:
                                e.tensor_tensor(dst, dst, ps[:, 4 + t, :], ALU.add).then_inc(added, 1)

                weigh(0)
                weigh(1)
                add(0, first=True)
                with e.Fori(0, (ECH - 2) // 2) as m:
                    for c in (2, 3):
                        weigh(c, m)
                        e.wait_ge(added, m * 16 + 8 * (c - 1))
                        add(c - 1, m)
                e.wait_ge(added, 8 * (ECH - 1))
                add(ECH - 1)
            stage(pe=pe, act=act, dve=dve, pool=pool)
            return acc

        def close_stage(acc):
            frow, _ = area(8192 - D, D)
            sq, ss, rs = w_spare = area(4096, D)[0], small[:, 0:T], small[:, T:2 * T]
            squared, inverse, rooted, fed = (sem("cl_" + n) for n in ("sq", "inv", "root", "fed"))

            def act(e):
                e.dma_start(frow, A["final_g"].partition_broadcast(P)).then_inc(loaded, 16)
                for t in range(T):
                    e.wait_ge(fed, t + 1)
                    if t:
                        e.wait_ge(squared, t)
                    e.activation(sq, x[:, t, :], ACT.Square, accum_out=ss[:, t:t + 1]).then_inc(squared, 1)
                e.wait_ge(inverse, 1)
                e.activation(rs, rs, ACT.Sqrt).then_inc(rooted, 1)

            def dve(e):
                link = chain(e, "dve_chain")
                e.wait_ge(loaded, 112)
                for t in range(T):
                    link(e.tensor_tensor(acc[:, t, :], acc[:, t, :], gate2, ALU.mult))
                    e.tensor_tensor(x[:, t, :], x[:, t, :], acc[:, t, :], ALU.add).then_inc(fed, 1)
                e.wait_ge(squared, T)
                link(e.tensor_scalar(rs, ss, 1.0 / D, EPS, ALU.mult, ALU.add))
                e.reciprocal(rs, rs).then_inc(inverse, 1)
                e.wait_ge(rooted, 1)
                for t in range(T):
                    link(e.scalar_tensor_tensor(x[:, t, :], x[:, t, :], rs[:, t:t + 1], frow, ALU.mult, ALU.mult))
            stage(act=act, dve=dve)

        def attention_stage():
            s0 = slabs(6)
            ao, at = area(0, T, D)
            qT, at = area(at, KC, S)
            kT, at = area(at, KC, S)
            v, at = area(at, T, D)
            strip, at = area(at, 2, S)
            sc, at = area(at, 3, S)
            pt, at = area(at, 3, S)
            U = HEADS2 * T
            den, neg = small[:, 64:64 + U], small[:, 128:128 + U]
            done, freed = sem("qkv_done"), sem("qkv_freed")
            scored, read, maxed, expd, turned, copied, valued, taken_o, strip_ok = (
                sem("at_" + n) for n in ("scored", "read", "maxed", "exp", "turned", "copied", "valued", "taken", "strip"))
            strip_in = [sem(f"at_strip{i}") for i in range(2)]
            rel = A["rel"]

            def pool(e):
                for b in range(2):
                    e.memset(strip[0:64, b, 0:CHUNK], NEG).then_inc(strip_ok, 1)
                for h in range(HEADS2):
                    if h >= 2:
                        e.wait_ge(read, 4 * (h - 1))
                    for r0, n0 in ((0, CHUNK), (64, 0)):
                        e.dma_start(strip[r0:r0 + 64, h % 2, n0:],
                                    bass.AP(rel.tensor, h * rel.shape[1] + r0 + n0, [[1, 64], [1, S - n0]])
                                    ).then_inc(strip_in[h % 2], 16)

            def pe(e):
                for i in range(6):
                    await_slab(e, s0 + i)
                    w = slab_k(s0 + i)
                    for j in range(4):
                        g = 4 * i + j
                        if g >= 8:
                            e.wait_ge(freed, g - 7)
                        for k in range(KC):
                            if i < 4:
                                mm = e.matmul(ps[:, g % 8, :], w[:, k, j * P:(j + 1) * P], hT[:, k, :],
                                              start=k == 0, stop=k == KC - 1)
                            else:
                                mm = e.matmul(ps[:, g % 8, :], hT[:, k, j * P:(j + 1) * P], w[:, k, :],
                                              start=k == 0, stop=k == KC - 1)
                        mm.then_inc(done, 1)
                    e.wait_ge(done, 4 * i + 4)
                    e.sem_inc(slab_used, 1)
                e.wait_ge(freed, 24)

                def values(u):
                    h, t = u // T, u % T
                    e.wait_ge(copied, u + 1)
                    if u % 8 == 0 and u >= 16:
                        e.wait_ge(taken_o, u // 8 - 1)
                    for kb in range(t + 1):
                        mm = e.matmul(ps[:, 4 + (u // 8) % 2, (u % 8) * HEAD:(u % 8 + 1) * HEAD],
                                      pt[:, u % 3, kb * P:(kb + 1) * P], v[:, kb, h * HEAD:(h + 1) * HEAD],
                                      start=kb == 0, stop=kb == t)
                    mm.then_inc(valued, 1)

                for u in range(U + 2):
                    if u < U:
                        h, t = u // T, u % T
                        b = 64 * (h % 2)
                        if u >= 2:
                            e.wait_ge(read, u - 1)
                        e.matmul(ps[:, u % 2, 0:(t + 1) * P], qT[b:b + 64, h // 2, t * P:(t + 1) * P],
                                 kT[b:b + 64, h // 2, 0:(t + 1) * P], start=True, stop=True).then_inc(scored, 1)
                    if 1 <= u <= U:
                        w = u - 1
                        e.wait_ge(expd, w + 1)
                        if w >= 2:
                            e.wait_ge(copied, w - 1)
                        for kb in range(w % T + 1):
                            mm = e.transpose(ps[:, 2 + w % 2, kb * P:(kb + 1) * P], sc[:, w % 3, kb * P:(kb + 1) * P],
                                             ident[:])
                        mm.then_inc(turned, 1)
                    if u >= 2:
                        values(u - 2)

            def act(e):
                for u in range(U + 1):
                    if u < U:
                        w = (u % T + 1) * P
                        e.wait_ge(maxed, u + 1)
                        e.activation(sc[:, u % 3, 0:w], sc[:, u % 3, 0:w], ACT.Exp, bias=neg[:, u:u + 1],
                                     accum_out=den[:, u:u + 1]).then_inc(expd, 1)
                    if u >= 1:
                        a = u - 1
                        w = (a % T + 1) * P
                        e.wait_ge(turned, a + 1)
                        if a >= 3:
                            e.wait_ge(valued, a - 2)
                        e.activation(pt[:, a % 3, 0:w], ps[:, 2 + a % 2, 0:w], ACT.Copy).then_inc(copied, 1)

            def dve(e):
                link = chain(e, "dve_chain")
                for g in range(24):
                    e.wait_ge(done, g + 1)
                    dst = qT[:, g, :] if g < 8 else kT[:, g - 8, :] if g < 16 else v[:, g % 4, (g // 4 - 4) * N:(g // 4 - 3) * N]
                    e.tensor_copy(dst, ps[:, g % 8, :]).then_inc(freed, 1)
                e.wait_ge(strip_ok, 2)

                def backwards(h, w):
                    f = strip[:, h % 2, 0:w]
                    return bass.AP(f.tensor, f.offset + w - 1, [list(f.ap[0]), [-1, w]])

                def take(g):
                    e.wait_ge(valued, 8 * g + 8)
                    e.tensor_copy(ao.rearrange("p t (h d) -> p h t d", d=HEAD)[:, 2 * g:2 * g + 2, :, :],
                                  ps[:, 4 + g % 2, :].rearrange("p (h t d) -> p h t d", h=2, t=T)).then_inc(taken_o, 1)

                for u in range(U):
                    h, t = u // T, u % T
                    w = (t + 1) * P
                    e.wait_ge(scored, u + 1)
                    if t == 0:
                        e.wait_ge(strip_in[h % 2], 32 * (h // 2 + 1))
                    if u >= 3:
                        e.wait_ge(turned, u - 2)
                    e.scalar_tensor_tensor(sc[:, u % 3, 0:w], ps[:, u % 2, 0:w], HEAD ** -0.5,
                                           backwards(h, w), ALU.mult, ALU.add).then_inc(read, 1)
                    e.wait_ge(read, u + 1)
                    e.tensor_reduce(neg[:, u:u + 1], sc[:, u % 3, 0:w], AX, ALU.max, negate=True).then_inc(maxed, 1)
                    if u >= 12 and (u - 12) % 8 == 0:
                        take((u - 12) // 8)
                take(7)
                e.wait_ge(expd, U)
                link(e.reciprocal(den, den))
                for t in range(T):
                    a3 = ao[:, t, :].rearrange("p (h d) -> p h d", d=HEAD)
                    if t == 0:
                        e.wait_ge(taken_o, 8)
                    e.tensor_tensor(a3, a3, bc(den.rearrange("p (h t) -> p h t", t=T)[:, :, t].unsqueeze(2), HEADS2, HEAD),
                                    ALU.mult)
            stage(pe=pe, act=act, dve=dve, pool=pool)
            return ao

        def turn_stage(src):
            r = call("turn")
            turned = shared("turn_turned")

            def pe(e):
                for c in range(KC):
                    for t in range(T):
                        mm = e.transpose(ps[:, c, t * P:(t + 1) * P], src[:, t, c * P:(c + 1) * P], ident[:])
                    mm.then_inc(turned, 1)

            def act(e):
                for c in range(0, KC, 2):
                    e.wait_ge(turned, KC * r + c + 1)
                    e.activation(hT[:, c, :], ps[:, c, :], ACT.Copy)

            def dve(e):
                for c in range(1, KC, 2):
                    e.wait_ge(turned, KC * r + c + 1)
                    e.tensor_copy(hT[:, c, :], ps[:, c, :])
            stage(pe=pe, act=act, dve=dve)

        def mlp_stage():
            s0 = slabs(16)
            f, at = area(0, FC, S)
            tmp, at = area(at, 2, S)
            r = call("mlp")
            up, rect, squared, down = (shared("mlp_" + n) for n in ("up", "rect", "squared", "down"))

            def pe(e):
                for i in range(8):
                    await_slab(e, s0 + i)
                    w = slab_k(s0 + i)
                    for j in range(4):
                        g = 4 * i + j
                        if g >= 8:
                            e.wait_ge(rect, r * FC + g - 7)
                        for k in range(KC):
                            mm = e.matmul(ps[:, g % 8, :], w[:, k, j * P:(j + 1) * P], hT[:, k, :],
                                          start=k == 0, stop=k == KC - 1)
                        mm.then_inc(up, 1)
                    e.wait_ge(up, r * FC + 4 * i + 4)
                    e.sem_inc(slab_used, 1)
                e.wait_ge(rect, (r + 1) * FC)
                for n in range(2):
                    for kb in range(4):
                        i = s0 + 8 + 4 * n + kb
                        await_slab(e, i)
                        w = slab_k(i)
                        if n == 0:
                            e.wait_ge(squared, r * FC + 8 * kb + 8)
                        for t in range(T):
                            for k in range(KC):
                                mm = e.matmul(ps[:, 4 * n + t, :], f[:, kb * KC + k, t * P:(t + 1) * P], w[:, k, :],
                                              start=kb == 0 and k == 0, stop=kb == 3 and k == KC - 1)
                            mm.then_inc(down, 1)
                        e.wait_ge(down, r * 32 + 16 * n + 4 * kb + 4)
                        e.sem_inc(slab_used, 1)

            def act(e):
                for g in range(FC):
                    e.wait_ge(up, r * FC + g + 1)
                    if g >= 2:
                        e.wait_ge(squared, r * FC + g - 1)
                    e.activation(tmp[:, g % 2, :], ps[:, g % 8, :], ACT.Relu).then_inc(rect, 1)

            def dve(e):
                for g in range(FC):
                    e.wait_ge(rect, r * FC + g + 1)
                    e.tensor_tensor(f[:, g, :], tmp[:, g % 2, :], tmp[:, g % 2, :], ALU.mult).then_inc(squared, 1)
                for n in range(2):
                    for t in range(T):
                        e.wait_ge(down, r * 32 + 16 * n + 12 + t + 1)
                        cs = slice(n * N, (n + 1) * N)
                        e.tensor_tensor(x[:, t, cs], x[:, t, cs], ps[:, 4 * n + t, :], ALU.add)
            stage(pe=pe, act=act, dve=dve)

        def dn_in_stage():
            s0 = slabs(8)
            qT, at = area(0, DNH, S)
            kT, at = area(at, DNH, S)
            k_, at = area(at, T, D)
            v, at = area(at, T, D)
            z, at = area(at, T, D)
            PAD = TAPS2 - 1
            zin, at = area(at, 2, S + PAD)
            y, at = area(at, 2, S)
            vt = k_[:, 0, :].rearrange("p (a b) -> p a b", b=S)
            ab = small[:, 192:192 + 64].rearrange("p (t c) -> p t c", c=2 * DNH)
            done, freed, filled, conved, silued, vturned, vcopied = (
                sem("dp_" + n) for n in ("done", "freed", "filled", "conved", "silued", "vturned", "vcopied"))
            zdone, abdone, abread = sem("dp_zdone"), sem("dp_abdone"), sem("dp_abread")

            def pe(e):
                def turn_v(c):
                    e.wait_ge(silued, 16 + c + 1)
                    if c >= 2:
                        e.wait_ge(vcopied, c - 1)
                    for t in range(T):
                        mm = e.transpose(ps[:, 6 + c % 2, t * P:(t + 1) * P], vt[:, c % 2, t * P:(t + 1) * P], ident[:])
                    mm.then_inc(vturned, 1)
                w = col("dn_ab").rearrange("p (k c) -> p k c", c=2 * DNH)
                for t in range(T):
                    for k in range(KC):
                        mm = e.matmul(ps[:, 7, t * 16:(t + 1) * 16], hT[:, k, t * P:(t + 1) * P], w[:, k, :],
                                      start=k == 0, stop=k == KC - 1)
                mm.then_inc(abdone, 1)
                for i in range(8):
                    await_slab(e, s0 + i)
                    w = slab_k(s0 + i)
                    for j in range(4):
                        g = 4 * i + j
                        if g >= 6:
                            e.wait_ge(freed, g - 5)
                        if g == 24:
                            e.wait_ge(abread, 1)
                        for k in range(KC):
                            if i < 6:
                                mm = e.matmul(ps[:, g % 6, :], w[:, k, j * P:(j + 1) * P], hT[:, k, :],
                                              start=k == 0, stop=k == KC - 1)
                            else:
                                mm = e.matmul(ps[:, g % 6, :], hT[:, k, j * P:(j + 1) * P], w[:, k, :],
                                              start=k == 0, stop=k == KC - 1)
                        mm.then_inc(done, 1)
                        if 18 <= g < 26:
                            turn_v(g - 18)
                    e.wait_ge(done, 4 * i + 4)
                    e.sem_inc(slab_used, 1)

            def dst(g):
                return qT[:, g, :] if g < 8 else kT[:, g - 8, :] if g < 16 else vt[:, g % 2, :]

            def act(e):
                def silu(g):
                    e.wait_ge(conved, g + 1)
                    if g >= 18:
                        e.wait_ge(vturned, g - 17)
                    e.activation(dst(g), y[:, g % 2, :], ACT.Silu).then_inc(silued, 1)
                for g in range(24):
                    e.wait_ge(done, g + 1)
                    if g >= 2:
                        e.wait_ge(conved, g - 1)
                    e.activation(zin[:, g % 2, PAD:], ps[:, g % 6, :], ACT.Copy).then_inc(freed, 1)
                    if g:
                        silu(g - 1)
                silu(23)
                for g in range(24, 32):
                    e.wait_ge(done, g + 1)
                    e.activation(z[:, g % 4, (g // 4 - 6) * N:(g // 4 - 5) * N], ps[:, g % 6, :],
                                 ACT.Silu).then_inc(freed, 1)

            def dve(e):
                link = chain(e, "dve_chain")
                link(e.memset(zin[:, :, 0:PAD], 0.0))
                e.wait_ge(abdone, 1)
                e.tensor_copy(ab, ps[:, 7, 0:64].rearrange("p (t c) -> p t c", c=16)).then_inc(abread, 1)
                cw = col("dn_conv_w")

                def copy_v(c):
                    e.wait_ge(vturned, c + 1)
                    e.tensor_copy(v[:, :, c * P:(c + 1) * P],
                                  ps[:, 6 + c % 2, :].rearrange("p (t q) -> p t q", q=P)).then_inc(vcopied, 1)
                for g in range(24):
                    e.wait_ge(freed, g + 1)
                    if g >= 2:
                        e.wait_ge(silued, g - 1)
                    zi, yo = zin[:, g % 2, :], y[:, g % 2, :]
                    link(e.tensor_scalar(yo, zi[:, 0:S], cw[:, g:g + 1], None, ALU.mult))
                    for tap in range(1, TAPS2):
                        ins = e.scalar_tensor_tensor(yo, zi[:, tap:tap + S], cw[:, 24 * tap + g:24 * tap + g + 1], yo,
                                                     ALU.mult, ALU.add)
                        if tap < TAPS2 - 1:
                            link(ins)
                    ins.then_inc(conved, 1)
                    if g >= 20:
                        copy_v(g - 20)
                for c in range(4, 8):
                    copy_v(c)
            stage(pe=pe, act=act, dve=dve)
            return qT, kT, k_, v, z, ab, at

        G_, BETA, EGC, REST, BEGC, EGL, GC = (small[:, 256 + 32 * i:288 + 32 * i] for i in range(7))
        EGL2 = small[:, 480:512]

        def dn_unit_stage(qT, kT, k_, v, z, ab, at):
            sqb, at = area(at - 2 * S - 2 * (S + 3), 2, S)
            squared, summed, summed_read, inverse, rooted, unit, turned = (
                sem("du_" + n) for n in ("sq", "sum", "sumread", "inv", "root", "unit", "turned"))
            ready, logs, sums, gsum, acted = (sem("du_" + n) for n in ("ready", "logs", "sums", "gsum", "acted"))
            tmp = small[:, 0:64]
            t8 = "p (t h) -> p t h"

            def act(e):
                for a, src in enumerate((qT, kT)):
                    for c in range(8):
                        n = 8 * a + c
                        if n >= 2:
                            e.wait_ge(summed, n - 1)
                        e.activation(sqb[:, c % 2, :], src[:, c, :], ACT.Square).then_inc(squared, 1)
                    e.wait_ge(inverse, 8 * (a + 1))
                    e.activation(hT[:], hT[:], ACT.Sqrt).then_inc(rooted, 1)
                e.wait_ge(ready, 1)
                e.activation(tmp[:, 0:32], tmp[:, 0:32], ACT.Exp, scale=-1.0)
                e.activation(small[:, 64:72], row("a_log"), ACT.Exp).then_inc(acted, 1)
                e.wait_ge(acted, 1)
                e.activation(tmp[:, 0:32], tmp[:, 0:32], ACT.Ln, bias=1.0)
                e.activation(BETA.rearrange(t8, h=DNH), ab[:, :, DNH:], ACT.Sigmoid).then_inc(acted, 1)
                e.wait_ge(sums, 1)
                for src in (EGC, REST, EGL, EGL2):
                    last = e.activation(src, src, ACT.Exp)
                last.then_inc(acted, 1)

            def pe(e):
                for n in range(16):
                    e.wait_ge(squared, n + 1)
                    if n >= 4:
                        e.wait_ge(summed_read, n - 3)
                    e.matmul(ps[:, n % 4, :], ones[:], sqb[:, n % 2, :], start=True, stop=True).then_inc(summed, 1)
                for c in range(DNH):
                    e.wait_ge(unit, 8 + c + 1)
                    if c >= 2:
                        e.wait_ge(turned, c - 1)
                    for t in range(T):
                        mm = e.transpose(ps[:, 4 + c % 2, t * P:(t + 1) * P], kT[:, c, t * P:(t + 1) * P], ident[:])
                    mm.then_inc(gsum, 1)
                e.wait_ge(logs, 1)
                e.matmul(ps[0:64, 6, 0:32], blk_tri[0:64, :], G_[0:64, :], start=True, stop=True)
                e.matmul(ps[64:128, 6, 0:32], blk_tri[64:128, :], G_[64:128, :], start=True, stop=True)
                e.matmul(ps[:, 6, 32:64], group64[:], G_, start=True, stop=True)
                e.matmul(ps[:, 6, 64:96], ones[0:64, :], G_[0:64, :], start=True, stop=True)
                e.matmul(ps[:, 7, 0:32], ones[64:128, :], G_[64:128, :], start=True, stop=True).then_inc(gsum, 1)

            def dve(e):
                link = chain(e, "dve_chain")
                a3 = tmp[:, 32:64].rearrange(t8, h=DNH)
                link(e.tensor_tensor(a3, ab[:, :, 0:DNH], bc(row("dt_bias").unsqueeze(1), T, DNH), ALU.add))
                link(e.scalar_tensor_tensor(tmp[:, 0:32], tmp[:, 32:64], -1.0, tmp[:, 32:64], ALU.mult, ALU.max))
                e.tensor_scalar(tmp[:, 32:64], tmp[:, 32:64], 0.0, None, ALU.max).then_inc(ready, 1)
                for a, src in enumerate((qT, kT)):
                    scale = float(DH) if a == 0 else 1.0
                    for c in range(8):
                        n = 8 * a + c
                        e.wait_ge(summed, n + 1)
                        if a == 1 and c == 0:
                            e.wait_ge(unit, 8)
                        e.tensor_scalar(hT[:, c, :], ps[:, n % 4, :], EPS, scale, ALU.add, ALU.mult).then_inc(summed_read, 1)
                        e.wait_ge(summed_read, n + 1)
                        e.reciprocal(hT[:, c, :], hT[:, c, :]).then_inc(inverse, 1)
                    e.wait_ge(rooted, a + 1)
                    for c in range(8):
                        e.tensor_tensor(src[:, c, :], src[:, c, :], hT[:, c, :], ALU.mult).then_inc(unit, 1)
                for c in range(DNH):
                    e.wait_ge(gsum, c + 1)
                    e.tensor_copy(k_[:, :, c * P:(c + 1) * P],
                                  ps[:, 4 + c % 2, :].rearrange("p (t q) -> p t q", q=P)).then_inc(turned, 1)
                e.wait_ge(acted, 2)
                link(e.tensor_tensor(tmp[:, 0:32], tmp[:, 0:32], tmp[:, 32:64], ALU.add))
                link(e.tensor_scalar(tmp[:, 0:32], tmp[:, 0:32], -1.0, None, ALU.mult))
                e.tensor_tensor(G_.rearrange(t8, h=DNH), tmp[:, 0:32].rearrange(t8, h=DNH),
                                bc(small[:, 64:72].unsqueeze(1), T, DNH), ALU.mult).then_inc(logs, 1)
                e.wait_ge(gsum, DNH + 1)
                link(e.tensor_copy(GC, ps[:, 6, 0:32]))
                e.tensor_copy(EGC, GC)
                e.tensor_copy(EGL, ps[:, 6, 64:96])
                e.tensor_copy(EGL2, ps[:, 7, 0:32])
                link(e.tensor_tensor(REST, ps[:, 6, 32:64], GC, ALU.subtract))
                e.sem_inc(sums, 1)
                e.wait_ge(acted, 3)
                link(e.tensor_tensor(BEGC, BETA, EGC, ALU.mult))
            stage(pe=pe, act=act, dve=dve)

        def dn_solve_stage(qT, kT, k_, v, z, ab, at):
            base = at - 2 * (S + 3) - 2 * S
            B4 = T * CHUNK
            mats = [area(base + hh * 6 * B4, 6, T, CHUNK)[0] for hh in range(2)]
            wide = [[area(base + hh * 6 * B4 + 2 * B4 * i, T, DH)[0] for i in range(3)] for hh in range(2)]
            qkT = gates.rearrange("p a b -> p (a b)").rearrange("p (h t c) -> p h t c", h=DNH, t=T)
            wT = hT
            DEC, QK, L, LT, X, XT = range(6)
            NP, ND, NA = 3 + 2 * (LEVELS - 1), 6 + 2 * (LEVELS - 1), 3
            pe_s, dve_s, act_s = sem("ds_pe"), sem("ds_dve"), sem("ds_act")
            halves = ((0, slice(0, 64)), (64, slice(64, 128)))

            def count(per, pair, step, hh):
                return pair * 2 * per + 2 * step + hh + 1

            def bank(hh, b):
                return ps[:, 4 * hh + b, :]

            def part(hh, b, half):
                return bank(hh, b)[:, half * B4:(half + 1) * B4].rearrange("p (t c) -> p t c", t=T)

            def pe(e):
                def blocks(out, lhs, rhs):
                    for t in range(T):
                        for _, sl in halves:
                            mm = e.matmul(out[sl, t, :], lhs(t, sl), rhs(t, sl), start=True, stop=True)
                    return mm

                def step(pair, n, hh):
                    h = 2 * pair + hh
                    m = mats[hh]
                    def wait_d(d):
                        e.wait_ge(dve_s, count(ND, pair, d, hh))

                    def tok(t, sl):
                        return slice(t * P + sl.start, t * P + sl.stop)
                    if n == 0:
                        wait_d(0)
                        if pair:
                            e.wait_ge(act_s, count(NA, pair - 1, 2, hh))
                        blocks(part(hh, 0, 0), lambda t, sl: ones[sl, 0:64], lambda t, sl: m[sl, L, t, :])
                        blocks(part(hh, 0, 1), lambda t, sl: kT[:, h, tok(t, sl)], lambda t, sl: kT[:, h, tok(t, sl)])
                        mm = blocks(part(hh, 1, 0), lambda t, sl: qT[:, h, tok(t, sl)],
                                    lambda t, sl: kT[:, h, tok(t, sl)])
                    elif n == 1:
                        wait_d(2)
                        blocks(part(hh, 2, 0), lambda t, sl: m[sl, L, t, :], lambda t, sl: ident[sl, sl])
                        mm = blocks(part(hh, 2, 1), lambda t, sl: m[sl, QK, t, :], lambda t, sl: ident[sl, sl])
                    elif n < NP - 1 and n % 2 == 0:
                        wait_d(3 + (n - 2))
                        mm = blocks(part(hh, 3, 0), lambda t, sl: m[sl, LT, t, :], lambda t, sl: m[sl, X, t, :])
                    elif n < NP - 1:
                        wait_d(3 + (n - 2))
                        blocks(part(hh, 0, 0), lambda t, sl: m[sl, XT, t, :], lambda t, sl: m[sl, DEC, t, :])
                        mm = blocks(part(hh, 0, 1), lambda t, sl: m[sl, DEC, t, :], lambda t, sl: m[sl, XT, t, :])
                    else:
                        wait_d(ND - 2)
                        kbe, vb = wide[hh][0], wide[hh][1]
                        for t in range(T):
                            for par, sl in enumerate((slice(0, 64), slice(64, 128))):
                                e.matmul(bank(hh, 1)[sl, t * P:(t + 1) * P], m[sl, XT, t, :], vb[sl, t, :],
                                         start=True, stop=True)
                                mm = e.matmul(bank(hh, 2 + par)[:, t * CHUNK:(t + 1) * CHUNK], kbe[sl, t, :], m[sl, XT, t, :],
                                              start=True, stop=True)
                    mm.then_inc(pe_s, 1)

                for pair in range(DNH // 2):
                    for n in range(NP):
                        for hh in range(2):
                            step(pair, n, hh)

            def act(e):
                for pair in range(DNH // 2):
                    for n in range(NA):
                        for hh in range(2):
                            h = 2 * pair + hh
                            m = mats[hh]
                            if n == 0:
                                e.wait_ge(dve_s, count(ND, pair, 1, hh))
                                e.activation(m[:, DEC], m[:, DEC], ACT.Exp, scale=-1.0).then_inc(act_s, 1)
                            elif n == 1:
                                e.wait_ge(pe_s, count(NP, pair, 1, hh))
                                e.activation(m[:, LT], part(hh, 2, 0), ACT.Copy)
                                e.activation(qkT[:, h, :, :], part(hh, 2, 1), ACT.Copy).then_inc(act_s, 1)
                            else:
                                e.wait_ge(pe_s, count(NP, pair, NP - 1, hh))
                                src = ps[:, 4 * hh + 2:4 * hh + 4, 0:B4].rearrange("p a (t c) -> p t a c", c=CHUNK)
                                e.activation(wT[:, h, :].rearrange("p (t a c) -> p t a c", t=T, a=2), src,
                                             ACT.Copy).then_inc(act_s, 1)

            def dve(e):
                link = chain(e, "dve_chain")
                t8 = "p (t h) -> p t h"

                def per_row(a, h, w):
                    return bc(a.rearrange(t8, h=DNH)[:, :, h:h + 1], T, w)

                def mask(m):
                    return bc(m.unsqueeze(1), T, CHUNK)

                def step(pair, n, hh):
                    h = 2 * pair + hh
                    m = mats[hh]
                    head = slice(h * DH, (h + 1) * DH)

                    def wait_p(p):
                        e.wait_ge(pe_s, count(NP, pair, p, hh))
                    if n == 0:
                        ins = e.tensor_tensor(m[:, L], mask(blk_tri[:]), per_row(G_, h, CHUNK), ALU.mult)
                    elif n == 1:
                        wait_p(0)
                        link(e.tensor_tensor(m[:, DEC], part(hh, 0, 0), per_row(GC, h, CHUNK), ALU.subtract))
                        ins = e.tensor_scalar(m[:, DEC], m[:, DEC], 0.0, None, ALU.max)
                    elif n == 2:
                        e.wait_ge(act_s, count(NA, pair, 0, hh))
                        link(e.tensor_tensor(m[:, DEC], m[:, DEC], mask(blk_incl[:]), ALU.mult))
                        e.tensor_tensor(m[:, QK], part(hh, 1, 0), m[:, DEC], ALU.mult)
                        link(e.tensor_tensor(m[:, L], part(hh, 0, 1), m[:, DEC], ALU.mult))
                        link(e.tensor_tensor(m[:, L], m[:, L], per_row(BETA, h, CHUNK), ALU.mult))
                        ins = e.tensor_tensor(m[:, L], m[:, L], mask(blk_strict[:]), ALU.mult)
                    elif n == 3:
                        e.wait_ge(act_s, count(NA, pair, 1, hh))
                        e.scalar_tensor_tensor(m[:, X], m[:, L], -1.0, mask(blk_low[:, 0, :]), ALU.mult, ALU.mult)
                        link(e.scalar_tensor_tensor(m[:, XT], m[:, LT], -1.0, mask(blk_low0[:]), ALU.mult, ALU.mult))
                        e.tensor_tensor(m[:, X], m[:, X], mask(blk_id[:]), ALU.add)
                        ins = e.tensor_tensor(m[:, XT], m[:, XT], mask(blk_id[:]), ALU.add)
                    elif n < ND - 2 and n % 2 == 0:
                        wait_p(n - 2)
                        ins = e.tensor_tensor(m[:, DEC], part(hh, 3, 0), mask(blk_low[:, (n - 2) // 2, :]), ALU.mult)
                    elif n < ND - 2:
                        wait_p(n - 2)
                        e.tensor_tensor(m[:, X], m[:, X], part(hh, 0, 0), ALU.subtract)
                        ins = e.tensor_tensor(m[:, XT], m[:, XT], part(hh, 0, 1), ALU.subtract)
                    elif n == ND - 2:
                        kbe, vb = wide[hh][0], wide[hh][1]
                        e.tensor_tensor(vb, v[:, :, head], per_row(BETA, h, DH), ALU.mult)
                        link(e.tensor_tensor(kbe, k_[:, :, head], per_row(BEGC, h, DH), ALU.mult))
                        ins = e.tensor_tensor(k_[:, :, head], k_[:, :, head], per_row(REST, h, DH), ALU.mult)
                    else:
                        wait_p(NP - 1)
                        ins = e.tensor_copy(v[:, :, head], bank(hh, 1).rearrange("p (t c) -> p t c", t=T))
                    ins.then_inc(dve_s, 1)
                    e.wait_ge(dve_s, count(ND, pair, n, hh))

                for pair in range(DNH // 2):
                    for n in range(ND):
                        for hh in range(2):
                            step(pair, n, hh)
            stage(pe=pe, act=act, dve=dve)
            return qkT, wT

        def dn_scan_stage(qT, kT, k_, v, z, ab, at, qkT, wT):
            o = kT.rearrange("p h s -> p (h s)").rearrange("p (t d) -> p t d", t=T)
            base = at - 2 * (S + 3) - 2 * S
            state, p1 = area(base, DNH, DH)
            fresh, p1 = area(p1, DNH, DH)
            old, p1 = area(p1, DNH, DH)
            NCH = S // CHUNK
            begun, stated, freshed, second, decayed, outs, zero = (
                sem("dc_" + n) for n in ("begun", "state", "fresh", "second", "decayed", "out", "zero"))

            def row_of(c):
                return c // 2, slice(64 * (c % 2), 64 * (c % 2) + 64)

            def egl(c):
                return (EGL, EGL2)[c % 2].rearrange("p (t h) -> p t h", h=DNH)[:, c // 2, :]

            def pool(e):
                e.memset(state, 0.0).then_inc(zero, 1)
                for c in range(NCH):
                    if c == 0:
                        e.wait_ge(zero, 1)
                    else:
                        e.wait_ge(stated, c)
                    e.tensor_tensor(old, state, bc(egl(c).unsqueeze(2), DNH, DH), ALU.mult).then_inc(decayed, 1)

            def pe(e):
                for c in range(NCH):
                    t, sl = row_of(c)
                    cs = slice(c * CHUNK, (c + 1) * CHUNK)
                    if c == 0:
                        e.wait_ge(zero, 1)
                    else:
                        e.wait_ge(stated, c)
                        e.wait_ge(outs, c)
                    for h in range(DNH):
                        mm = e.matmul(ps[sl, h // 4, (h % 4) * DH:(h % 4 + 1) * DH], wT[:, h, cs], state[:, h, :],
                                      start=True, stop=True)
                    mm.then_inc(begun, 1)
                    for h in range(DNH):
                        mm = e.matmul(ps[sl, 2 + h // 4, (h % 4) * DH:(h % 4 + 1) * DH], qT[:, h, cs], state[:, h, :],
                                      start=True, stop=True)
                    e.wait_ge(freshed, c + 1)
                    for h in range(DNH):
                        mm = e.matmul(ps[:, 6 + h // 4, (h % 4) * DH:(h % 4 + 1) * DH],
                                      k_[sl, t, h * DH:(h + 1) * DH], fresh[sl, h, :], start=True, stop=True)
                    mm.then_inc(second, 1)
                    for h in range(DNH):
                        mm = e.matmul(ps[sl, 4 + h // 4, (h % 4) * DH:(h % 4 + 1) * DH], qkT[sl, h, t, :],
                                      fresh[sl, h, :], start=True, stop=True)
                    mm.then_inc(second, 1)

            def dve(e):
                link = chain(e, "dve_chain")
                e.wait_ge(zero, 1)
                for c in range(NCH):
                    t, sl = row_of(c)

                    def wide(a):
                        return a.rearrange("p b (h d) -> p (b h) d", d=DH)
                    e.wait_ge(begun, c + 1)
                    e.tensor_tensor(fresh[sl, :, :], v[sl, t, :].rearrange("p (h d) -> p h d", d=DH),
                                    wide(ps[sl, 0:2, :]), ALU.subtract).then_inc(freshed, 1)
                    e.wait_ge(second, 2 * c + 1)
                    e.wait_ge(decayed, c + 1)
                    e.tensor_tensor(state, old, wide(ps[:, 6:8, :]), ALU.add).then_inc(stated, 1)
                    e.wait_ge(second, 2 * c + 2)
                    ov = o[sl, t, :].rearrange("p (h d) -> p h d", d=DH)
                    eg = EGC.rearrange("p (t h) -> p t h", h=DNH)[sl, t, :]
                    link(e.tensor_tensor(ov, wide(ps[sl, 2:4, :]), bc(eg.unsqueeze(2), DNH, DH), ALU.mult))
                    e.tensor_tensor(ov, ov, wide(ps[sl, 4:6, :]), ALU.add).then_inc(outs, 1)
            stage(pe=pe, dve=dve, pool=pool)
            return o

        def dn_out_stage(o, z, at):
            base = at - 2 * (S + 3) - 2 * S
            sq, _ = area(base, 2, D)
            ss, rs = small[:, 0:32], small[:, 32:64]
            squared, summed, inverse, rooted = (sem("do_" + n) for n in ("sq", "sum", "inv", "root"))

            def act(e):
                for t in range(T):
                    if t >= 2:
                        e.wait_ge(summed, t - 1)
                    e.activation(sq[:, t % 2, :], o[:, t, :], ACT.Square).then_inc(squared, 1)
                e.wait_ge(inverse, 1)
                e.activation(rs, rs, ACT.Sqrt).then_inc(rooted, 1)

            def dve(e):
                link = chain(e, "dve_chain")
                for t in range(T):
                    e.wait_ge(squared, t + 1)
                    e.tensor_reduce(ss[:, t * DNH:(t + 1) * DNH], sq[:, t % 2, :].rearrange("p (h d) -> p h d", d=DH),
                                    AX, ALU.add).then_inc(summed, 1)
                e.wait_ge(summed, T)
                link(e.tensor_scalar(rs, ss, 1.0 / DH, EPS, ALU.mult, ALU.add))
                e.reciprocal(rs, rs).then_inc(inverse, 1)
                for t in range(T):
                    z3 = z[:, t, :].rearrange("p (h d) -> p h d", d=DH)
                    last = e.tensor_tensor(z3, z3, bc(row("head_norm").unsqueeze(1), DNH, DH), ALU.mult)
                link(last)
                e.wait_ge(rooted, 1)
                for t in range(T):
                    o3 = o[:, t, :].rearrange("p (h d) -> p h d", d=DH)
                    last = e.tensor_tensor(o3, o3, bc(rs[:, t * DNH:(t + 1) * DNH].unsqueeze(2), DNH, DH), ALU.mult)
                link(last)
                for t in range(T):
                    e.tensor_tensor(o[:, t, :], o[:, t, :], z[:, t, :], ALU.mult)
            stage(act=act, dve=dve)

        def final_stage():
            y, at = area(0, T, D)
            frow, at = area(at, D)
            ss, rs = small[:, 0:T], small[:, T:2 * T]
            squared, inverse, rooted, ready = (sem("fi_" + n) for n in ("sq", "inv", "root", "ready"))

            def act(e):
                e.dma_start(frow, A["final_norm"].partition_broadcast(P)).then_inc(loaded, 16)
                for t in range(T):
                    e.activation(y[:, t, :], x[:, t, :], ACT.Square, accum_out=ss[:, t:t + 1]).then_inc(squared, 1)
                e.wait_ge(inverse, 1)
                e.activation(rs, rs, ACT.Sqrt).then_inc(rooted, 1)
                for t in range(T):
                    e.wait_ge(ready, t + 1)
                    e.dma_start(out[t * P:(t + 1) * P, :], y[:, t, :]).then_inc(stored, 16)
                e.wait_ge(stored, 16 * T)

            def dve(e):
                link = chain(e, "dve_chain")
                e.wait_ge(loaded, 128)
                e.wait_ge(squared, T)
                link(e.tensor_scalar(rs, ss, 1.0 / D, EPS, ALU.mult, ALU.add))
                e.reciprocal(rs, rs).then_inc(inverse, 1)
                e.wait_ge(rooted, 1)
                for t in range(T):
                    e.scalar_tensor_tensor(y[:, t, :], x[:, t, :], rs[:, t:t + 1], frow, ALU.mult,
                                           ALU.mult).then_inc(ready, 1)
            stage(act=act, dve=dve)

        ada_stage()
        norm_stage("n1", mod1, ada[:, 0:KC])
        a = in_stage()
        mix_stage(*a)
        residual_stage("wo1", gate1, A["b_out"])
        norm_stage("n2", mod2, ada[:, 3 * KC:4 * KC])
        egT = route_stage()
        gate_stage(egT)
        acc = expert_stage()
        close_stage(acc)
        norm_stage("n3", col("attn_norm"))
        ao = attention_stage()
        turn_stage(ao)
        residual_stage("wo2")
        norm_stage("n4", col("mlp_norm0"))
        mlp_stage()
        norm_stage("n5", col("dn_norm"))
        dn = dn_in_stage()
        dn_unit_stage(*dn)
        qk = dn_solve_stage(*dn)
        o = dn_scan_stage(*dn, *qk)
        dn_out_stage(o, dn[4], dn[6])
        turn_stage(o)
        residual_stage("wo3")
        norm_stage("n6", col("mlp_norm1"))
        mlp_stage()
        final_stage()
        assert taken[0] == NSLABS

        block = ctx.enter_context(nc.Block())

        def between(e, n):
            e.drain().then_inc(stage_done, 1)
            e.wait_ge(stage_done, 4 * (n + 1))

        @block.sync
        def _(e):
            for i in range(NSLABS):
                if i >= RING:
                    e.wait_ge(slab_used, i - RING + 1)
                e.dma_start(slab(i), A["stream"][i]).then_inc(slab_in[i % RING], 16)
        @block.tensor
        def _(e):
            for n, s in enumerate(stages):
                if "pe" in s:
                    s["pe"](e)
                between(e, n)

        @block.scalar
        def _(e):
            for n, s in enumerate(stages):
                if "act" in s:
                    s["act"](e)
                between(e, n)

        @block.vector
        def _(e):
            for n, s in enumerate(stages):
                if "dve" in s:
                    s["dve"](e)
                between(e, n)

        @block.gpsimd
        def _(e):
            for n, s in enumerate(stages):
                if "pool" in s:
                    s["pool"](e)
                between(e, n)


def layout(inp):
    def colv(a):
        return np.asarray(a).reshape(-1, P).T

    def slabs(w, width=N):
        w = np.asarray(w)
        n = w.shape[1] // width
        return w.reshape(KC, P, n, width).transpose(2, 1, 0, 3).reshape(n, P, KC * width)

    g = {k: np.asarray(v) for k, v in inp.items()}
    heads = [h for c in range(4) for h in (c, c + 4)]
    perm = np.concatenate([np.arange(h * HEAD, (h + 1) * HEAD) for h in heads] + [np.arange(AW, g["w_in"].shape[1])])
    w_in, b_in = g["w_in"][:, perm], g["b_in"][perm]
    kv = np.zeros((1, P, SLAB), np.float32)
    kv[:, :, :KC * 256] = slabs(w_in[:, AW:AW + 256], 256)
    keys = np.zeros((1, P, SLAB), np.float32)
    keys[0, :, :16 * KEYS] = np.stack([g["peer_keys1"], g["peer_keys2"]], 1).transpose(3, 0, 1, 2).reshape(P, 16 * KEYS)
    u = g["peer_u"].reshape(KEYS, ECH, E2C, KC, P).transpose(1, 4, 3, 2, 0).reshape(ECH, P, SLAB)
    v = g["peer_v"].reshape(KEYS, ECH, SLAB).transpose(1, 0, 2)
    experts = np.empty((2 * ECH, P, SLAB), np.float32)
    experts[0], experts[-1] = u[0], v[-1]
    experts[1:-1:2], experts[2:-1:2] = u[1:], v[:-1]

    def down(w):
        return [slabs(w[kb * D:(kb + 1) * D, n * N:(n + 1) * N]) for n in range(2) for kb in range(4)]

    dn = g["dn_w_in_2"][0]
    parts = [slabs(g["w_ada"]), slabs(w_in[:, :AW]), kv, slabs(w_in[:, AW + 256:]), slabs(g["w_out"]),
             slabs(g["w_query"]), keys, experts, slabs(g["attn_w_qkv_2"][0]), slabs(g["attn_w_o_2"][0]),
             slabs(g["mlp_w_up_2"][0]), *down(g["mlp_w_down_2"][0]), slabs(dn[:, :4 * D]), slabs(g["dn_w_o_2"][0]),
             slabs(g["mlp_w_up_2"][1]), *down(g["mlp_w_down_2"][1])]
    ab = dn[:, 4 * D:].reshape(KC, P, 2 * DNH).transpose(1, 0, 2).reshape(P, -1)
    cv = {"c": colv(g["c"]), "b_ada": colv(g["b_ada"]), "norm1_g": colv(g["norm1_g"]), "b_in": colv(b_in),
          "conv_w": colv(g["conv_w"]), "conv_out_g": colv(g["conv_out_g"]), "norm2_g": colv(g["norm2_g"]),
          "attn_norm": colv(g["attn_norm_2"]), "mlp_norm0": colv(g["mlp_norm_2"][0]),
          "mlp_norm1": colv(g["mlp_norm_2"][1]), "dn_norm": colv(g["dn_norm_2"]),
          "dn_conv_w": colv(g["dn_conv_w_2"]), "dn_ab": ab}
    rv = {"b_v": g["b_in"][AW + P:AW + 2 * P], "attn_out_g": g["attn_out_g"], "sinks": g["attn_sinks"],
          "head_norm": g["dn_head_norm_2"][0], "dt_bias": g["dn_dt_bias_2"][0], "a_log": g["dn_a_log_2"][0]}
    rb = g["attn_rel_bias_2"][0]
    rel = np.concatenate([rb[:, MAX_REL - P + 1:], np.repeat(rb[:, -1:], S - 1 - MAX_REL, 1)], 1)
    return {
        "stream": np.concatenate(parts), "cols": np.concatenate([cv[n] for n in COLS], 1),
        "rows": np.concatenate([rv[n] for n in ROWS]), "b_gate1": g["b_ada"][2 * D:3 * D],
        "b_gate2": g["b_ada"][5 * D:], "b_out": g["b_out"], "final_g": g["final_g"],
        "final_norm": g["final_norm_2"], "rel": rel, "x": g["x"].reshape(T, P, D).transpose(1, 0, 2),
    }


def kernel(**inputs):
    import concourse.bacc as bacc
    from concourse.bass_utils import run_bass_kernel_spmd

    nc = bacc.Bacc("TRN2", target_bir_lowering=False, num_devices=1)
    arrays = {name: np.ascontiguousarray(a) for name, a in layout(inputs).items()}
    handles = {name: nc.dram_tensor(name, a.shape, mybir.dt.from_np(a.dtype), kind="ExternalInput").ap()
               for name, a in arrays.items()}
    out = nc.dram_tensor("out", (S, D), F32, kind="ExternalOutput").ap()
    program(nc, handles, out)
    result = run_bass_kernel_spmd(nc, [arrays], core_ids=[0])
    return result.results[0]["out"].reshape(1, S, D)
```

```python
from contextlib import ExitStack

import numpy as np
import concourse.bass as bass
from concourse import mybir

F32 = mybir.dt.float32
F32R = mybir.dt.float32r
U32 = mybir.dt.uint32
ALU = mybir.AluOpType
ACT = mybir.ActivationFunctionType
AX = mybir.AxisListType.X

P = 128
D = 1024
S = 512
T = S // P
KC = D // P
N = 512
EPS = 1e-6
NEG = -1e30
LOWEST = -3.4e38

HEAD = 64
HEADS1 = 8
AW = HEADS1 * HEAD
CW = D - AW
TAPS1 = 3
KEYS = 128
EXPERTS = KEYS * KEYS
PH = 8
TOPK = 16
HEADS2 = 16
MAX_REL = 256
CHUNK = 64
DH = 128
DNH = D // DH
TAPS2 = 4
FF = 4 * D
FC = FF // P

SLAB = KC * N
HALF = SLAB // 2
RING = 4
E2C = SLAB // D
ECH = KEYS // E2C
GT = 64
NG = S // GT

COLS = {}
_at = 0
for _name, _n in (("c", KC), ("b_ada", 6 * KC), ("norm1_g", KC), ("b_in", 18), ("conv_w", TAPS1 * 4),
                  ("conv_out_g", 4), ("norm2_g", KC), ("attn_norm", KC), ("mlp_norm0", KC), ("mlp_norm1", KC),
                  ("dn_norm", KC), ("dn_conv_w", TAPS2 * 24), ("dn_ab", KC * 2 * DNH)):
    COLS[_name] = (_at, _n)
    _at += _n
NCOL = _at
ROWS = {}
_at = 0
for _name, _n in (("b_v", P), ("attn_out_g", AW), ("sinks", HEADS1), ("head_norm", DH), ("dt_bias", DNH),
                  ("a_log", DNH)):
    ROWS[_name] = (_at, _n)
    _at += _n
NROW = _at
BIGROWS = ("b_gate1", "b_gate2", "b_out", "final_g", "final_norm")

ARENA = 23568
ADA_SLABS = 12
MLP_CH = FF // N
PASSES = ((0, 0), (0, 1), (1, 0))


def program(nc, A, out):
    ctx = ExitStack()
    with ctx:
        def sb(name, shape, dt=F32):
            return ctx.enter_context(nc.sbuf_tensor(name, shape, dt))

        def sem(name):
            return ctx.enter_context(nc.semaphore(name))

        ps = ctx.enter_context(nc.psum_tensor("ps", [P, 8, N], F32))
        x = sb("x_res", [P, T, D])
        hT = sb("hT", [P, KC, S])
        hT_parts = nc.alloc_sbuf_tensor_at("hT_parts", [P, KC, S], F32R, offset=nc.sbuf_base - 4 * KC * S)
        ring = sb("ring", [P, RING, SLAB])
        parts_at = nc.sbuf_base - 4 * RING * SLAB // 2
        w_parts = nc.alloc_sbuf_tensor_at("w_parts", [P, 2, 2, HALF], F32R, offset=parts_at)
        cols = sb("cols_sb", [P, NCOL])
        rows = sb("rows_sb", [P, NROW])
        gates = sb("gates", [P, 2, D])
        gate1, gate2 = gates[:, 0, :], gates[:, 1, :]
        ada = sb("ada", [P, 6 * KC])
        mod1 = sb("mod1", [P, KC])
        mod2 = sb("mod2", [P, KC])
        ident = sb("ident", [P, P])
        ones = sb("ones", [P, P])
        group64 = sb("group64", [P, P])
        iota = sb("iota", [P, P])
        LEVELS = 6
        blk_id, blk_tri, blk_strict, blk_incl, blk_low0 = (
            sb("blk_" + n, [P, CHUNK]) for n in ("id", "tri", "strict", "incl", "low0"))
        blk_low = sb("blk_low", [P, LEVELS, CHUNK])
        small = sb("small", [P, 512])
        arena = sb("arena", [P, ARENA])
        arena_parts = nc.alloc_sbuf_tensor_at("arena_parts", [P, ARENA], F32R, offset=nc.sbuf_base - 4 * ARENA)

        def col(name, i=0, n=None):
            at, m = COLS[name]
            return cols[:, at + i:at + i + (n if n is not None else m - i)]

        def row(name):
            at, m = ROWS[name]
            return rows[:, at:at + m]

        def area(at, *shape):
            n = int(np.prod(shape))
            v = arena[:, at:at + n]
            if len(shape) == 2:
                v = v.rearrange("p (a b) -> p a b", b=shape[1])
            if len(shape) == 3:
                v = v.rearrange("p (a b c) -> p a b c", b=shape[1], c=shape[2])
            return v, at + n

        def bc(ap, *shape):
            return ap.broadcast_to([ap.shape[0], *shape])

        slab_in = [sem(f"slab_in{i}") for i in range(RING)]
        slab_used = sem("slab_used")
        stage_done = sem("stage_done")
        loaded = sem("loaded")
        consts = sem("consts")
        stored = sem("stored")

        gates_dram = nc.dram_tensor("gates_dram", [ECH, P, NG, E2C * GT], F32, kind="Internal").ap()
        by_name, calls = {}, {}

        def shared(name):
            if name not in by_name:
                by_name[name] = sem(name)
            return by_name[name]

        def call(kind):
            calls[kind] = calls.get(kind, -1) + 1
            return calls[kind]

        feed_chunks = [0]
        stages = []
        taken = [0]

        def stage(**parts):
            stages.append(parts)

        loads = []

        def slabs(n):
            at = taken[0]
            taken[0] += n
            loads.append((at, n, None))
            return at

        def halves(n, done):
            at = taken[0]
            taken[0] += n
            loads.append((at, n, done))
            return at

        def half(i):
            return ring[:, (i % RING) // 2, (i % 2) * HALF:(i % 2 + 1) * HALF]

        def slab(i):
            return ring[:, i % RING, :]

        def slab_k(i, width=N):
            return ring[:, i % RING, 0:KC * width].rearrange("p (k n) -> p k n", n=width)

        def await_slab(eng, i):
            eng.wait_ge(slab_in[i % RING], 16 * (i // RING + 1))

        class Chain:
            def __init__(self, eng, name):
                self.eng, self.sem, self.n = eng, sem(name), 0

            def __call__(self, ins):
                self.n += 1
                ins.then_inc(self.sem, 1)
                self.eng.wait_ge(self.sem, self.n)

        chains = {}

        def chain(eng, name):
            if name not in chains:
                chains[name] = Chain(eng, name)
            return chains[name]

        def ada_stage():
            s0 = slabs(ADA_SLABS)
            sc, at = area(0, KC)
            scb, at = area(at, KC, P)
            bits, at = area(at, 6, CHUNK)
            bitf, at = area(at, 6, CHUNK)
            I32 = mybir.dt.int32
            act_silu = sem("act_silu")
            wide = sem("silu_wide")
            cols_done = sem("ada_cols_done")
            gates_done = sem("ada_gates_done")

            def act(e):
                e.dma_start(cols[:], A["cols"]).then_inc(loaded, 16)
                e.dma_start(rows[:], A["rows"].partition_broadcast(P)).then_inc(loaded, 16)
                e.dma_start(gate1, A["b_gate1"].partition_broadcast(P)).then_inc(loaded, 16)
                e.dma_start(gate2, A["b_gate2"].partition_broadcast(P)).then_inc(loaded, 16)
                e.dma_start(x[:], A["x"]).then_inc(loaded, 16)
                e.wait_ge(loaded, 80)
                e.activation(sc, col("c"), ACT.Silu).then_inc(act_silu, 1)

            def pool(e):
                e.memset(ident[:], 0.0).then_inc(consts, 1)
                e.memset(ones[:], 1.0).then_inc(consts, 1)
                e.memset(group64[:], 0.0).then_inc(consts, 1)
                e.iota(iota[:], [[1, P]], base=0, channel_multiplier=0,
                       allow_small_or_imprecise_dtypes=True).then_inc(consts, 1)
                e.wait_ge(consts, 4)
                e.affine_select(out=ident[:], in_=ident[:], compare_op=ALU.not_equal, fill=1.0, base=0,
                                pattern=[[-1, P]], channel_multiplier=1).then_inc(consts, 1)
                e.wait_ge(consts, 5)
                e.memset(group64[0:64, 0:64], 1.0).then_inc(consts, 1)
                e.wait_ge(consts, 6)
                e.memset(group64[64:128, 64:128], 1.0).then_inc(consts, 1)
                e.wait_ge(consts, 7)
                for r0 in (0, 64):
                    e.iota(bits[r0:r0 + 64, 0, :].bitcast(I32), [[0, CHUNK]], base=0, channel_multiplier=1
                           ).then_inc(consts, 1)
                e.wait_ge(consts, 9)
                e.iota(bits[:, 1, :].bitcast(I32), [[1, CHUNK]], base=0, channel_multiplier=0).then_inc(consts, 1)
                e.wait_ge(consts, 10)

            def pe(e):
                e.wait_ge(act_silu, 1)
                e.wait_ge(wide, 1)
                for i in range(ADA_SLABS):
                    part = i // 2
                    await_slab(e, s0 + i)
                    w = slab_k(s0 + i)
                    if part in (2, 5):
                        bank = 1 + (part == 5) * 2 + i % 2
                        for k in range(KC):
                            mm = e.matmul(ps[:, bank, :], scb[:, k, :], w[:, k, :], start=k == 0, stop=k == KC - 1)
                    else:
                        for j in range(N // P):
                            for k in range(KC):
                                c = i * (N // P) + j
                                mm = e.matmul(ps[:, 0, c:c + 1], w[:, k, j * P:(j + 1) * P], sc[:, k:k + 1],
                                              start=k == 0, stop=k == KC - 1)
                    mm.then_inc(slab_used, 1)

            def dve(e):
                link = chain(e, "dve_chain")
                e.wait_ge(consts, 2)
                e.wait_ge(act_silu, 1)
                for k in range(KC):
                    last = e.tensor_scalar(scb[:, k, :], ones[:], sc[:, k:k + 1], None, ALU.mult)
                last.then_inc(wide, 1)
                e.wait_ge(consts, 10)
                link(e.tensor_copy(bitf[:, 0:2, :], bits[:, 0:2, :].bitcast(I32)))
                rf, cf = bitf[:, 0, :], bitf[:, 1, :]
                for m, op in ((blk_id, ALU.is_equal), (blk_tri, ALU.is_le), (blk_strict, ALU.is_gt),
                              (blk_incl, ALU.is_ge)):
                    e.tensor_tensor(m[:], rf, cf, op)
                for s in range(LEVELS):
                    link(e.tensor_scalar(bits[:, 2:4, :].bitcast(I32), bits[:, 0:2, :].bitcast(I32), s, None,
                                         ALU.arith_shift_right))
                    link(e.tensor_tensor(bits[:, 4, :].bitcast(I32), bits[:, 2, :].bitcast(I32),
                                         bits[:, 3, :].bitcast(I32), ALU.bitwise_xor))
                    link(e.tensor_scalar(bits[:, 2:4, :].bitcast(I32), bits[:, 2:4, :].bitcast(I32), 1, None,
                                         ALU.bitwise_and))
                    link(e.tensor_copy(bitf[:, 2:5, :], bits[:, 2:5, :].bitcast(I32)))
                    link(e.scalar_tensor_tensor(blk_low[:, s, :], bitf[:, 4, :], 1.0, bitf[:, 2, :], ALU.is_equal,
                                                ALU.mult))
                    if s == 0:
                        link(e.scalar_tensor_tensor(blk_low0[:], bitf[:, 4, :], 1.0, bitf[:, 3, :], ALU.is_equal,
                                                    ALU.mult))
                e.wait_ge(slab_used, s0 + ADA_SLABS)
                e.wait_ge(loaded, 80)
                link(e.memset(ada[:], 0.0))
                for a, b in ((0, 2), (3, 5)):
                    link(e.tensor_tensor(ada[:, a * KC:b * KC], ps[:, 0, a * KC:b * KC],
                                         col("b_ada", a * KC, (b - a) * KC), ALU.add))
                for mod, g, a in ((mod1, "norm1_g", 1), (mod2, "norm2_g", 4)):
                    link(e.scalar_tensor_tensor(mod[:], ada[:, a * KC:(a + 1) * KC], 1.0, col(g), ALU.add, ALU.mult))
                for g, bank in ((gate1, 1), (gate2, 3)):
                    for n in range(2):
                        link(e.tensor_tensor(g[:, n * N:(n + 1) * N], ps[:, bank + n, :], g[:, n * N:(n + 1) * N],
                                             ALU.add))
            stage(pe=pe, act=act, dve=dve, pool=pool)

        def rms_scale(e_dve, link, e_act_sem, dst, ss, width):
            link(e_dve.tensor_scalar(dst, ss, 1.0 / width, EPS, ALU.mult, ALU.add))

        def norm_stage(tag, g, b=None, at=0):
            xn, _ = area(at, T, D)
            ss, rs = small[:, 0:T], small[:, T:2 * T]
            r = call("norm")
            squared, inverse, rooted, normed, turned = (
                shared("norm_" + n) for n in ("squared", "inverse", "rooted", "normed", "turned"))

            def act(e):
                for t in range(T):
                    e.activation(xn[:, t, :], x[:, t, :], ACT.Square, accum_out=ss[:, t:t + 1]).then_inc(squared, 1)
                e.wait_ge(inverse, r + 1)
                e.activation(rs, rs, ACT.Sqrt).then_inc(rooted, 1)
                for c in range(0, KC, 2):
                    e.wait_ge(turned, r * KC + c + 1)
                    e.activation(hT[:, c, :], ps[:, c, :], ACT.Identity, scale=g[:, c:c + 1],
                                 bias=b[:, c:c + 1] if b is not None else 0.0)

            def dve(e):
                link = chain(e, "dve_chain")
                e.wait_ge(squared, (r + 1) * T)
                link(e.tensor_scalar(rs, ss, 1.0 / D, EPS, ALU.mult, ALU.add))
                e.reciprocal(rs, rs).then_inc(inverse, 1)
                e.wait_ge(rooted, r + 1)
                for t in range(T):
                    e.tensor_scalar(xn[:, t, :], x[:, t, :], rs[:, t:t + 1], None, ALU.mult).then_inc(normed, 1)
                for c in range(1, KC, 2):
                    e.wait_ge(turned, r * KC + c + 1)
                    if b is None:
                        e.tensor_scalar(hT[:, c, :], ps[:, c, :], g[:, c:c + 1], None, ALU.mult)
                    else:
                        e.tensor_scalar(hT[:, c, :], ps[:, c, :], g[:, c:c + 1], b[:, c:c + 1], ALU.mult, ALU.add)

            def pe(e):
                for c in range(KC):
                    for t in range(T):
                        if c == 0:
                            e.wait_ge(normed, r * T + t + 1)
                        mm = e.transpose(ps[:, c, t * P:(t + 1) * P], xn[:, t, c * P:(c + 1) * P], ident[:])
                    mm.then_inc(turned, 1)
            stage(pe=pe, act=act, dve=dve)

        def slab_channels(e, i, outs, width=N, src=None, first=0, done=None, wait=None):
            src = hT if src is None else src
            w = slab_k(i, width)
            await_slab(e, i)
            for j in outs:
                if wait:
                    wait(j)
                for k in range(KC):
                    mm = e.matmul(ps[:, (first + j) % 8, :], w[:, k, j * P:(j + 1) * P], src[:, k, :],
                                  start=k == 0, stop=k == KC - 1)
                mm.then_inc(done, 1)
            return mm

        def in_stage():
            s0 = slabs(5)
            qT, at = area(0, 4, S)
            kT, at = area(at, S)
            v, at = area(at, T, P)
            bcu, at = area(at, 12, S)
            done, freed = sem("in_done"), sem("in_freed")

            def pe(e):
                def wait(g):
                    if g >= 8:
                        e.wait_ge(freed, g - 7)
                for i in range(5):
                    await_slab(e, s0 + i)
                    w = slab_k(s0 + i, 256 if i == 1 else N)
                    for j in range(2 if i == 1 else 4):
                        g = (0, 4, 6, 10, 14)[i] + j
                        wait(g)
                        if i == 1 and j == 1:
                            for t in range(T):
                                for k in range(KC):
                                    mm = e.matmul(ps[:, g % 8, t * P:(t + 1) * P], hT[:, k, t * P:(t + 1) * P],
                                                  w[:, k, P:2 * P], start=k == 0, stop=k == KC - 1)
                        else:
                            for k in range(KC):
                                mm = e.matmul(ps[:, g % 8, :], w[:, k, j * P:(j + 1) * P], hT[:, k, :],
                                              start=k == 0, stop=k == KC - 1)
                        mm.then_inc(done, 1)
                    e.wait_ge(done, g + 1)
                    e.sem_inc(slab_used, 1)

            def dve(e):
                for g in range(18):
                    e.wait_ge(done, g + 1)
                    if g == 5:
                        ins = e.tensor_tensor(v, ps[:, g % 8, :].rearrange("p (t c) -> p t c", c=P),
                                              bc(row("b_v").unsqueeze(1), T, P), ALU.add)
                    else:
                        dst = qT[:, g, :] if g < 4 else kT if g == 4 else bcu[:, g - 6, :]
                        ins = e.tensor_scalar(dst, ps[:, g % 8, :], col("b_in", g, 1), None, ALU.add)
                    ins.then_inc(freed, 1)
            stage(pe=pe, dve=dve)
            return qT, kT, v, bcu, at

        def mix_stage(qT, kT, v, bcu, at):
            z, at = area(at, 4, S + TAPS1 - 1)
            y, at = area(at, 4, S)
            sc, at = area(at, HEADS1, 2 * P)
            mask, at = area(at, 2 * P)
            pt, at = area(at, 4, 4, P)
            ao, at = area(at, AW)
            sq, at = area(at, AW)
            tmp = bcu
            mx, es, den, rd = (small[:, 16 + 8 * i:24 + 8 * i] for i in range(4))
            hs, hr = small[:, 48:56], small[:, 56:64]
            masked, squares, sums, inverse, rooted = (sem("mix_" + n) for n in ("mask", "sq", "sum", "inv", "root"))
            scored, read, prob, expd = (sem("mix_" + n) for n in ("scored", "read", "prob", "exp"))
            turned, copied, valued, hinv, hroot, normed, oT, oC = (
                sem("mix_" + n) for n in ("turned", "copied", "valued", "hinv", "hroot", "normed", "oT", "oC"))

            def pool(e):
                e.memset(mask, 0.0).then_inc(masked, 1)
                e.wait_ge(masked, 1)
                e.affine_select(out=mask[:, 0:P], in_=mask[:, 0:P], compare_op=ALU.is_gt, fill=NEG, base=0,
                                pattern=[[1, P]], channel_multiplier=-1).then_inc(masked, 1)
                e.affine_select(out=mask[:, P:], in_=mask[:, P:], compare_op=ALU.is_ge, fill=NEG, base=0,
                                pattern=[[-1, P]], channel_multiplier=1).then_inc(masked, 1)

            def lo(t):
                return P if t == 0 else 0

            def pe(e):
                e.wait_ge(squares, 1)
                for c in range(4):
                    mm = e.matmul(ps[:, c, :], group64[:], tmp[:, c, :], start=True, stop=True)
                mm.then_inc(sums, 1)
                e.wait_ge(inverse, 1)

                def turn_out(t):
                    e.wait_ge(normed, t + 1)
                    if t:
                        e.wait_ge(oC, t)
                    for c in range(4):
                        mm = e.transpose(ps[:, 7, c * P:(c + 1) * P], ao[:, c * P:(c + 1) * P], ident[:])
                    mm.then_inc(oT, 1)

                for t in range(T):
                    if t:
                        e.wait_ge(read, t)
                    for h in range(HEADS1):
                        b = 64 * (h // 4)
                        mm = e.matmul(ps[:, h // 2, (h % 2) * 2 * P + lo(t):(h % 2 + 1) * 2 * P],
                                      qT[b:b + 64, h % 4, t * P:(t + 1) * P],
                                      kT[b:b + 64, (t - 1) * P + lo(t):(t + 1) * P], start=True, stop=True)
                    mm.then_inc(scored, 1)
                    if t:
                        turn_out(t - 1)
                    e.wait_ge(prob, t + 1)
                    for pair in range(4):
                        n = 4 * t + pair
                        if n >= 2:
                            e.wait_ge(copied, n - 1)
                        blocks = [(h, half) for h in (2 * pair, 2 * pair + 1) for half in (0, 1) if t or half]
                        for h, half in blocks:
                            mm = e.transpose(ps[:, 4 + n % 2, (2 * (h % 2) + half) * P:(2 * (h % 2) + half + 1) * P],
                                             sc[:, h, half * P:(half + 1) * P], ident[:])
                        mm.then_inc(turned, 1)
                        if pair:
                            values(e, t, pair - 1)
                    values(e, t, 3)
                turn_out(T - 1)

            def values(e, t, pair):
                n = 4 * t + pair
                e.wait_ge(copied, n + 1)
                if pair == 0 and t:
                    e.wait_ge(hinv, t)
                for h in (2 * pair, 2 * pair + 1):
                    kv = h // 4
                    for half in range(t == 0, 2):
                        mm = e.matmul(ps[:, 6, h * HEAD:(h + 1) * HEAD], pt[:, n % 4, 2 * (h % 2) + half, :],
                                      v[:, t - 1 + half, kv * HEAD:(kv + 1) * HEAD],
                                      start=half == (t == 0), stop=half == 1)
                mm.then_inc(valued, 1)

            def dve(e):
                link = chain(e, "dve_chain")
                link(e.memset(z[:, :, 0:TAPS1 - 1], 0.0))
                link(e.tensor_tensor(z[:, :, TAPS1 - 1:], bcu[:, 4:8, :], bcu[:, 8:12, :], ALU.mult))
                for c in range(4):
                    e.tensor_scalar(y[:, c, :], z[:, c, 0:S], col("conv_w", c, 1), None, ALU.mult)
                for tap in (1, 2):
                    link(e.engine_nop())
                    for c in range(4):
                        last = e.scalar_tensor_tensor(y[:, c, :], z[:, c, tap:tap + S], col("conv_w", 4 * tap + c, 1),
                                                      y[:, c, :], ALU.mult, ALU.add)
                link(last)
                link(e.tensor_tensor(y, y, bcu[:, 0:4, :], ALU.mult))
                e.tensor_tensor(tmp[:, 0:4, :], y, y, ALU.mult).then_inc(squares, 1)
                e.wait_ge(sums, 1)
                link(e.tensor_scalar(z[:, :, 0:S], ps[:, 0:4, :], 1.0 / HEAD, EPS, ALU.mult, ALU.add))
                e.reciprocal(z[:, :, 0:S], z[:, :, 0:S]).then_inc(inverse, 1)
                e.wait_ge(masked, 3)

                def finish(t):
                    e.wait_ge(valued, 4 * t + 4)
                    a3 = ao.rearrange("p (h d) -> p h d", d=HEAD)
                    s3 = sq.rearrange("p (h d) -> p h d", d=HEAD)
                    if t:
                        e.wait_ge(oT, t)
                    link(e.tensor_tensor(a3, ps[:, 6, :].rearrange("p (h d) -> p h d", d=HEAD),
                                         bc(rd.unsqueeze(2), HEADS1, HEAD), ALU.mult))
                    link(e.tensor_tensor(sq, ao, ao, ALU.mult))
                    link(e.tensor_reduce(hs, s3, AX, ALU.add))
                    link(e.tensor_scalar(hr, hs, 1.0 / HEAD, EPS, ALU.mult, ALU.add))
                    e.reciprocal(hr, hr).then_inc(hinv, 1)
                    e.wait_ge(hroot, t + 1)
                    link(e.tensor_tensor(a3, a3, bc(hr.unsqueeze(2), HEADS1, HEAD), ALU.mult))
                    e.tensor_tensor(ao, ao, row("attn_out_g"), ALU.mult).then_inc(normed, 1)

                for t in range(T):
                    e.wait_ge(scored, t + 1)
                    if t:
                        e.wait_ge(turned, 4 * t)
                    w = 2 * P - lo(t)
                    s3 = sc[:, :, lo(t):]
                    e.scalar_tensor_tensor(
                        s3, ps[:, 0:4, :].rearrange("p b (h k) -> p (b h) k", k=2 * P)[:, :, lo(t):], HEAD ** -0.5,
                        bc(mask[:, lo(t):].unsqueeze(1), HEADS1, w), ALU.mult, ALU.add).then_inc(read, 1)
                    e.wait_ge(read, t + 1)
                    link(e.tensor_reduce(mx, s3, AX, ALU.max))
                    link(e.tensor_tensor(mx, mx, row("sinks"), ALU.max))
                    link(e.tensor_tensor(es, row("sinks"), mx, ALU.subtract))
                    e.tensor_scalar(mx, mx, -1.0, None, ALU.mult).then_inc(expd, 1)
                    e.wait_ge(prob, t + 1)
                    link(e.tensor_tensor(den, den, es, ALU.add))
                    link(e.reciprocal(rd, den))
                    finish(t)
                e.wait_ge(rooted, 1)
                link(e.tensor_tensor(y, y, z[:, :, 0:S], ALU.mult))
                for c in range(4):
                    e.tensor_scalar(hT[:, 4 + c, :], y[:, c, :], col("conv_out_g", c, 1), None, ALU.mult)

            def act(e):
                e.wait_ge(inverse, 1)
                e.activation(z[:, :, 0:S], z[:, :, 0:S], ACT.Sqrt).then_inc(rooted, 1)

                def out_copy(t):
                    e.wait_ge(oT, t + 1)
                    e.activation(hT[:, 0:4, t * P:(t + 1) * P], ps[:, 7, :].rearrange("p (c q) -> p c q", q=P),
                                 ACT.Copy).then_inc(oC, 1)

                for t in range(T):
                    e.wait_ge(expd, t + 1)
                    e.activation(es, es, ACT.Exp)
                    for h in range(HEADS1):
                        last = e.activation(sc[:, h, lo(t):], sc[:, h, lo(t):], ACT.Exp, bias=mx[:, h:h + 1],
                                            accum_out=den[:, h:h + 1])
                    last.then_inc(prob, 1)
                    if t:
                        out_copy(t - 1)
                    for pair in range(4):
                        n = 4 * t + pair
                        e.wait_ge(turned, n + 1)
                        if n >= 4:
                            e.wait_ge(valued, n - 3)
                        src = ps[:, 4 + n % 2, :].rearrange("p (b q) -> p b q", q=P)
                        if t:
                            e.activation(pt[:, n % 4, :, :], src, ACT.Copy).then_inc(copied, 1)
                        else:
                            e.activation(pt[:, n % 4, 1::2, :], src[:, 1::2, :], ACT.Copy).then_inc(copied, 1)
                    e.wait_ge(hinv, t + 1)
                    e.activation(hr, hr, ACT.Sqrt).then_inc(hroot, 1)
                out_copy(T - 1)
            stage(pe=pe, act=act, dve=dve, pool=pool)

        def residual_stage(tag, gate=None, bias=None, src=None):
            s0 = slabs(2)
            src = hT if src is None else src
            brow, at = area(0, D)
            tmp, at = area(at, 2, N)
            r = call("residual")
            done = shared("residual_done")

            def act(e):
                if bias is not None:
                    e.dma_start(brow, bias.partition_broadcast(P)).then_inc(loaded, 16)

            def pe(e):
                for n in range(2):
                    await_slab(e, s0 + n)
                    w = slab_k(s0 + n)
                    for t in range(T):
                        for k in range(KC):
                            mm = e.matmul(ps[:, 4 * n + t, :], src[:, k, t * P:(t + 1) * P], w[:, k, :],
                                          start=k == 0, stop=k == KC - 1)
                        mm.then_inc(done, 1)
                    e.wait_ge(done, 8 * r + 4 * n + 4)
                    e.sem_inc(slab_used, 1)

            def dve(e):
                link = chain(e, "dve_chain")
                if bias is not None:
                    e.wait_ge(loaded, 96)
                for n in range(2):
                    cs = slice(n * N, (n + 1) * N)
                    for t in range(T):
                        e.wait_ge(done, 8 * r + 4 * n + t + 1)
                        src_ = ps[:, 4 * n + t, :]
                        if bias is not None:
                            link(e.tensor_tensor(tmp[:, 0, :], src_, brow[:, cs], ALU.add))
                            src_ = tmp[:, 0, :]
                        if gate is not None:
                            link(e.tensor_tensor(tmp[:, 1, :], src_, gate[:, cs], ALU.mult))
                            src_ = tmp[:, 1, :]
                        link(e.tensor_tensor(x[:, t, cs], x[:, t, cs], src_, ALU.add))
            stage(pe=pe, act=act, dve=dve)

        def route_stage():
            s0 = slabs(5)
            qT, at = area(0, 16, S)
            s1, at = area(at, 16, KEYS)
            s2, at = area(at, 16, KEYS)
            cand, at = area(at, PH, TOPK * TOPK)
            cand2 = s2.rearrange("p a b -> p (a b)").rearrange("p (h c) -> p h c", c=TOPK * TOPK)
            vals, at = area(at, 16, TOPK)
            idx, at = area(at, 16, TOPK)
            fidx, at = area(at, 16, TOPK)
            top, at = area(at, PH, TOPK)
            ci, at = area(at, PH, TOPK)
            cab, at = area(at, 2, PH * TOPK)
            fab, at = area(at, 2, PH * TOPK)
            eg, at = area(at, 3, PH * TOPK)
            gsum, at = area(at, PH)
            assert at <= 2 * KEYS * GT
            egT, at = area(2 * KEYS * GT, 3, S)
            done, freed = sem("rt_done"), sem("rt_freed")
            scored, read, expd, gated, ready, turned = (
                sem("rt_" + n) for n in ("scored", "read", "exp", "gated", "ready", "turned"))

            def pe(e):
                for i in range(4):
                    await_slab(e, s0 + i)
                    w = slab_k(s0 + i)
                    for j in range(4):
                        g = 4 * i + j
                        if g >= 8:
                            e.wait_ge(freed, g - 7)
                        for k in range(KC):
                            mm = e.matmul(ps[:, g % 8, :], w[:, k, j * P:(j + 1) * P], hT[:, k, :],
                                          start=k == 0, stop=k == KC - 1)
                        mm.then_inc(done, 1)
                    e.wait_ge(done, 4 * i + 4)
                    e.sem_inc(slab_used, 1)
                await_slab(e, s0 + 4)
                keys = slab(s0 + 4)
                e.wait_ge(freed, 16)

                def turn(t):
                    e.wait_ge(ready, t + 1)
                    for i in range(3):
                        mm = e.transpose(ps[:, 7, i * P:(i + 1) * P], eg[:, i, :], ident[:])
                    mm.then_inc(turned, 1)

                for t in range(T):
                    if t:
                        e.wait_ge(read, t)
                    for c in range(16):
                        mm = e.matmul(ps[:, c // 4, (c % 4) * P:(c % 4 + 1) * P], qT[:, c, t * P:(t + 1) * P],
                                      keys[:, c * KEYS:(c + 1) * KEYS], start=True, stop=True)
                    mm.then_inc(scored, 1)
                    if t:
                        turn(t - 1)
                e.wait_ge(scored, T)
                e.sem_inc(slab_used, 1)
                turn(T - 1)

            def act(e):
                for g in range(16):
                    e.wait_ge(done, g + 1)
                    e.activation(qT[:, g, :], ps[:, g % 8, :], ACT.Copy).then_inc(freed, 1)
                for t in range(T):
                    e.wait_ge(expd, t + 1)
                    e.activation(top, top, ACT.Exp).then_inc(gated, 1)

            def dve(e):
                link = chain(e, "dve_chain")
                for t in range(T):
                    e.wait_ge(scored, t + 1)
                    e.tensor_copy(s1, ps[:, 0:4, :].rearrange("p b (c k) -> p (b c) k", k=KEYS)).then_inc(read, 1)
                    e.wait_ge(read, t + 1)

                    def top16(n, src, spare, v, i):
                        for c in range(n):
                            last = e.max(v[:, c, 0:8], src[:, c, :])
                        link(last)
                        for c in range(n):
                            e.max_index(i[:, c, 0:8].bitcast(U32), v[:, c, 0:8], src[:, c, :])
                            last = e.match_replace(spare[:, c, :], v[:, c, 0:8], src[:, c, :], LOWEST)
                        link(last)
                        for c in range(n):
                            last = e.max(v[:, c, 8:16], spare[:, c, :])
                        link(last)
                        for c in range(n):
                            last = e.max_index(i[:, c, 8:16].bitcast(U32), v[:, c, 8:16], spare[:, c, :])
                        link(last)

                    top16(16, s1, s2, vals, idx)
                    link(e.tensor_copy(fidx, idx.bitcast(U32)))
                    v4 = vals.rearrange("p (h a) k -> p h a k", a=2)
                    for h in range(PH):
                        last = e.tensor_tensor(cand[:, h, :].rearrange("p (a b) -> p a b", b=TOPK),
                                               bc(v4[:, h, 0, :].unsqueeze(2), TOPK, TOPK),
                                               bc(v4[:, h, 1, :].unsqueeze(1), TOPK, TOPK), ALU.add)
                    link(last)
                    top16(PH, cand, cand2, top, ci)
                    ciu = ci.bitcast(U32).rearrange("p h k -> p (h k)")
                    e.tensor_scalar(cab[:, 0, :].bitcast(U32), ciu, 4, None, ALU.logical_shift_right)
                    link(e.tensor_scalar(cab[:, 1, :].bitcast(U32), ciu, 15, None, ALU.bitwise_and))
                    link(e.tensor_copy(fab, cab.bitcast(U32)))
                    link(e.tensor_copy(gsum, top[:, :, 0]))
                    e.tensor_tensor(top, top, bc(gsum.unsqueeze(2), PH, TOPK), ALU.subtract).then_inc(expd, 1)
                    if t:
                        e.wait_ge(turned, t)
                    f4 = fidx.rearrange("p (h a) k -> p h a k", a=2)
                    for a in range(2):
                        for h in range(PH):
                            last = e.tensor_tensor(cand[:, h, :].rearrange("p (k j) -> p k j", j=TOPK),
                                                   bc(fab[:, a, h * TOPK:(h + 1) * TOPK].unsqueeze(2), TOPK, TOPK),
                                                   bc(iota[:, 0:TOPK].unsqueeze(1), TOPK, TOPK), ALU.is_equal)
                        link(last)
                        for h in range(PH):
                            last = e.tensor_tensor(cand2[:, h, :].rearrange("p (k j) -> p k j", j=TOPK),
                                                   cand[:, h, :].rearrange("p (k j) -> p k j", j=TOPK),
                                                   bc(f4[:, h, a, :].unsqueeze(1), TOPK, TOPK), ALU.mult)
                        link(last)
                        link(e.tensor_reduce(eg[:, a, :], cand2.rearrange("p h (k j) -> p (h k) j", j=TOPK), AX,
                                             ALU.add))
                    e.wait_ge(gated, t + 1)
                    link(e.tensor_reduce(gsum, top, AX, ALU.add))
                    link(e.reciprocal(gsum, gsum))
                    e.tensor_tensor(eg[:, 2, :].rearrange("p (h k) -> p h k", k=TOPK), top,
                                    bc(gsum.unsqueeze(2), PH, TOPK), ALU.mult).then_inc(ready, 1)
                    e.wait_ge(turned, t + 1)
                    e.tensor_copy(egT[:, :, t * P:(t + 1) * P], ps[:, 7, 0:3 * P].rearrange("p (a q) -> p a q", q=P))
            stage(pe=pe, act=act, dve=dve)
            return egT

        GB = 8
        NB = GT // GB

        def gate_stage(egT):
            stg, at = area(0, 2, KEYS, GT)
            oh, at = area(at + 3 * S, 2 * GB, 2, KEYS)
            one_hot, oh_used, copied = (sem("gm_" + n) for n in ("oh", "ohused", "copy"))
            written = [sem(f"gm_written{i}") for i in range(2)]

            def dve(e):
                with e.Fori(0, S // (2 * GB)) as i:
                    for j in range(2 * GB):
                        tok = i * (2 * GB) + j
                        e.wait_ge(oh_used, tok + 1)
                        e.tensor_scalar(oh[:, j, 0, :], iota[:], egT[:, 0, bass.ds(tok, 1)], None, ALU.is_equal)
                        e.tensor_scalar(oh[:, j, 1, :], iota[:], egT[:, 1, bass.ds(tok, 1)],
                                        egT[:, 2, bass.ds(tok, 1)], ALU.is_equal, ALU.mult).then_inc(one_hot, 1)

            def pe(e):
                e.sem_inc(oh_used, 2 * GB)
                with e.Fori(0, S // (2 * GB)) as i:
                    for j in range(2 * GB):
                        if j % 4 == 0:
                            e.wait_ge(copied, i * 4 + j // 4 + 1)
                        e.wait_ge(one_hot, i * (2 * GB) + j + 1)
                        mm = e.matmul(ps[:, j // 4, (j % 4) * P:(j % 4 + 1) * P], oh[:, j, 0, :], oh[:, j, 1, :],
                                      start=True, stop=True)
                        mm.then_inc(oh_used, 1)

            def act(e):
                e.sem_inc(copied, 4)
                for b in range(2):
                    e.sem_inc(written[b], 16)
                quads = GT // 4
                with e.Fori(0, NG // 2) as i:
                    for b in range(2):
                        e.wait_ge(written[b], i * 16 + 16)
                        for q in range(quads):
                            e.wait_ge(oh_used, i * (2 * GT) + (b * GT + 4 * q + 4 + 2 * GB))
                            e.activation(stg[:, b, :, 4 * q:4 * q + 4],
                                         ps[:, q % 4, :].rearrange("p (t k) -> p k t", k=KEYS),
                                         ACT.Copy).then_inc(copied, 1)
                        e.wait_ge(copied, i * (2 * quads) + ((b + 1) * quads + 4))
                        e.dma_start(gates_dram[:, :, bass.ds(i * 2 + b, 1), :].rearrange("c p g n -> p (c g) n"),
                                    stg[:, b, :, :].rearrange("p (c k) t -> p c (k t)", k=E2C)
                                    ).then_inc(written[b], 16)
                for b in range(2):
                    e.wait_ge(written[b], 16 + 16 * (NG // 2))
            stage(pe=pe, act=act, dve=dve)

        FEED_G, FEED_TMP, FEED_W, FEED_ACC, FEED_H = 0, 4096, 6144, 14336, 18432

        def feed_stage(chunks, gated):
            J = N // P
            before = feed_chunks[0]
            feed_chunks[0] += chunks
            r = call("feed")
            scored, acted, weighted, rounded, split, summed, added, w_rounded, h_rounded, h_split = (
                shared("feed_" + n) for n in ("scored", "acted", "weighted", "rounded", "split", "summed", "added",
                                              "w_rounded", "h_rounded", "h_split"))
            s0 = halves(4 * chunks, (summed, 8 * (before + chunks)))
            g, _ = area(FEED_G, 2, NG, E2C * GT)
            tmp, _ = area(FEED_TMP, J, S)
            w = arena_parts[:, FEED_W:FEED_W + 4 * J * S].rearrange("p (c h j t) -> p c h j t", c=2, h=2, j=J)
            acc = area(FEED_ACC, T, D)[0] if gated else x
            h_high = arena_parts[:, FEED_H:FEED_H + KC * S].rearrange("p (k t) -> p k t", k=KC)
            h = (h_high, hT_parts)
            if gated:
                g_in = [sem(f"feed_g{i}") for i in range(2)]

            def what(q):
                if q < 4:
                    return "u", q // 2, q % 2
                k = (q - 4) // 2
                return ("v", k // 2, q % 2) if k % 2 == 0 else ("u", 2 + k // 2, q % 2)

            def wait_products(e, q, m):
                kind, c, a = what(q)
                if kind == "u":
                    e.wait_ge(scored, m * 2 * J + J * (before + c) + 2 * a + 2)
                else:
                    e.wait_ge(summed, m * 16 + 8 * (before + c) + 4 * a + 4)

            def steps(do):
                for q in range(6):
                    do(q, *what(q), 0)
                with do.eng.Fori(0, (chunks - 2) // 2) as m:
                    for q in range(6, 14):
                        do(q, *what(q), m)
                for a in range(2):
                    do(4 * chunks - 2 + a, "v", chunks - 1, a, None)

            def pe(e):
                def do(q, kind, c, a, m):
                    m = 0 if m is None else m
                    e.wait_ge(slab_used, m * 8 + s0 + q + 1)
                    part = w_parts[:, q % 2]
                    if kind == "u":
                        u = part.rearrange("p h (k n) -> p h k n", k=KC)
                        for j in (2 * a, 2 * a + 1):
                            if c:
                                e.wait_ge(acted, m * 2 * J + J * (before + c - 1) + j + 1)
                            for k in range(KC):
                                if c == 0 and j == 0:
                                    e.wait_ge(h_split, r * KC + k + 1)
                                for n, (pw, ph) in enumerate(PASSES):
                                    mm = e.matmul(ps[:, j, :], u[:, pw, k, (j % 2) * P:(j % 2 + 1) * P],
                                                  h[ph][:, k, :], start=k == 0 and n == 0,
                                                  stop=k == KC - 1 and n == 2)
                            mm.then_inc(scored, 1)
                        return
                    v = part.rearrange("p h (j n) -> p h j n", j=J)
                    if a == 0:
                        e.wait_ge(split, m * 2 * J + J * (before + c + 1))
                    for t in range(T):
                        if c or a:
                            e.wait_ge(added, m * 16 + 8 * (before + c) + 4 * a + t - 3)
                        for j in range(J):
                            for n, (pw, pv) in enumerate(PASSES):
                                mm = e.matmul(ps[:, 4 + t, :], w[:, c % 2, pw, j, t * P:(t + 1) * P],
                                              v[:, pv, j, :], start=j == 0 and n == 0, stop=j == J - 1 and n == 2)
                        mm.then_inc(summed, 1)
                do.eng = e
                steps(do)

            def act(e):
                def high(q, m=0):
                    i = s0 + q
                    e.wait_ge(slab_in[i % RING], m * (16 * 8 // RING) + 16 * (i // RING + 1))
                    if q >= 2:
                        wait_products(e, q - 2, m)
                    e.activation(w_parts[:, q % 2, 0, :], half(i), ACT.Copy).then_inc(w_rounded, 1)

                def do(q, kind, c, a, m):
                    if kind == "u":
                        for j in (2 * a, 2 * a + 1):
                            e.wait_ge(scored, m * 2 * J + J * (before + c) + j + 1)
                            if c:
                                e.wait_ge(split, m * 2 * J + J * (before + c - 1) + j + 1)
                            e.activation(tmp[:, j, :], ps[:, j, :], ACT.Gelu if gated else ACT.Relu
                                         ).then_inc(acted, 1)
                        for j in (2 * a, 2 * a + 1):
                            e.wait_ge(weighted, m * 2 * J + J * (before + c) + j + 1)
                            if c >= 2:
                                e.wait_ge(summed, m * 16 + 8 * (before + c - 1))
                            e.activation(w[:, c % 2, 0, j, :], tmp[:, j, :], ACT.Copy).then_inc(rounded, 1)
                    if m is not None:
                        high(q + 2, m)
                high(0)
                for k in range(KC):
                    e.activation(h_high[:, k, :], hT[:, k, :], ACT.Copy).then_inc(h_rounded, 1)
                high(1)
                do.eng = e
                steps(do)

            def pool(e):
                for b in range(2):
                    e.dma_start(g[:, b, :, :], gates_dram[b]).then_inc(g_in[b], 16)
                with e.Fori(0, (chunks - 2) // 2) as m:
                    for b in range(2):
                        e.wait_ge(weighted, m * J * 2 + J * (before + b + 1))
                        e.dma_start(g[:, b, :, :], gates_dram[m * 2 + (b + 2)]).then_inc(g_in[b], 16)

            def dve(e):
                def low(q, m=0):
                    i = s0 + q
                    e.wait_ge(w_rounded, m * 8 + 4 * before + q + 1)
                    e.tensor_tensor(w_parts[:, q % 2, 1, :], half(i), w_parts[:, q % 2, 0, :].bitcast(F32),
                                    ALU.subtract).then_inc(slab_used, 1)

                def do(q, kind, c, a, m):
                    if kind == "u":
                        for j in (2 * a, 2 * a + 1):
                            e.wait_ge(acted, m * 2 * J + J * (before + c) + j + 1)
                            if gated:
                                if j == 0:
                                    e.wait_ge(g_in[c % 2], m * 16 + 16 * (c // 2 + 1))
                                tj = tmp[:, j, :].rearrange("p (g t) -> p g t", t=GT)
                                by = g[:, c % 2, :, j * GT:(j + 1) * GT]
                            else:
                                tj = by = tmp[:, j, :]
                            e.tensor_tensor(tj, tj, by, ALU.mult).then_inc(weighted, 1)
                        for j in (2 * a, 2 * a + 1):
                            e.wait_ge(rounded, m * 2 * J + J * (before + c) + j + 1)
                            e.tensor_tensor(w[:, c % 2, 1, j, :], tmp[:, j, :], w[:, c % 2, 0, j, :].bitcast(F32),
                                            ALU.subtract).then_inc(split, 1)
                    else:
                        for t in range(T):
                            mm = 0 if m is None else m
                            n = mm * 16 + 8 * (before + c) + 4 * a + t + 1
                            e.wait_ge(summed, n)
                            if c:
                                e.wait_ge(added, mm * 16 + 8 * (before + c - 1) + 4 * a + t + 1)
                            to = acc[:, t, a * N:(a + 1) * N]
                            if gated and c == 0:
                                e.tensor_copy(to, ps[:, 4 + t, :]).then_inc(added, 1)
                            else:
                                e.tensor_tensor(to, to, ps[:, 4 + t, :], ALU.add).then_inc(added, 1)
                    if m is not None:
                        low(q + 2, m)
                low(0)
                for k in range(KC):
                    e.wait_ge(h_rounded, r * KC + k + 1)
                    e.tensor_tensor(hT_parts[:, k, :], hT[:, k, :], h_high[:, k, :].bitcast(F32),
                                    ALU.subtract).then_inc(h_split, 1)
                low(1)
                do.eng = e
                steps(do)
            stage(pe=pe, act=act, dve=dve, **({"pool": pool} if gated else {}))
            return acc

        def close_stage(acc):
            frow, _ = area(8192 - D, D)
            sq, ss, rs = w_spare = area(4096, D)[0], small[:, 0:T], small[:, T:2 * T]
            squared, inverse, rooted, fed = (sem("cl_" + n) for n in ("sq", "inv", "root", "fed"))

            def act(e):
                e.dma_start(frow, A["final_g"].partition_broadcast(P)).then_inc(loaded, 16)
                for t in range(T):
                    e.wait_ge(fed, t + 1)
                    if t:
                        e.wait_ge(squared, t)
                    e.activation(sq, x[:, t, :], ACT.Square, accum_out=ss[:, t:t + 1]).then_inc(squared, 1)
                e.wait_ge(inverse, 1)
                e.activation(rs, rs, ACT.Sqrt).then_inc(rooted, 1)

            def dve(e):
                link = chain(e, "dve_chain")
                e.wait_ge(loaded, 112)
                for t in range(T):
                    link(e.tensor_tensor(acc[:, t, :], acc[:, t, :], gate2, ALU.mult))
                    e.tensor_tensor(x[:, t, :], x[:, t, :], acc[:, t, :], ALU.add).then_inc(fed, 1)
                e.wait_ge(squared, T)
                link(e.tensor_scalar(rs, ss, 1.0 / D, EPS, ALU.mult, ALU.add))
                e.reciprocal(rs, rs).then_inc(inverse, 1)
                e.wait_ge(rooted, 1)
                for t in range(T):
                    link(e.scalar_tensor_tensor(x[:, t, :], x[:, t, :], rs[:, t:t + 1], frow, ALU.mult, ALU.mult))
            stage(act=act, dve=dve)

        def attention_stage():
            s0 = slabs(6)
            ao, at = area(0, T, D)
            qT, at = area(at, KC, S)
            kT, at = area(at, KC, S)
            v, at = area(at, T, D)
            strip, at = area(at, 2, S)
            sc, at = area(at, 3, S)
            pt, at = area(at, 3, S)
            U = HEADS2 * T
            den, neg = small[:, 64:64 + U], small[:, 128:128 + U]
            done, freed = sem("qkv_done"), sem("qkv_freed")
            scored, read, maxed, expd, turned, copied, valued, taken_o, strip_ok = (
                sem("at_" + n) for n in ("scored", "read", "maxed", "exp", "turned", "copied", "valued", "taken", "strip"))
            strip_in = [sem(f"at_strip{i}") for i in range(2)]
            rel = A["rel"]

            def pool(e):
                for b in range(2):
                    e.memset(strip[0:64, b, 0:CHUNK], NEG).then_inc(strip_ok, 1)
                for h in range(HEADS2):
                    if h >= 2:
                        e.wait_ge(read, 4 * (h - 1))
                    for r0, n0 in ((0, CHUNK), (64, 0)):
                        e.dma_start(strip[r0:r0 + 64, h % 2, n0:],
                                    bass.AP(rel.tensor, h * rel.shape[1] + r0 + n0, [[1, 64], [1, S - n0]])
                                    ).then_inc(strip_in[h % 2], 16)

            def pe(e):
                for i in range(6):
                    await_slab(e, s0 + i)
                    w = slab_k(s0 + i)
                    for j in range(4):
                        g = 4 * i + j
                        if g >= 8:
                            e.wait_ge(freed, g - 7)
                        for k in range(KC):
                            if i < 4:
                                mm = e.matmul(ps[:, g % 8, :], w[:, k, j * P:(j + 1) * P], hT[:, k, :],
                                              start=k == 0, stop=k == KC - 1)
                            else:
                                mm = e.matmul(ps[:, g % 8, :], hT[:, k, j * P:(j + 1) * P], w[:, k, :],
                                              start=k == 0, stop=k == KC - 1)
                        mm.then_inc(done, 1)
                    e.wait_ge(done, 4 * i + 4)
                    e.sem_inc(slab_used, 1)
                e.wait_ge(freed, 24)

                def values(u):
                    h, t = u // T, u % T
                    e.wait_ge(copied, u + 1)
                    if u % 8 == 0 and u >= 16:
                        e.wait_ge(taken_o, u // 8 - 1)
                    for kb in range(t + 1):
                        mm = e.matmul(ps[:, 4 + (u // 8) % 2, (u % 8) * HEAD:(u % 8 + 1) * HEAD],
                                      pt[:, u % 3, kb * P:(kb + 1) * P], v[:, kb, h * HEAD:(h + 1) * HEAD],
                                      start=kb == 0, stop=kb == t)
                    mm.then_inc(valued, 1)

                for u in range(U + 2):
                    if u < U:
                        h, t = u // T, u % T
                        b = 64 * (h % 2)
                        if u >= 2:
                            e.wait_ge(read, u - 1)
                        e.matmul(ps[:, u % 2, 0:(t + 1) * P], qT[b:b + 64, h // 2, t * P:(t + 1) * P],
                                 kT[b:b + 64, h // 2, 0:(t + 1) * P], start=True, stop=True).then_inc(scored, 1)
                    if 1 <= u <= U:
                        w = u - 1
                        e.wait_ge(expd, w + 1)
                        if w >= 2:
                            e.wait_ge(copied, w - 1)
                        for kb in range(w % T + 1):
                            mm = e.transpose(ps[:, 2 + w % 2, kb * P:(kb + 1) * P], sc[:, w % 3, kb * P:(kb + 1) * P],
                                             ident[:])
                        mm.then_inc(turned, 1)
                    if u >= 2:
                        values(u - 2)

            def act(e):
                for u in range(U + 1):
                    if u < U:
                        w = (u % T + 1) * P
                        e.wait_ge(maxed, u + 1)
                        e.activation(sc[:, u % 3, 0:w], sc[:, u % 3, 0:w], ACT.Exp, bias=neg[:, u:u + 1],
                                     accum_out=den[:, u:u + 1]).then_inc(expd, 1)
                    if u >= 1:
                        a = u - 1
                        w = (a % T + 1) * P
                        e.wait_ge(turned, a + 1)
                        if a >= 3:
                            e.wait_ge(valued, a - 2)
                        e.activation(pt[:, a % 3, 0:w], ps[:, 2 + a % 2, 0:w], ACT.Copy).then_inc(copied, 1)

            def dve(e):
                link = chain(e, "dve_chain")
                for g in range(24):
                    e.wait_ge(done, g + 1)
                    dst = qT[:, g, :] if g < 8 else kT[:, g - 8, :] if g < 16 else v[:, g % 4, (g // 4 - 4) * N:(g // 4 - 3) * N]
                    e.tensor_copy(dst, ps[:, g % 8, :]).then_inc(freed, 1)
                e.wait_ge(strip_ok, 2)

                def backwards(h, w):
                    f = strip[:, h % 2, 0:w]
                    return bass.AP(f.tensor, f.offset + w - 1, [list(f.ap[0]), [-1, w]])

                def take(g):
                    e.wait_ge(valued, 8 * g + 8)
                    e.tensor_copy(ao.rearrange("p t (h d) -> p h t d", d=HEAD)[:, 2 * g:2 * g + 2, :, :],
                                  ps[:, 4 + g % 2, :].rearrange("p (h t d) -> p h t d", h=2, t=T)).then_inc(taken_o, 1)

                for u in range(U):
                    h, t = u // T, u % T
                    w = (t + 1) * P
                    e.wait_ge(scored, u + 1)
                    if t == 0:
                        e.wait_ge(strip_in[h % 2], 32 * (h // 2 + 1))
                    if u >= 3:
                        e.wait_ge(turned, u - 2)
                    e.scalar_tensor_tensor(sc[:, u % 3, 0:w], ps[:, u % 2, 0:w], HEAD ** -0.5,
                                           backwards(h, w), ALU.mult, ALU.add).then_inc(read, 1)
                    e.wait_ge(read, u + 1)
                    e.tensor_reduce(neg[:, u:u + 1], sc[:, u % 3, 0:w], AX, ALU.max, negate=True).then_inc(maxed, 1)
                    if u >= 12 and (u - 12) % 8 == 0:
                        take((u - 12) // 8)
                take(7)
                e.wait_ge(expd, U)
                link(e.reciprocal(den, den))
                for t in range(T):
                    a3 = ao[:, t, :].rearrange("p (h d) -> p h d", d=HEAD)
                    if t == 0:
                        e.wait_ge(taken_o, 8)
                    e.tensor_tensor(a3, a3, bc(den.rearrange("p (h t) -> p h t", t=T)[:, :, t].unsqueeze(2), HEADS2, HEAD),
                                    ALU.mult)
            stage(pe=pe, act=act, dve=dve, pool=pool)
            return ao

        def turn_stage(src):
            r = call("turn")
            turned = shared("turn_turned")

            def pe(e):
                for c in range(KC):
                    for t in range(T):
                        mm = e.transpose(ps[:, c, t * P:(t + 1) * P], src[:, t, c * P:(c + 1) * P], ident[:])
                    mm.then_inc(turned, 1)

            def act(e):
                for c in range(0, KC, 2):
                    e.wait_ge(turned, KC * r + c + 1)
                    e.activation(hT[:, c, :], ps[:, c, :], ACT.Copy)

            def dve(e):
                for c in range(1, KC, 2):
                    e.wait_ge(turned, KC * r + c + 1)
                    e.tensor_copy(hT[:, c, :], ps[:, c, :])
            stage(pe=pe, act=act, dve=dve)


        def dn_in_stage():
            s0 = slabs(8)
            qT, at = area(0, DNH, S)
            kT, at = area(at, DNH, S)
            k_, at = area(at, T, D)
            v, at = area(at, T, D)
            z, at = area(at, T, D)
            PAD = TAPS2 - 1
            zin, at = area(at, 2, S + PAD)
            y, at = area(at, 2, S)
            vt = k_[:, 0, :].rearrange("p (a b) -> p a b", b=S)
            ab = small[:, 192:192 + 64].rearrange("p (t c) -> p t c", c=2 * DNH)
            done, freed, filled, conved, silued, vturned, vcopied = (
                sem("dp_" + n) for n in ("done", "freed", "filled", "conved", "silued", "vturned", "vcopied"))
            zdone, abdone, abread = sem("dp_zdone"), sem("dp_abdone"), sem("dp_abread")

            def pe(e):
                def turn_v(c):
                    e.wait_ge(silued, 16 + c + 1)
                    if c >= 2:
                        e.wait_ge(vcopied, c - 1)
                    for t in range(T):
                        mm = e.transpose(ps[:, 6 + c % 2, t * P:(t + 1) * P], vt[:, c % 2, t * P:(t + 1) * P], ident[:])
                    mm.then_inc(vturned, 1)
                w = col("dn_ab").rearrange("p (k c) -> p k c", c=2 * DNH)
                for t in range(T):
                    for k in range(KC):
                        mm = e.matmul(ps[:, 7, t * 16:(t + 1) * 16], hT[:, k, t * P:(t + 1) * P], w[:, k, :],
                                      start=k == 0, stop=k == KC - 1)
                mm.then_inc(abdone, 1)
                for i in range(8):
                    await_slab(e, s0 + i)
                    w = slab_k(s0 + i)
                    for j in range(4):
                        g = 4 * i + j
                        if g >= 6:
                            e.wait_ge(freed, g - 5)
                        if g == 24:
                            e.wait_ge(abread, 1)
                        for k in range(KC):
                            if i < 6:
                                mm = e.matmul(ps[:, g % 6, :], w[:, k, j * P:(j + 1) * P], hT[:, k, :],
                                              start=k == 0, stop=k == KC - 1)
                            else:
                                mm = e.matmul(ps[:, g % 6, :], hT[:, k, j * P:(j + 1) * P], w[:, k, :],
                                              start=k == 0, stop=k == KC - 1)
                        mm.then_inc(done, 1)
                        if 18 <= g < 26:
                            turn_v(g - 18)
                    e.wait_ge(done, 4 * i + 4)
                    e.sem_inc(slab_used, 1)

            def dst(g):
                return qT[:, g, :] if g < 8 else kT[:, g - 8, :] if g < 16 else vt[:, g % 2, :]

            def act(e):
                def silu(g):
                    e.wait_ge(conved, g + 1)
                    if g >= 18:
                        e.wait_ge(vturned, g - 17)
                    e.activation(dst(g), y[:, g % 2, :], ACT.Silu).then_inc(silued, 1)
                for g in range(24):
                    e.wait_ge(done, g + 1)
                    if g >= 2:
                        e.wait_ge(conved, g - 1)
                    e.activation(zin[:, g % 2, PAD:], ps[:, g % 6, :], ACT.Copy).then_inc(freed, 1)
                    if g:
                        silu(g - 1)
                silu(23)
                for g in range(24, 32):
                    e.wait_ge(done, g + 1)
                    e.activation(z[:, g % 4, (g // 4 - 6) * N:(g // 4 - 5) * N], ps[:, g % 6, :],
                                 ACT.Silu).then_inc(freed, 1)

            def dve(e):
                link = chain(e, "dve_chain")
                link(e.memset(zin[:, :, 0:PAD], 0.0))
                e.wait_ge(abdone, 1)
                e.tensor_copy(ab, ps[:, 7, 0:64].rearrange("p (t c) -> p t c", c=16)).then_inc(abread, 1)
                cw = col("dn_conv_w")

                def copy_v(c):
                    e.wait_ge(vturned, c + 1)
                    e.tensor_copy(v[:, :, c * P:(c + 1) * P],
                                  ps[:, 6 + c % 2, :].rearrange("p (t q) -> p t q", q=P)).then_inc(vcopied, 1)
                for g in range(24):
                    e.wait_ge(freed, g + 1)
                    if g >= 2:
                        e.wait_ge(silued, g - 1)
                    zi, yo = zin[:, g % 2, :], y[:, g % 2, :]
                    link(e.tensor_scalar(yo, zi[:, 0:S], cw[:, g:g + 1], None, ALU.mult))
                    for tap in range(1, TAPS2):
                        ins = e.scalar_tensor_tensor(yo, zi[:, tap:tap + S], cw[:, 24 * tap + g:24 * tap + g + 1], yo,
                                                     ALU.mult, ALU.add)
                        if tap < TAPS2 - 1:
                            link(ins)
                    ins.then_inc(conved, 1)
                    if g >= 20:
                        copy_v(g - 20)
                for c in range(4, 8):
                    copy_v(c)
            stage(pe=pe, act=act, dve=dve)
            return qT, kT, k_, v, z, ab, at

        G_, BETA, EGC, REST, BEGC, EGL, GC = (small[:, 256 + 32 * i:288 + 32 * i] for i in range(7))
        EGL2 = small[:, 480:512]

        def dn_unit_stage(qT, kT, k_, v, z, ab, at):
            sqb, at = area(at - 2 * S - 2 * (S + 3), 2, S)
            squared, summed, summed_read, inverse, rooted, unit, turned = (
                sem("du_" + n) for n in ("sq", "sum", "sumread", "inv", "root", "unit", "turned"))
            ready, logs, sums, gsum, acted = (sem("du_" + n) for n in ("ready", "logs", "sums", "gsum", "acted"))
            tmp = small[:, 0:64]
            t8 = "p (t h) -> p t h"

            def act(e):
                for a, src in enumerate((qT, kT)):
                    for c in range(8):
                        n = 8 * a + c
                        if n >= 2:
                            e.wait_ge(summed, n - 1)
                        e.activation(sqb[:, c % 2, :], src[:, c, :], ACT.Square).then_inc(squared, 1)
                    e.wait_ge(inverse, 8 * (a + 1))
                    e.activation(hT[:], hT[:], ACT.Sqrt).then_inc(rooted, 1)
                e.wait_ge(ready, 1)
                e.activation(tmp[:, 0:32], tmp[:, 0:32], ACT.Exp, scale=-1.0)
                e.activation(small[:, 64:72], row("a_log"), ACT.Exp).then_inc(acted, 1)
                e.wait_ge(acted, 1)
                e.activation(tmp[:, 0:32], tmp[:, 0:32], ACT.Ln, bias=1.0)
                e.activation(BETA.rearrange(t8, h=DNH), ab[:, :, DNH:], ACT.Sigmoid).then_inc(acted, 1)
                e.wait_ge(sums, 1)
                for src in (EGC, REST, EGL, EGL2):
                    last = e.activation(src, src, ACT.Exp)
                last.then_inc(acted, 1)

            def pe(e):
                for n in range(16):
                    e.wait_ge(squared, n + 1)
                    if n >= 4:
                        e.wait_ge(summed_read, n - 3)
                    e.matmul(ps[:, n % 4, :], ones[:], sqb[:, n % 2, :], start=True, stop=True).then_inc(summed, 1)
                for c in range(DNH):
                    e.wait_ge(unit, 8 + c + 1)
                    if c >= 2:
                        e.wait_ge(turned, c - 1)
                    for t in range(T):
                        mm = e.transpose(ps[:, 4 + c % 2, t * P:(t + 1) * P], kT[:, c, t * P:(t + 1) * P], ident[:])
                    mm.then_inc(gsum, 1)
                e.wait_ge(logs, 1)
                e.matmul(ps[0:64, 6, 0:32], blk_tri[0:64, :], G_[0:64, :], start=True, stop=True)
                e.matmul(ps[64:128, 6, 0:32], blk_tri[64:128, :], G_[64:128, :], start=True, stop=True)
                e.matmul(ps[:, 6, 32:64], group64[:], G_, start=True, stop=True)
                e.matmul(ps[:, 6, 64:96], ones[0:64, :], G_[0:64, :], start=True, stop=True)
                e.matmul(ps[:, 7, 0:32], ones[64:128, :], G_[64:128, :], start=True, stop=True).then_inc(gsum, 1)

            def dve(e):
                link = chain(e, "dve_chain")
                a3 = tmp[:, 32:64].rearrange(t8, h=DNH)
                link(e.tensor_tensor(a3, ab[:, :, 0:DNH], bc(row("dt_bias").unsqueeze(1), T, DNH), ALU.add))
                link(e.scalar_tensor_tensor(tmp[:, 0:32], tmp[:, 32:64], -1.0, tmp[:, 32:64], ALU.mult, ALU.max))
                e.tensor_scalar(tmp[:, 32:64], tmp[:, 32:64], 0.0, None, ALU.max).then_inc(ready, 1)
                for a, src in enumerate((qT, kT)):
                    scale = float(DH) if a == 0 else 1.0
                    for c in range(8):
                        n = 8 * a + c
                        e.wait_ge(summed, n + 1)
                        if a == 1 and c == 0:
                            e.wait_ge(unit, 8)
                        e.tensor_scalar(hT[:, c, :], ps[:, n % 4, :], EPS, scale, ALU.add, ALU.mult).then_inc(summed_read, 1)
                        e.wait_ge(summed_read, n + 1)
                        e.reciprocal(hT[:, c, :], hT[:, c, :]).then_inc(inverse, 1)
                    e.wait_ge(rooted, a + 1)
                    for c in range(8):
                        e.tensor_tensor(src[:, c, :], src[:, c, :], hT[:, c, :], ALU.mult).then_inc(unit, 1)
                for c in range(DNH):
                    e.wait_ge(gsum, c + 1)
                    e.tensor_copy(k_[:, :, c * P:(c + 1) * P],
                                  ps[:, 4 + c % 2, :].rearrange("p (t q) -> p t q", q=P)).then_inc(turned, 1)
                e.wait_ge(acted, 2)
                link(e.tensor_tensor(tmp[:, 0:32], tmp[:, 0:32], tmp[:, 32:64], ALU.add))
                link(e.tensor_scalar(tmp[:, 0:32], tmp[:, 0:32], -1.0, None, ALU.mult))
                e.tensor_tensor(G_.rearrange(t8, h=DNH), tmp[:, 0:32].rearrange(t8, h=DNH),
                                bc(small[:, 64:72].unsqueeze(1), T, DNH), ALU.mult).then_inc(logs, 1)
                e.wait_ge(gsum, DNH + 1)
                link(e.tensor_copy(GC, ps[:, 6, 0:32]))
                e.tensor_copy(EGC, GC)
                e.tensor_copy(EGL, ps[:, 6, 64:96])
                e.tensor_copy(EGL2, ps[:, 7, 0:32])
                link(e.tensor_tensor(REST, ps[:, 6, 32:64], GC, ALU.subtract))
                e.sem_inc(sums, 1)
                e.wait_ge(acted, 3)
                link(e.tensor_tensor(BEGC, BETA, EGC, ALU.mult))
            stage(pe=pe, act=act, dve=dve)

        def dn_solve_stage(qT, kT, k_, v, z, ab, at):
            base = at - 2 * (S + 3) - 2 * S
            B4 = T * CHUNK
            mats = [area(base + hh * 6 * B4, 6, T, CHUNK)[0] for hh in range(2)]
            wide = [[area(base + hh * 6 * B4 + 2 * B4 * i, T, DH)[0] for i in range(3)] for hh in range(2)]
            qkT = gates.rearrange("p a b -> p (a b)").rearrange("p (h t c) -> p h t c", h=DNH, t=T)
            wT = hT
            DEC, QK, L, LT, X, XT = range(6)
            NP, ND, NA = 3 + 2 * (LEVELS - 1), 6 + 2 * (LEVELS - 1), 3
            pe_s, dve_s, act_s = sem("ds_pe"), sem("ds_dve"), sem("ds_act")
            halves = ((0, slice(0, 64)), (64, slice(64, 128)))

            def count(per, pair, step, hh):
                return pair * 2 * per + 2 * step + hh + 1

            def bank(hh, b):
                return ps[:, 4 * hh + b, :]

            def part(hh, b, half):
                return bank(hh, b)[:, half * B4:(half + 1) * B4].rearrange("p (t c) -> p t c", t=T)

            def pe(e):
                def blocks(out, lhs, rhs):
                    for t in range(T):
                        for _, sl in halves:
                            mm = e.matmul(out[sl, t, :], lhs(t, sl), rhs(t, sl), start=True, stop=True)
                    return mm

                def step(pair, n, hh):
                    h = 2 * pair + hh
                    m = mats[hh]
                    def wait_d(d):
                        e.wait_ge(dve_s, count(ND, pair, d, hh))

                    def tok(t, sl):
                        return slice(t * P + sl.start, t * P + sl.stop)
                    if n == 0:
                        wait_d(0)
                        if pair:
                            e.wait_ge(act_s, count(NA, pair - 1, 2, hh))
                        blocks(part(hh, 0, 0), lambda t, sl: ones[sl, 0:64], lambda t, sl: m[sl, L, t, :])
                        blocks(part(hh, 0, 1), lambda t, sl: kT[:, h, tok(t, sl)], lambda t, sl: kT[:, h, tok(t, sl)])
                        mm = blocks(part(hh, 1, 0), lambda t, sl: qT[:, h, tok(t, sl)],
                                    lambda t, sl: kT[:, h, tok(t, sl)])
                    elif n == 1:
                        wait_d(2)
                        blocks(part(hh, 2, 0), lambda t, sl: m[sl, L, t, :], lambda t, sl: ident[sl, sl])
                        mm = blocks(part(hh, 2, 1), lambda t, sl: m[sl, QK, t, :], lambda t, sl: ident[sl, sl])
                    elif n < NP - 1 and n % 2 == 0:
                        wait_d(3 + (n - 2))
                        mm = blocks(part(hh, 3, 0), lambda t, sl: m[sl, LT, t, :], lambda t, sl: m[sl, X, t, :])
                    elif n < NP - 1:
                        wait_d(3 + (n - 2))
                        blocks(part(hh, 0, 0), lambda t, sl: m[sl, XT, t, :], lambda t, sl: m[sl, DEC, t, :])
                        mm = blocks(part(hh, 0, 1), lambda t, sl: m[sl, DEC, t, :], lambda t, sl: m[sl, XT, t, :])
                    else:
                        wait_d(ND - 2)
                        kbe, vb = wide[hh][0], wide[hh][1]
                        for t in range(T):
                            for par, sl in enumerate((slice(0, 64), slice(64, 128))):
                                e.matmul(bank(hh, 1)[sl, t * P:(t + 1) * P], m[sl, XT, t, :], vb[sl, t, :],
                                         start=True, stop=True)
                                mm = e.matmul(bank(hh, 2 + par)[:, t * CHUNK:(t + 1) * CHUNK], kbe[sl, t, :], m[sl, XT, t, :],
                                              start=True, stop=True)
                    mm.then_inc(pe_s, 1)

                for pair in range(DNH // 2):
                    for n in range(NP):
                        for hh in range(2):
                            step(pair, n, hh)

            def act(e):
                for pair in range(DNH // 2):
                    for n in range(NA):
                        for hh in range(2):
                            h = 2 * pair + hh
                            m = mats[hh]
                            if n == 0:
                                e.wait_ge(dve_s, count(ND, pair, 1, hh))
                                e.activation(m[:, DEC], m[:, DEC], ACT.Exp, scale=-1.0).then_inc(act_s, 1)
                            elif n == 1:
                                e.wait_ge(pe_s, count(NP, pair, 1, hh))
                                e.activation(m[:, LT], part(hh, 2, 0), ACT.Copy)
                                e.activation(qkT[:, h, :, :], part(hh, 2, 1), ACT.Copy).then_inc(act_s, 1)
                            else:
                                e.wait_ge(pe_s, count(NP, pair, NP - 1, hh))
                                src = ps[:, 4 * hh + 2:4 * hh + 4, 0:B4].rearrange("p a (t c) -> p t a c", c=CHUNK)
                                e.activation(wT[:, h, :].rearrange("p (t a c) -> p t a c", t=T, a=2), src,
                                             ACT.Copy).then_inc(act_s, 1)

            def dve(e):
                link = chain(e, "dve_chain")
                t8 = "p (t h) -> p t h"

                def per_row(a, h, w):
                    return bc(a.rearrange(t8, h=DNH)[:, :, h:h + 1], T, w)

                def mask(m):
                    return bc(m.unsqueeze(1), T, CHUNK)

                def step(pair, n, hh):
                    h = 2 * pair + hh
                    m = mats[hh]
                    head = slice(h * DH, (h + 1) * DH)

                    def wait_p(p):
                        e.wait_ge(pe_s, count(NP, pair, p, hh))
                    if n == 0:
                        ins = e.tensor_tensor(m[:, L], mask(blk_tri[:]), per_row(G_, h, CHUNK), ALU.mult)
                    elif n == 1:
                        wait_p(0)
                        link(e.tensor_tensor(m[:, DEC], part(hh, 0, 0), per_row(GC, h, CHUNK), ALU.subtract))
                        ins = e.tensor_scalar(m[:, DEC], m[:, DEC], 0.0, None, ALU.max)
                    elif n == 2:
                        e.wait_ge(act_s, count(NA, pair, 0, hh))
                        link(e.tensor_tensor(m[:, DEC], m[:, DEC], mask(blk_incl[:]), ALU.mult))
                        e.tensor_tensor(m[:, QK], part(hh, 1, 0), m[:, DEC], ALU.mult)
                        link(e.tensor_tensor(m[:, L], part(hh, 0, 1), m[:, DEC], ALU.mult))
                        link(e.tensor_tensor(m[:, L], m[:, L], per_row(BETA, h, CHUNK), ALU.mult))
                        ins = e.tensor_tensor(m[:, L], m[:, L], mask(blk_strict[:]), ALU.mult)
                    elif n == 3:
                        e.wait_ge(act_s, count(NA, pair, 1, hh))
                        e.scalar_tensor_tensor(m[:, X], m[:, L], -1.0, mask(blk_low[:, 0, :]), ALU.mult, ALU.mult)
                        link(e.scalar_tensor_tensor(m[:, XT], m[:, LT], -1.0, mask(blk_low0[:]), ALU.mult, ALU.mult))
                        e.tensor_tensor(m[:, X], m[:, X], mask(blk_id[:]), ALU.add)
                        ins = e.tensor_tensor(m[:, XT], m[:, XT], mask(blk_id[:]), ALU.add)
                    elif n < ND - 2 and n % 2 == 0:
                        wait_p(n - 2)
                        ins = e.tensor_tensor(m[:, DEC], part(hh, 3, 0), mask(blk_low[:, (n - 2) // 2, :]), ALU.mult)
                    elif n < ND - 2:
                        wait_p(n - 2)
                        e.tensor_tensor(m[:, X], m[:, X], part(hh, 0, 0), ALU.subtract)
                        ins = e.tensor_tensor(m[:, XT], m[:, XT], part(hh, 0, 1), ALU.subtract)
                    elif n == ND - 2:
                        kbe, vb = wide[hh][0], wide[hh][1]
                        e.tensor_tensor(vb, v[:, :, head], per_row(BETA, h, DH), ALU.mult)
                        link(e.tensor_tensor(kbe, k_[:, :, head], per_row(BEGC, h, DH), ALU.mult))
                        ins = e.tensor_tensor(k_[:, :, head], k_[:, :, head], per_row(REST, h, DH), ALU.mult)
                    else:
                        wait_p(NP - 1)
                        ins = e.tensor_copy(v[:, :, head], bank(hh, 1).rearrange("p (t c) -> p t c", t=T))
                    ins.then_inc(dve_s, 1)
                    e.wait_ge(dve_s, count(ND, pair, n, hh))

                for pair in range(DNH // 2):
                    for n in range(ND):
                        for hh in range(2):
                            step(pair, n, hh)
            stage(pe=pe, act=act, dve=dve)
            return qkT, wT

        def dn_scan_stage(qT, kT, k_, v, z, ab, at, qkT, wT):
            o = kT.rearrange("p h s -> p (h s)").rearrange("p (t d) -> p t d", t=T)
            base = at - 2 * (S + 3) - 2 * S
            state, p1 = area(base, DNH, DH)
            fresh, p1 = area(p1, DNH, DH)
            old, p1 = area(p1, DNH, DH)
            NCH = S // CHUNK
            begun, stated, freshed, second, decayed, outs, zero = (
                sem("dc_" + n) for n in ("begun", "state", "fresh", "second", "decayed", "out", "zero"))

            def row_of(c):
                return c // 2, slice(64 * (c % 2), 64 * (c % 2) + 64)

            def egl(c):
                return (EGL, EGL2)[c % 2].rearrange("p (t h) -> p t h", h=DNH)[:, c // 2, :]

            def pool(e):
                e.memset(state, 0.0).then_inc(zero, 1)
                for c in range(NCH):
                    if c == 0:
                        e.wait_ge(zero, 1)
                    else:
                        e.wait_ge(stated, c)
                    e.tensor_tensor(old, state, bc(egl(c).unsqueeze(2), DNH, DH), ALU.mult).then_inc(decayed, 1)

            def pe(e):
                for c in range(NCH):
                    t, sl = row_of(c)
                    cs = slice(c * CHUNK, (c + 1) * CHUNK)
                    if c == 0:
                        e.wait_ge(zero, 1)
                    else:
                        e.wait_ge(stated, c)
                        e.wait_ge(outs, c)
                    for h in range(DNH):
                        mm = e.matmul(ps[sl, h // 4, (h % 4) * DH:(h % 4 + 1) * DH], wT[:, h, cs], state[:, h, :],
                                      start=True, stop=True)
                    mm.then_inc(begun, 1)
                    for h in range(DNH):
                        mm = e.matmul(ps[sl, 2 + h // 4, (h % 4) * DH:(h % 4 + 1) * DH], qT[:, h, cs], state[:, h, :],
                                      start=True, stop=True)
                    e.wait_ge(freshed, c + 1)
                    for h in range(DNH):
                        mm = e.matmul(ps[:, 6 + h // 4, (h % 4) * DH:(h % 4 + 1) * DH],
                                      k_[sl, t, h * DH:(h + 1) * DH], fresh[sl, h, :], start=True, stop=True)
                    mm.then_inc(second, 1)
                    for h in range(DNH):
                        mm = e.matmul(ps[sl, 4 + h // 4, (h % 4) * DH:(h % 4 + 1) * DH], qkT[sl, h, t, :],
                                      fresh[sl, h, :], start=True, stop=True)
                    mm.then_inc(second, 1)

            def dve(e):
                link = chain(e, "dve_chain")
                e.wait_ge(zero, 1)
                for c in range(NCH):
                    t, sl = row_of(c)

                    def wide(a):
                        return a.rearrange("p b (h d) -> p (b h) d", d=DH)
                    e.wait_ge(begun, c + 1)
                    e.tensor_tensor(fresh[sl, :, :], v[sl, t, :].rearrange("p (h d) -> p h d", d=DH),
                                    wide(ps[sl, 0:2, :]), ALU.subtract).then_inc(freshed, 1)
                    e.wait_ge(second, 2 * c + 1)
                    e.wait_ge(decayed, c + 1)
                    e.tensor_tensor(state, old, wide(ps[:, 6:8, :]), ALU.add).then_inc(stated, 1)
                    e.wait_ge(second, 2 * c + 2)
                    ov = o[sl, t, :].rearrange("p (h d) -> p h d", d=DH)
                    eg = EGC.rearrange("p (t h) -> p t h", h=DNH)[sl, t, :]
                    link(e.tensor_tensor(ov, wide(ps[sl, 2:4, :]), bc(eg.unsqueeze(2), DNH, DH), ALU.mult))
                    e.tensor_tensor(ov, ov, wide(ps[sl, 4:6, :]), ALU.add).then_inc(outs, 1)
            stage(pe=pe, dve=dve, pool=pool)
            return o

        def dn_out_stage(o, z, at):
            base = at - 2 * (S + 3) - 2 * S
            sq, _ = area(base, 2, D)
            ss, rs = small[:, 0:32], small[:, 32:64]
            squared, summed, inverse, rooted = (sem("do_" + n) for n in ("sq", "sum", "inv", "root"))

            def act(e):
                for t in range(T):
                    if t >= 2:
                        e.wait_ge(summed, t - 1)
                    e.activation(sq[:, t % 2, :], o[:, t, :], ACT.Square).then_inc(squared, 1)
                e.wait_ge(inverse, 1)
                e.activation(rs, rs, ACT.Sqrt).then_inc(rooted, 1)

            def dve(e):
                link = chain(e, "dve_chain")
                for t in range(T):
                    e.wait_ge(squared, t + 1)
                    e.tensor_reduce(ss[:, t * DNH:(t + 1) * DNH], sq[:, t % 2, :].rearrange("p (h d) -> p h d", d=DH),
                                    AX, ALU.add).then_inc(summed, 1)
                e.wait_ge(summed, T)
                link(e.tensor_scalar(rs, ss, 1.0 / DH, EPS, ALU.mult, ALU.add))
                e.reciprocal(rs, rs).then_inc(inverse, 1)
                for t in range(T):
                    z3 = z[:, t, :].rearrange("p (h d) -> p h d", d=DH)
                    last = e.tensor_tensor(z3, z3, bc(row("head_norm").unsqueeze(1), DNH, DH), ALU.mult)
                link(last)
                e.wait_ge(rooted, 1)
                for t in range(T):
                    o3 = o[:, t, :].rearrange("p (h d) -> p h d", d=DH)
                    last = e.tensor_tensor(o3, o3, bc(rs[:, t * DNH:(t + 1) * DNH].unsqueeze(2), DNH, DH), ALU.mult)
                link(last)
                for t in range(T):
                    e.tensor_tensor(o[:, t, :], o[:, t, :], z[:, t, :], ALU.mult)
            stage(act=act, dve=dve)

        def final_stage():
            y, at = area(0, T, D)
            frow, at = area(at, D)
            ss, rs = small[:, 0:T], small[:, T:2 * T]
            squared, inverse, rooted, ready = (sem("fi_" + n) for n in ("sq", "inv", "root", "ready"))

            def act(e):
                e.dma_start(frow, A["final_norm"].partition_broadcast(P)).then_inc(loaded, 16)
                for t in range(T):
                    e.activation(y[:, t, :], x[:, t, :], ACT.Square, accum_out=ss[:, t:t + 1]).then_inc(squared, 1)
                e.wait_ge(inverse, 1)
                e.activation(rs, rs, ACT.Sqrt).then_inc(rooted, 1)
                for t in range(T):
                    e.wait_ge(ready, t + 1)
                    e.dma_start(out[t * P:(t + 1) * P, :], y[:, t, :]).then_inc(stored, 16)
                e.wait_ge(stored, 16 * T)

            def dve(e):
                link = chain(e, "dve_chain")
                e.wait_ge(loaded, 128)
                e.wait_ge(squared, T)
                link(e.tensor_scalar(rs, ss, 1.0 / D, EPS, ALU.mult, ALU.add))
                e.reciprocal(rs, rs).then_inc(inverse, 1)
                e.wait_ge(rooted, 1)
                for t in range(T):
                    e.scalar_tensor_tensor(y[:, t, :], x[:, t, :], rs[:, t:t + 1], frow, ALU.mult,
                                           ALU.mult).then_inc(ready, 1)
            stage(act=act, dve=dve)

        ada_stage()
        norm_stage("n1", mod1, ada[:, 0:KC])
        a = in_stage()
        mix_stage(*a)
        residual_stage("wo1", gate1, A["b_out"])
        norm_stage("n2", mod2, ada[:, 3 * KC:4 * KC])
        egT = route_stage()
        gate_stage(egT)
        acc = feed_stage(ECH, True)
        close_stage(acc)
        norm_stage("n3", col("attn_norm"))
        ao = attention_stage()
        turn_stage(ao)
        residual_stage("wo2")
        norm_stage("n4", col("mlp_norm0"))
        feed_stage(MLP_CH, False)
        norm_stage("n5", col("dn_norm"))
        dn = dn_in_stage()
        dn_unit_stage(*dn)
        qk = dn_solve_stage(*dn)
        o = dn_scan_stage(*dn, *qk)
        dn_out_stage(o, dn[4], dn[6])
        turn_stage(o)
        residual_stage("wo3")
        norm_stage("n6", col("mlp_norm1"))
        feed_stage(MLP_CH, False)
        final_stage()

        block = ctx.enter_context(nc.Block())

        def between(e, n):
            e.drain().then_inc(stage_done, 1)
            e.wait_ge(stage_done, 4 * (n + 1))

        @block.sync
        def _(e):
            full, part = 0, 0
            for n, (at, count, _) in enumerate(loads):
                halved = loads[n][2] is not None
                if n and halved != (loads[n - 1][2] is not None):
                    e.wait_ge(slab_used, at)
                    if not halved:
                        e.wait_ge(*loads[n - 1][2])
                if halved:
                    for b in range(RING):
                        if not (n and loads[n - 1][2] is None):
                            e.wait_ge(slab_used, at + b - RING + 1)
                        e.dma_start(half(at + b), A["halves"][part + b]).then_inc(slab_in[(at + b) % RING], 16)
                    with e.Fori(0, count // RING - 1) as m:
                        for b in range(RING):
                            e.wait_ge(slab_used, m * RING + (at + b + 1))
                            e.dma_start(half(at + b),
                                        A["halves"][bass.ds(m * RING + (part + RING + b), 1)].rearrange(
                                            "o p n -> p (o n)")).then_inc(slab_in[(at + b) % RING], 16)
                    part += count
                    continue
                for i in range(at, at + count):
                    if i >= RING:
                        e.wait_ge(slab_used, i - RING + 1)
                    e.dma_start(slab(i), A["stream"][full + i - at]).then_inc(slab_in[i % RING], 16)
                full += count

        @block.tensor
        def _(e):
            for n, s in enumerate(stages):
                if "pe" in s:
                    s["pe"](e)
                between(e, n)

        @block.scalar
        def _(e):
            for n, s in enumerate(stages):
                if "act" in s:
                    s["act"](e)
                between(e, n)

        @block.vector
        def _(e):
            for n, s in enumerate(stages):
                if "dve" in s:
                    s["dve"](e)
                between(e, n)

        @block.gpsimd
        def _(e):
            for n, s in enumerate(stages):
                if "pool" in s:
                    s["pool"](e)
                between(e, n)


def layout(inp):
    def colv(a):
        return np.asarray(a).reshape(-1, P).T

    def slabs(w, width=N):
        w = np.asarray(w)
        n = w.shape[1] // width
        return w.reshape(KC, P, n, width).transpose(2, 1, 0, 3).reshape(n, P, KC * width)

    g = {k: np.asarray(v) for k, v in inp.items()}
    heads = [h for c in range(4) for h in (c, c + 4)]
    perm = np.concatenate([np.arange(h * HEAD, (h + 1) * HEAD) for h in heads] + [np.arange(AW, g["w_in"].shape[1])])
    w_in, b_in = g["w_in"][:, perm], g["b_in"][perm]
    kv = np.zeros((1, P, SLAB), np.float32)
    kv[:, :, :KC * 256] = slabs(w_in[:, AW:AW + 256], 256)
    keys = np.zeros((1, P, SLAB), np.float32)
    keys[0, :, :16 * KEYS] = np.stack([g["peer_keys1"], g["peer_keys2"]], 1).transpose(3, 0, 1, 2).reshape(P, 16 * KEYS)
    u = g["peer_u"].reshape(KEYS, ECH, 2, 2, KC, P).transpose(1, 2, 5, 4, 3, 0).reshape(ECH, 2, P, HALF)
    v = g["peer_v"].reshape(KEYS, ECH, E2C, 2, N).transpose(1, 3, 0, 2, 4).reshape(ECH, 2, P, HALF)

    def feed(u, v):
        order = [u[0]] + [h for c in range(1, len(u)) for h in (u[c], v[c - 1])] + [v[-1]]
        return np.concatenate(order)

    def mlp(i):
        up = slabs(g["mlp_w_up_2"][i], 2 * P).reshape(MLP_CH, 2, P, HALF)
        down = g["mlp_w_down_2"][i].reshape(MLP_CH, N // P, P, 2, N).transpose(0, 3, 2, 1, 4)
        return feed(up, down.reshape(MLP_CH, 2, P, HALF))

    dn = g["dn_w_in_2"][0]
    parts = [slabs(g["w_ada"]), slabs(w_in[:, :AW]), kv, slabs(w_in[:, AW + 256:]), slabs(g["w_out"]),
             slabs(g["w_query"]), keys, slabs(g["attn_w_qkv_2"][0]), slabs(g["attn_w_o_2"][0]),
             slabs(dn[:, :4 * D]), slabs(g["dn_w_o_2"][0])]
    ab = dn[:, 4 * D:].reshape(KC, P, 2 * DNH).transpose(1, 0, 2).reshape(P, -1)
    cv = {"c": colv(g["c"]), "b_ada": colv(g["b_ada"]), "norm1_g": colv(g["norm1_g"]), "b_in": colv(b_in),
          "conv_w": colv(g["conv_w"]), "conv_out_g": colv(g["conv_out_g"]), "norm2_g": colv(g["norm2_g"]),
          "attn_norm": colv(g["attn_norm_2"]), "mlp_norm0": colv(g["mlp_norm_2"][0]),
          "mlp_norm1": colv(g["mlp_norm_2"][1]), "dn_norm": colv(g["dn_norm_2"]),
          "dn_conv_w": colv(g["dn_conv_w_2"]), "dn_ab": ab}
    rv = {"b_v": g["b_in"][AW + P:AW + 2 * P], "attn_out_g": g["attn_out_g"], "sinks": g["attn_sinks"],
          "head_norm": g["dn_head_norm_2"][0], "dt_bias": g["dn_dt_bias_2"][0], "a_log": g["dn_a_log_2"][0]}
    rb = g["attn_rel_bias_2"][0]
    rel = np.concatenate([rb[:, MAX_REL - P + 1:], np.repeat(rb[:, -1:], S - 1 - MAX_REL, 1)], 1)
    return {
        "stream": np.concatenate(parts), "halves": np.concatenate([feed(u, v), mlp(0), mlp(1)]), "cols": np.concatenate([cv[n] for n in COLS], 1),
        "rows": np.concatenate([rv[n] for n in ROWS]), "b_gate1": g["b_ada"][2 * D:3 * D],
        "b_gate2": g["b_ada"][5 * D:], "b_out": g["b_out"], "final_g": g["final_g"],
        "final_norm": g["final_norm_2"], "rel": rel, "x": g["x"].reshape(T, P, D).transpose(1, 0, 2),
    }


def kernel(**inputs):
    import concourse.bacc as bacc
    from concourse.bass_utils import run_bass_kernel_spmd

    nc = bacc.Bacc("TRN2", target_bir_lowering=False, num_devices=1)
    arrays = {name: np.ascontiguousarray(a) for name, a in layout(inputs).items()}
    handles = {name: nc.dram_tensor(name, a.shape, mybir.dt.from_np(a.dtype), kind="ExternalInput").ap()
               for name, a in arrays.items()}
    out = nc.dram_tensor("out", (S, D), F32, kind="ExternalOutput").ap()
    program(nc, handles, out)
    result = run_bass_kernel_spmd(nc, [arrays], core_ids=[0])
    return result.results[0]["out"].reshape(1, S, D)
```

```python
from contextlib import ExitStack

import numpy as np
import concourse.bass as bass
from concourse import mybir

F32 = mybir.dt.float32
F32R = mybir.dt.float32r
U32 = mybir.dt.uint32
ALU = mybir.AluOpType
ACT = mybir.ActivationFunctionType
AX = mybir.AxisListType.X

P = 128
D = 1024
S = 512
T = S // P
KC = D // P
N = 512
EPS = 1e-6
NEG = -1e30
LOWEST = -3.4e38

HEAD = 64
HEADS1 = 8
AW = HEADS1 * HEAD
CW = D - AW
TAPS1 = 3
KEYS = 128
EXPERTS = KEYS * KEYS
PH = 8
TOPK = 16
HEADS2 = 16
MAX_REL = 256
CHUNK = 64
DH = 128
DNH = D // DH
TAPS2 = 4
FF = 4 * D
FC = FF // P

SLAB = KC * N
HALF = SLAB // 2
RING = 4
E2C = SLAB // D
ECH = KEYS // E2C
GT = 64
NG = S // GT

COLS = {}
_at = 0
for _name, _n in (("c", KC), ("b_ada", 6 * KC), ("norm1_g", KC), ("b_in", 18), ("conv_w", TAPS1 * 4),
                  ("conv_out_g", 4), ("norm2_g", KC), ("attn_norm", KC), ("mlp_norm0", KC), ("mlp_norm1", KC),
                  ("dn_norm", KC), ("dn_conv_w", TAPS2 * 24), ("dn_ab", KC * 2 * DNH)):
    COLS[_name] = (_at, _n)
    _at += _n
NCOL = _at
ROWS = {}
_at = 0
for _name, _n in (("b_v", P), ("attn_out_g", AW), ("sinks", HEADS1), ("head_norm", DH), ("dt_bias", DNH),
                  ("a_log", DNH)):
    ROWS[_name] = (_at, _n)
    _at += _n
NROW = _at
BIGROWS = ("b_gate1", "b_gate2", "b_out", "final_g", "final_norm")

ARENA = 23568
ADA_SLABS = 12
MLP_CH = FF // N
PASSES = ((0, 0), (0, 1), (1, 0))


def program(nc, A, out):
    ctx = ExitStack()
    with ctx:
        def sb(name, shape, dt=F32):
            return ctx.enter_context(nc.sbuf_tensor(name, shape, dt))

        def sem(name):
            return ctx.enter_context(nc.semaphore(name))

        ps = ctx.enter_context(nc.psum_tensor("ps", [P, 8, N], F32))
        x = sb("x_res", [P, T, D])
        hT = sb("hT", [P, KC, S])
        hT_parts = nc.alloc_sbuf_tensor_at("hT_parts", [P, KC, S], F32R, offset=nc.sbuf_base - 4 * KC * S)
        ring = sb("ring", [P, RING, SLAB])
        parts_at = nc.sbuf_base - 4 * RING * SLAB // 2
        w_parts = nc.alloc_sbuf_tensor_at("w_parts", [P, 2, 2, HALF], F32R, offset=parts_at)
        cols = sb("cols_sb", [P, NCOL])
        rows = sb("rows_sb", [P, NROW])
        gates = sb("gates", [P, 2, D])
        gate1, gate2 = gates[:, 0, :], gates[:, 1, :]
        ada = sb("ada", [P, 6 * KC])
        mod1 = sb("mod1", [P, KC])
        mod2 = sb("mod2", [P, KC])
        ident = sb("ident", [P, P])
        ones = sb("ones", [P, P])
        group64 = sb("group64", [P, P])
        iota = sb("iota", [P, P])
        LEVELS = 6
        blk_id, blk_tri, blk_strict, blk_incl, blk_low0 = (
            sb("blk_" + n, [P, CHUNK]) for n in ("id", "tri", "strict", "incl", "low0"))
        blk_low = sb("blk_low", [P, LEVELS, CHUNK])
        small = sb("small", [P, 512])
        arena = sb("arena", [P, ARENA])
        arena_parts = nc.alloc_sbuf_tensor_at("arena_parts", [P, ARENA], F32R, offset=nc.sbuf_base - 4 * ARENA)

        def col(name, i=0, n=None):
            at, m = COLS[name]
            return cols[:, at + i:at + i + (n if n is not None else m - i)]

        def row(name):
            at, m = ROWS[name]
            return rows[:, at:at + m]

        def area(at, *shape):
            n = int(np.prod(shape))
            v = arena[:, at:at + n]
            if len(shape) == 2:
                v = v.rearrange("p (a b) -> p a b", b=shape[1])
            if len(shape) == 3:
                v = v.rearrange("p (a b c) -> p a b c", b=shape[1], c=shape[2])
            return v, at + n

        def bc(ap, *shape):
            return ap.broadcast_to([ap.shape[0], *shape])

        slab_in = [sem(f"slab_in{i}") for i in range(RING)]
        slab_used = sem("slab_used")
        stage_done = sem("stage_done")
        loaded = sem("loaded")
        consts = sem("consts")
        stored = sem("stored")

        gates_dram = nc.dram_tensor("gates_dram", [ECH, P, NG, E2C * GT], F32, kind="Internal").ap()
        by_name, calls = {}, {}

        def shared(name):
            if name not in by_name:
                by_name[name] = sem(name)
            return by_name[name]

        def call(kind):
            calls[kind] = calls.get(kind, -1) + 1
            return calls[kind]

        feed_chunks = [0]
        stages = []
        halves_taken = [0]
        taken = [0]

        def stage(**parts):
            stages.append(parts)

        loads = []

        def slabs(n):
            at = taken[0]
            taken[0] += n
            loads.append((at, n, None))
            return at

        def halves(n, done):
            at, before = taken[0], halves_taken[0]
            taken[0] += n
            halves_taken[0] += n
            loads.append((at, n, done))
            return at, before

        def half(i):
            return ring[:, (i % RING) // 2, (i % 2) * HALF:(i % 2 + 1) * HALF]

        def slab(i):
            return ring[:, i % RING, :]

        def slab_k(i, width=N):
            return ring[:, i % RING, 0:KC * width].rearrange("p (k n) -> p k n", n=width)

        def await_slab(eng, i):
            eng.wait_ge(slab_in[i % RING], 16 * (i // RING + 1))

        class Chain:
            def __init__(self, eng, name):
                self.eng, self.sem, self.n = eng, sem(name), 0

            def __call__(self, ins):
                self.n += 1
                ins.then_inc(self.sem, 1)
                self.eng.wait_ge(self.sem, self.n)

        chains = {}

        def chain(eng, name):
            if name not in chains:
                chains[name] = Chain(eng, name)
            return chains[name]

        def ada_stage():
            s0 = slabs(ADA_SLABS)
            sc, at = area(0, KC)
            scb, at = area(at, KC, P)
            diag, at = area(at, ADA_SLABS - 4, N)
            bits, at = area(at, 6, CHUNK)
            bitf, at = area(at, 6, CHUNK)
            I32 = mybir.dt.int32
            act_silu = sem("act_silu")
            wide = sem("silu_wide")
            picked = sem("ada_picked")

            def act(e):
                e.dma_start(cols[:], A["cols"]).then_inc(loaded, 16)
                e.wait_ge(loaded, 16)
                e.activation(sc, col("c"), ACT.Silu).then_inc(act_silu, 1)
                e.dma_start(rows[:], A["rows"].partition_broadcast(P)).then_inc(loaded, 16)
                e.dma_start(gate1, A["b_gate1"].partition_broadcast(P)).then_inc(loaded, 16)
                e.dma_start(gate2, A["b_gate2"].partition_broadcast(P)).then_inc(loaded, 16)
                e.dma_start(x[:], A["x"]).then_inc(loaded, 16)

            def pool(e):
                e.memset(ident[:], 0.0).then_inc(consts, 1)
                e.memset(ones[:], 1.0).then_inc(consts, 1)
                e.memset(group64[:], 0.0).then_inc(consts, 1)
                e.iota(iota[:], [[1, P]], base=0, channel_multiplier=0,
                       allow_small_or_imprecise_dtypes=True).then_inc(consts, 1)
                e.wait_ge(consts, 4)
                e.affine_select(out=ident[:], in_=ident[:], compare_op=ALU.not_equal, fill=1.0, base=0,
                                pattern=[[-1, P]], channel_multiplier=1).then_inc(consts, 1)
                e.wait_ge(consts, 5)
                e.memset(group64[0:64, 0:64], 1.0).then_inc(consts, 1)
                e.wait_ge(consts, 6)
                e.memset(group64[64:128, 64:128], 1.0).then_inc(consts, 1)
                e.wait_ge(consts, 7)
                for r0 in (0, 64):
                    e.iota(bits[r0:r0 + 64, 0, :].bitcast(I32), [[0, CHUNK]], base=0, channel_multiplier=1
                           ).then_inc(consts, 1)
                e.wait_ge(consts, 9)
                e.iota(bits[:, 1, :].bitcast(I32), [[1, CHUNK]], base=0, channel_multiplier=0).then_inc(consts, 1)
                e.wait_ge(consts, 10)

            def bank(i):
                return 1 + (i // 2 == 5) * 2 + i % 2 if i // 2 in (2, 5) else (0, 5, 6, 7)[i % 4]

            vectors = [i for i in range(ADA_SLABS) if i // 2 not in (2, 5)]

            def pe(e):
                e.wait_ge(wide, 1)
                for i in range(ADA_SLABS):
                    before = [n for n, v in enumerate(vectors) if v < i and bank(v) == bank(i)]
                    if i in vectors and before:
                        e.wait_ge(picked, before[-1] + 1)
                    await_slab(e, s0 + i)
                    w = slab_k(s0 + i)
                    for k in range(KC):
                        mm = e.matmul(ps[:, bank(i), :], scb[:, k, :], w[:, k, :], start=k == 0, stop=k == KC - 1)
                    mm.then_inc(slab_used, 1)

            def dve(e):
                link = chain(e, "dve_chain")
                e.wait_ge(consts, 2)
                e.wait_ge(act_silu, 1)
                for k in range(KC):
                    last = e.tensor_scalar(scb[:, k, :], ones[:], sc[:, k:k + 1], None, ALU.mult)
                last.then_inc(wide, 1)
                e.wait_ge(consts, 10)
                link(e.tensor_copy(bitf[:, 0:2, :], bits[:, 0:2, :].bitcast(I32)))
                rf, cf = bitf[:, 0, :], bitf[:, 1, :]
                for m, op in ((blk_id, ALU.is_equal), (blk_tri, ALU.is_le), (blk_strict, ALU.is_gt),
                              (blk_incl, ALU.is_ge)):
                    e.tensor_tensor(m[:], rf, cf, op)
                for s in range(LEVELS):
                    link(e.tensor_scalar(bits[:, 2:4, :].bitcast(I32), bits[:, 0:2, :].bitcast(I32), s, None,
                                         ALU.arith_shift_right))
                    link(e.tensor_tensor(bits[:, 4, :].bitcast(I32), bits[:, 2, :].bitcast(I32),
                                         bits[:, 3, :].bitcast(I32), ALU.bitwise_xor))
                    link(e.tensor_scalar(bits[:, 2:4, :].bitcast(I32), bits[:, 2:4, :].bitcast(I32), 1, None,
                                         ALU.bitwise_and))
                    link(e.tensor_copy(bitf[:, 2:5, :], bits[:, 2:5, :].bitcast(I32)))
                    link(e.scalar_tensor_tensor(blk_low[:, s, :], bitf[:, 4, :], 1.0, bitf[:, 2, :], ALU.is_equal,
                                                ALU.mult))
                    if s == 0:
                        link(e.scalar_tensor_tensor(blk_low0[:], bitf[:, 4, :], 1.0, bitf[:, 3, :], ALU.is_equal,
                                                    ALU.mult))
                for n, i in enumerate(vectors):
                    d = diag[:, n, :].rearrange("p (c q) -> p c q", q=P)
                    e.wait_ge(slab_used, s0 + i + 1)
                    e.tensor_tensor(d, ps[:, bank(i), :].rearrange("p (c q) -> p c q", q=P),
                                    bc(ident[:].unsqueeze(1), N // P, P), ALU.mult).then_inc(picked, 1)
                    e.wait_ge(picked, n + 1)
                    link(e.tensor_reduce(ada[:, i * (N // P):(i + 1) * (N // P)], d, AX, ALU.add))
                e.wait_ge(slab_used, s0 + ADA_SLABS)
                e.wait_ge(loaded, 80)
                for a, b in ((0, 2), (3, 5)):
                    link(e.tensor_tensor(ada[:, a * KC:b * KC], ada[:, a * KC:b * KC],
                                         col("b_ada", a * KC, (b - a) * KC), ALU.add))
                for mod, g, a in ((mod1, "norm1_g", 1), (mod2, "norm2_g", 4)):
                    link(e.scalar_tensor_tensor(mod[:], ada[:, a * KC:(a + 1) * KC], 1.0, col(g), ALU.add, ALU.mult))
                for g, i in ((gate1, 4), (gate2, 10)):
                    for n in range(2):
                        link(e.tensor_tensor(g[:, n * N:(n + 1) * N], ps[:, bank(i + n), :], g[:, n * N:(n + 1) * N],
                                             ALU.add))
            stage(pe=pe, act=act, dve=dve, pool=pool)

        def rms_scale(e_dve, link, e_act_sem, dst, ss, width):
            link(e_dve.tensor_scalar(dst, ss, 1.0 / width, EPS, ALU.mult, ALU.add))

        def norm_stage(tag, g, b=None, at=0):
            xn, _ = area(at, T, D)
            ss, rs = small[:, 0:T], small[:, T:2 * T]
            r = call("norm")
            squared, inverse, rooted, normed, turned = (
                shared("norm_" + n) for n in ("squared", "inverse", "rooted", "normed", "turned"))

            def act(e):
                for t in range(T + 1):
                    if t < T:
                        e.activation(xn[:, t, :], x[:, t, :], ACT.Square, accum_out=ss[:, t:t + 1]
                                     ).then_inc(squared, 1)
                    if t:
                        e.wait_ge(inverse, r * T + t)
                        e.activation(rs[:, t - 1:t], rs[:, t - 1:t], ACT.Sqrt).then_inc(rooted, 1)
                for c in range(0, KC, 2):
                    e.wait_ge(turned, r * KC + c + 1)
                    e.activation(hT[:, c, :], ps[:, c, :], ACT.Identity, scale=g[:, c:c + 1],
                                 bias=b[:, c:c + 1] if b is not None else 0.0)

            def dve(e):
                link = chain(e, "dve_chain")
                for t in range(T + 1):
                    if t < T:
                        e.wait_ge(squared, r * T + t + 1)
                        link(e.tensor_scalar(rs[:, t:t + 1], ss[:, t:t + 1], 1.0 / D, EPS, ALU.mult, ALU.add))
                        e.reciprocal(rs[:, t:t + 1], rs[:, t:t + 1]).then_inc(inverse, 1)
                    if t:
                        e.wait_ge(rooted, r * T + t)
                        e.tensor_scalar(xn[:, t - 1, :], x[:, t - 1, :], rs[:, t - 1:t], None, ALU.mult
                                        ).then_inc(normed, 1)
                for c in range(1, KC, 2):
                    e.wait_ge(turned, r * KC + c + 1)
                    if b is None:
                        e.tensor_scalar(hT[:, c, :], ps[:, c, :], g[:, c:c + 1], None, ALU.mult)
                    else:
                        e.tensor_scalar(hT[:, c, :], ps[:, c, :], g[:, c:c + 1], b[:, c:c + 1], ALU.mult, ALU.add)

            def pe(e):
                for t in range(T):
                    e.wait_ge(normed, r * T + t + 1)
                    for c in range(KC):
                        mm = e.transpose(ps[:, c, t * P:(t + 1) * P], xn[:, t, c * P:(c + 1) * P], ident[:])
                        if t == T - 1:
                            mm.then_inc(turned, 1)
            stage(pe=pe, act=act, dve=dve)

        def slab_channels(e, i, outs, width=N, src=None, first=0, done=None, wait=None):
            src = hT if src is None else src
            w = slab_k(i, width)
            await_slab(e, i)
            for j in outs:
                if wait:
                    wait(j)
                for k in range(KC):
                    mm = e.matmul(ps[:, (first + j) % 8, :], w[:, k, j * P:(j + 1) * P], src[:, k, :],
                                  start=k == 0, stop=k == KC - 1)
                mm.then_inc(done, 1)
            return mm

        class Projection:
            def __init__(self, channels, tokens, banks, h_at, done):
                self.channels, self.count, self.banks, self.done = channels, channels + tokens, banks, done
                self.r = call("split")
                self.s0, self.h0 = halves(self.count, (done, self.groups(self.count)))
                high = arena_parts[:, h_at:h_at + KC * S].rearrange("p (k t) -> p k t", k=KC)
                self.h = (high, hT_parts)
                self.w_rounded, self.h_rounded, self.h_split = (
                    shared(n) for n in ("w_rounded", "h_rounded", "h_split"))

            def groups(self, q):
                return 2 * min(q, self.channels) + 4 * max(q - self.channels, 0)

            def last(self, g):
                return next((q for q in range(self.count) if self.groups(q + 1) == g + 1), None)

            def products(self, e, q, before):
                e.wait_ge(slab_used, self.s0 + q + 1)
                if q == 0:
                    e.wait_ge(self.h_split, (self.r + 1) * KC)
                w = w_parts[:, q % 2].rearrange("p h (k n) -> p h k n", k=KC)
                for g in range(self.groups(q), self.groups(q + 1)):
                    before(g)
                    j = g - self.groups(q)
                    for k in range(KC):
                        for n, (a, b) in enumerate(PASSES):
                            flags = dict(start=k == 0 and n == 0, stop=k == KC - 1 and n == 2)
                            if q < self.channels:
                                mm = e.matmul(ps[:, g % self.banks, :], w[:, a, k, j * P:(j + 1) * P],
                                              self.h[b][:, k, :], **flags)
                            else:
                                mm = e.matmul(ps[:, g % self.banks, 0:2 * P], self.h[a][:, k, j * P:(j + 1) * P],
                                              w[:, b, k, :], **flags)
                    mm.then_inc(self.done, 1)

            def high(self, e, q):
                if q >= self.count:
                    return
                i = self.s0 + q
                await_slab(e, i)
                if q >= 2:
                    e.wait_ge(self.done, self.groups(q - 1))
                e.activation(w_parts[:, q % 2, 0, :], half(i), ACT.Copy).then_inc(self.w_rounded, 1)

            def low(self, e, q):
                if q >= self.count:
                    return
                e.wait_ge(self.w_rounded, self.h0 + q + 1)
                e.tensor_tensor(w_parts[:, q % 2, 1, :], half(self.s0 + q), w_parts[:, q % 2, 0, :].bitcast(F32),
                                ALU.subtract).then_inc(slab_used, 1)

            def start_high(self, e, src=None, ready=None):
                self.high(e, 0)
                for k in range(KC):
                    if ready is not None:
                        e.wait_ge(ready, k + 1)
                    e.activation(self.h[0][:, k, :], (hT if src is None else src)[:, k, :], ACT.Copy
                                 ).then_inc(self.h_rounded, 1)
                self.high(e, 1)

            def start_low(self, e, src=None):
                self.low(e, 0)
                for k in range(KC):
                    e.wait_ge(self.h_rounded, self.r * KC + k + 1)
                    e.tensor_tensor(hT_parts[:, k, :], (hT if src is None else src)[:, k, :],
                                    self.h[0][:, k, :].bitcast(F32),
                                    ALU.subtract).then_inc(self.h_split, 1)
                self.low(e, 1)

        def in_stage():
            s0 = slabs(5)
            qT, at = area(0, 4, S)
            kT, at = area(at, S)
            v, at = area(at, T, P)
            bcu, at = area(at, 12, S)
            done, freed = sem("in_done"), sem("in_freed")

            def pe(e):
                def wait(g):
                    if g >= 8:
                        e.wait_ge(freed, g - 7)
                for i in range(5):
                    await_slab(e, s0 + i)
                    w = slab_k(s0 + i, 256 if i == 1 else N)
                    for j in range(2 if i == 1 else 4):
                        g = (0, 4, 6, 10, 14)[i] + j
                        wait(g)
                        if i == 1 and j == 1:
                            for t in range(T):
                                for k in range(KC):
                                    mm = e.matmul(ps[:, g % 8, t * P:(t + 1) * P], hT[:, k, t * P:(t + 1) * P],
                                                  w[:, k, P:2 * P], start=k == 0, stop=k == KC - 1)
                        else:
                            for k in range(KC):
                                mm = e.matmul(ps[:, g % 8, :], w[:, k, j * P:(j + 1) * P], hT[:, k, :],
                                              start=k == 0, stop=k == KC - 1)
                        mm.then_inc(done, 1)
                    e.wait_ge(done, g + 1)
                    e.sem_inc(slab_used, 1)

            def dve(e):
                for g in range(18):
                    e.wait_ge(done, g + 1)
                    if g == 5:
                        ins = e.tensor_tensor(v, ps[:, g % 8, :].rearrange("p (t c) -> p t c", c=P),
                                              bc(row("b_v").unsqueeze(1), T, P), ALU.add)
                    else:
                        dst = qT[:, g, :] if g < 4 else kT if g == 4 else bcu[:, g - 6, :]
                        ins = e.tensor_scalar(dst, ps[:, g % 8, :], col("b_in", g, 1), None, ALU.add)
                    ins.then_inc(freed, 1)
            stage(pe=pe, dve=dve)
            return qT, kT, v, bcu, at

        def mix_stage(qT, kT, v, bcu, at):
            z, at = area(at, 4, S + TAPS1 - 1)
            y, at = area(at, 4, S)
            sc, at = area(at, HEADS1, 2 * P)
            mask, at = area(at, 2 * P)
            pt, at = area(at, 4, 4, P)
            ao, at = area(at, AW)
            sq, at = area(at, AW)
            tmp = bcu
            mx, es, den, rd = (small[:, 16 + 8 * i:24 + 8 * i] for i in range(4))
            hs, hr = small[:, 48:56], small[:, 56:64]
            masked, squares, sums, sums_read, inverse, rooted = (
                sem("mix_" + n) for n in ("mask", "sq", "sum", "sumread", "inv", "root"))
            scored, read, prob, expd = (sem("mix_" + n) for n in ("scored", "read", "prob", "exp"))
            turned, copied, valued, hinv, hroot, normed, oT, oC = (
                sem("mix_" + n) for n in ("turned", "copied", "valued", "hinv", "hroot", "normed", "oT", "oC"))

            def pool(e):
                e.memset(mask, 0.0).then_inc(masked, 1)
                e.wait_ge(masked, 1)
                e.affine_select(out=mask[:, 0:P], in_=mask[:, 0:P], compare_op=ALU.is_gt, fill=NEG, base=0,
                                pattern=[[1, P]], channel_multiplier=-1).then_inc(masked, 1)
                e.affine_select(out=mask[:, P:], in_=mask[:, P:], compare_op=ALU.is_ge, fill=NEG, base=0,
                                pattern=[[-1, P]], channel_multiplier=1).then_inc(masked, 1)

            def lo(t):
                return P if t == 0 else 0

            def pe(e):
                def conv_sums():
                    e.wait_ge(squares, 1)
                    for c in range(4):
                        mm = e.matmul(ps[:, c, :], group64[:], tmp[:, c, :], start=True, stop=True)
                    mm.then_inc(sums, 1)
                    e.wait_ge(sums_read, 1)

                def turn_out(t):
                    e.wait_ge(normed, t + 1)
                    if t:
                        e.wait_ge(oC, t)
                    for c in range(4):
                        mm = e.transpose(ps[:, 7, c * P:(c + 1) * P], ao[:, c * P:(c + 1) * P], ident[:])
                    mm.then_inc(oT, 1)

                for t in range(T):
                    if t:
                        e.wait_ge(read, t)
                    if t == 2:
                        conv_sums()
                    for h in range(HEADS1):
                        b = 64 * (h // 4)
                        mm = e.matmul(ps[:, h // 2, (h % 2) * 2 * P + lo(t):(h % 2 + 1) * 2 * P],
                                      qT[b:b + 64, h % 4, t * P:(t + 1) * P],
                                      kT[b:b + 64, (t - 1) * P + lo(t):(t + 1) * P], start=True, stop=True)
                    mm.then_inc(scored, 1)
                    if t:
                        turn_out(t - 1)
                    e.wait_ge(prob, t + 1)
                    for pair in range(4):
                        n = 4 * t + pair
                        if n >= 2:
                            e.wait_ge(copied, n - 1)
                        blocks = [(h, half) for h in (2 * pair, 2 * pair + 1) for half in (0, 1) if t or half]
                        for h, half in blocks:
                            mm = e.transpose(ps[:, 4 + n % 2, (2 * (h % 2) + half) * P:(2 * (h % 2) + half + 1) * P],
                                             sc[:, h, half * P:(half + 1) * P], ident[:])
                        mm.then_inc(turned, 1)
                        if pair:
                            values(e, t, pair - 1)
                    values(e, t, 3)
                turn_out(T - 1)

            def values(e, t, pair):
                n = 4 * t + pair
                e.wait_ge(copied, n + 1)
                if pair == 0 and t:
                    e.wait_ge(hinv, t)
                for h in (2 * pair, 2 * pair + 1):
                    kv = h // 4
                    for half in range(t == 0, 2):
                        mm = e.matmul(ps[:, 6, h * HEAD:(h + 1) * HEAD], pt[:, n % 4, 2 * (h % 2) + half, :],
                                      v[:, t - 1 + half, kv * HEAD:(kv + 1) * HEAD],
                                      start=half == (t == 0), stop=half == 1)
                mm.then_inc(valued, 1)

            def dve(e):
                link = chain(e, "dve_chain")
                def conv():
                    link(e.memset(z[:, :, 0:TAPS1 - 1], 0.0))
                    link(e.tensor_tensor(z[:, :, TAPS1 - 1:], bcu[:, 4:8, :], bcu[:, 8:12, :], ALU.mult))
                    for c in range(4):
                        e.tensor_scalar(y[:, c, :], z[:, c, 0:S], col("conv_w", c, 1), None, ALU.mult)
                    for tap in (1, 2):
                        link(e.engine_nop())
                        for c in range(4):
                            last = e.scalar_tensor_tensor(y[:, c, :], z[:, c, tap:tap + S], col("conv_w", 4 * tap + c, 1),
                                                          y[:, c, :], ALU.mult, ALU.add)
                    link(last)
                    link(e.tensor_tensor(y, y, bcu[:, 0:4, :], ALU.mult))
                    e.tensor_tensor(tmp[:, 0:4, :], y, y, ALU.mult).then_inc(squares, 1)

                e.wait_ge(masked, 3)

                def finish(t):
                    e.wait_ge(valued, 4 * t + 4)
                    a3 = ao.rearrange("p (h d) -> p h d", d=HEAD)
                    s3 = sq.rearrange("p (h d) -> p h d", d=HEAD)
                    if t:
                        e.wait_ge(oT, t)
                    link(e.tensor_tensor(a3, ps[:, 6, :].rearrange("p (h d) -> p h d", d=HEAD),
                                         bc(rd.unsqueeze(2), HEADS1, HEAD), ALU.mult))
                    link(e.tensor_tensor(sq, ao, ao, ALU.mult))
                    link(e.tensor_reduce(hs, s3, AX, ALU.add))
                    link(e.tensor_scalar(hr, hs, 1.0 / HEAD, EPS, ALU.mult, ALU.add))
                    e.reciprocal(hr, hr).then_inc(hinv, 1)
                    e.wait_ge(hroot, t + 1)
                    link(e.tensor_tensor(a3, a3, bc(hr.unsqueeze(2), HEADS1, HEAD), ALU.mult))
                    e.tensor_tensor(ao, ao, row("attn_out_g"), ALU.mult).then_inc(normed, 1)

                for t in range(T):
                    e.wait_ge(scored, t + 1)
                    if t:
                        e.wait_ge(turned, 4 * t)
                    w = 2 * P - lo(t)
                    s3 = sc[:, :, lo(t):]
                    e.scalar_tensor_tensor(
                        s3, ps[:, 0:4, :].rearrange("p b (h k) -> p (b h) k", k=2 * P)[:, :, lo(t):], HEAD ** -0.5,
                        bc(mask[:, lo(t):].unsqueeze(1), HEADS1, w), ALU.mult, ALU.add).then_inc(read, 1)
                    e.wait_ge(read, t + 1)
                    link(e.tensor_reduce(mx, s3, AX, ALU.max))
                    link(e.tensor_tensor(mx, mx, row("sinks"), ALU.max))
                    link(e.tensor_tensor(es, row("sinks"), mx, ALU.subtract))
                    e.tensor_scalar(mx, mx, -1.0, None, ALU.mult).then_inc(expd, 1)
                    if t == 0:
                        conv()
                    if t == 2:
                        e.reciprocal(z[:, :, 0:S], z[:, :, 0:S]).then_inc(inverse, 1)
                    if t == 3:
                        e.wait_ge(rooted, 1)
                        link(e.tensor_tensor(y, y, z[:, :, 0:S], ALU.mult))
                        for c in range(4):
                            e.tensor_scalar(hT[:, 4 + c, :], y[:, c, :], col("conv_out_g", c, 1), None, ALU.mult)
                    e.wait_ge(prob, t + 1)
                    link(e.tensor_tensor(den, den, es, ALU.add))
                    link(e.reciprocal(rd, den))
                    finish(t)
                    if t == 1:
                        e.wait_ge(sums, 1)
                        e.tensor_scalar(z[:, :, 0:S], ps[:, 0:4, :], 1.0 / HEAD, EPS, ALU.mult, ALU.add
                                        ).then_inc(sums_read, 1)
                        e.wait_ge(sums_read, 1)

            def act(e):
                def out_copy(t):
                    e.wait_ge(oT, t + 1)
                    e.activation(hT[:, 0:4, t * P:(t + 1) * P], ps[:, 7, :].rearrange("p (c q) -> p c q", q=P),
                                 ACT.Copy).then_inc(oC, 1)

                for t in range(T):
                    e.wait_ge(expd, t + 1)
                    e.activation(es, es, ACT.Exp)
                    for h in range(HEADS1):
                        last = e.activation(sc[:, h, lo(t):], sc[:, h, lo(t):], ACT.Exp, bias=mx[:, h:h + 1],
                                            accum_out=den[:, h:h + 1])
                    last.then_inc(prob, 1)
                    if t:
                        out_copy(t - 1)
                    for pair in range(4):
                        n = 4 * t + pair
                        e.wait_ge(turned, n + 1)
                        if n >= 4:
                            e.wait_ge(valued, n - 3)
                        src = ps[:, 4 + n % 2, :].rearrange("p (b q) -> p b q", q=P)
                        if t:
                            e.activation(pt[:, n % 4, :, :], src, ACT.Copy).then_inc(copied, 1)
                        else:
                            e.activation(pt[:, n % 4, 1::2, :], src[:, 1::2, :], ACT.Copy).then_inc(copied, 1)
                    e.wait_ge(hinv, t + 1)
                    e.activation(hr, hr, ACT.Sqrt).then_inc(hroot, 1)
                    if t == 2:
                        e.wait_ge(inverse, 1)
                        e.activation(z[:, :, 0:S], z[:, :, 0:S], ACT.Sqrt).then_inc(rooted, 1)
                out_copy(T - 1)
            stage(pe=pe, act=act, dve=dve, pool=pool)

        def residual_stage(tag, gate=None, bias=None, src=None):
            s0 = slabs(2)
            src = hT if src is None else src
            brow, at = area(0, D)
            tmp, at = area(at, 2, N)
            r = call("residual")
            done = shared("residual_done")

            def act(e):
                if bias is not None:
                    e.dma_start(brow, bias.partition_broadcast(P)).then_inc(loaded, 16)

            def pe(e):
                for n in range(2):
                    await_slab(e, s0 + n)
                    w = slab_k(s0 + n)
                    for t in range(T):
                        for k in range(KC):
                            mm = e.matmul(ps[:, 4 * n + t, :], src[:, k, t * P:(t + 1) * P], w[:, k, :],
                                          start=k == 0, stop=k == KC - 1)
                        mm.then_inc(done, 1)
                    e.wait_ge(done, 8 * r + 4 * n + 4)
                    e.sem_inc(slab_used, 1)

            def dve(e):
                link = chain(e, "dve_chain")
                if bias is not None:
                    e.wait_ge(loaded, 96)
                for n in range(2):
                    cs = slice(n * N, (n + 1) * N)
                    for t in range(T):
                        e.wait_ge(done, 8 * r + 4 * n + t + 1)
                        src_ = ps[:, 4 * n + t, :]
                        if bias is not None:
                            link(e.tensor_tensor(tmp[:, 0, :], src_, brow[:, cs], ALU.add))
                            src_ = tmp[:, 0, :]
                        if gate is not None:
                            link(e.tensor_tensor(tmp[:, 1, :], src_, gate[:, cs], ALU.mult))
                            src_ = tmp[:, 1, :]
                        link(e.tensor_tensor(x[:, t, cs], x[:, t, cs], src_, ALU.add))
            stage(pe=pe, act=act, dve=dve)

        def route_stage():
            s0 = slabs(4)
            qT, at = area(0, 16, S)
            s1, at = area(at, 16, KEYS)
            s2, at = area(at, 16, KEYS)
            cand, at = area(at, PH, TOPK * TOPK)
            cand2 = s2.rearrange("p a b -> p (a b)").rearrange("p (h c) -> p h c", c=TOPK * TOPK)
            vals, at = area(at, 16, TOPK)
            idx, at = area(at, 16, TOPK)
            fidx, at = area(at, 16, TOPK)
            top, at = area(at, PH, TOPK)
            ci, at = area(at, PH, TOPK)
            cab, at = area(at, 2, PH * TOPK)
            fab, at = area(at, 2, PH * TOPK)
            eg, at = area(at, 3, PH * TOPK)
            gsum, at = area(at, PH)
            assert at <= 2 * KEYS * GT
            egT, at = area(2 * KEYS * GT, 3, S)
            keys, _ = area(2 * KEYS * GT + 3 * S, 16 * KEYS)
            done, freed, keys_in = sem("rt_done"), sem("rt_freed"), sem("rt_keys")
            scored, read, expd, gated, ready, turned = (
                sem("rt_" + n) for n in ("scored", "read", "exp", "gated", "ready", "turned"))

            def pe(e):
                def query(t, i):
                    n = 4 * t + i
                    if n >= 3:
                        e.wait_ge(freed, n - 2)
                    w = slab_k(s0 + i)
                    if t == 0:
                        await_slab(e, s0 + i)
                    for j in range(4):
                        for k in range(KC):
                            mm = e.matmul(ps[:, 4 + n % 3, j * P:(j + 1) * P], w[:, k, j * P:(j + 1) * P],
                                          hT[:, k, t * P:(t + 1) * P], start=k == 0, stop=k == KC - 1)
                    mm.then_inc(done, 1)

                def turn(t):
                    e.wait_ge(ready, t + 1)
                    for i in range(3):
                        mm = e.transpose(ps[:, 7, i * P:(i + 1) * P], eg[:, i, :], ident[:])
                    mm.then_inc(turned, 1)

                for t in range(T):
                    for i in range(4):
                        query(t, i)
                    if t:
                        e.wait_ge(read, t)
                    else:
                        e.wait_ge(keys_in, 16)
                    e.wait_ge(freed, 4 * t + 4)
                    for c in range(16):
                        mm = e.matmul(ps[:, c // 4, (c % 4) * P:(c % 4 + 1) * P], qT[:, c, t * P:(t + 1) * P],
                                      keys[:, c * KEYS:(c + 1) * KEYS], start=True, stop=True)
                    mm.then_inc(scored, 1)
                    if t:
                        turn(t - 1)
                e.wait_ge(done, 4 * T)
                e.sem_inc(slab_used, 4)
                turn(T - 1)

            def act(e):
                e.dma_start(keys, A["keys"]).then_inc(keys_in, 16)
                def copy(t):
                    for i in range(4):
                        n = 4 * t + i
                        e.wait_ge(done, n + 1)
                        e.activation(qT[:, 4 * i:4 * i + 4, t * P:(t + 1) * P],
                                     ps[:, 4 + n % 3, :].rearrange("p (c q) -> p c q", q=P), ACT.Copy
                                     ).then_inc(freed, 1)

                copy(0)
                for t in range(T):
                    if t + 1 < T:
                        copy(t + 1)
                    e.wait_ge(expd, t + 1)
                    e.activation(top, top, ACT.Exp).then_inc(gated, 1)

            def dve(e):
                link = chain(e, "dve_chain")
                for t in range(T):
                    e.wait_ge(scored, t + 1)
                    e.tensor_copy(s1, ps[:, 0:4, :].rearrange("p b (c k) -> p (b c) k", k=KEYS)).then_inc(read, 1)
                    e.wait_ge(read, t + 1)

                    def top16(n, src, spare, v, i):
                        for c in range(n):
                            last = e.max(v[:, c, 0:8], src[:, c, :])
                        link(last)
                        for c in range(n):
                            e.max_index(i[:, c, 0:8].bitcast(U32), v[:, c, 0:8], src[:, c, :])
                            last = e.match_replace(spare[:, c, :], v[:, c, 0:8], src[:, c, :], LOWEST)
                        link(last)
                        for c in range(n):
                            last = e.max(v[:, c, 8:16], spare[:, c, :])
                        link(last)
                        for c in range(n):
                            last = e.max_index(i[:, c, 8:16].bitcast(U32), v[:, c, 8:16], spare[:, c, :])
                        link(last)

                    top16(16, s1, s2, vals, idx)
                    link(e.tensor_copy(fidx, idx.bitcast(U32)))
                    v4 = vals.rearrange("p (h a) k -> p h a k", a=2)
                    for h in range(PH):
                        last = e.tensor_tensor(cand[:, h, :].rearrange("p (a b) -> p a b", b=TOPK),
                                               bc(v4[:, h, 0, :].unsqueeze(2), TOPK, TOPK),
                                               bc(v4[:, h, 1, :].unsqueeze(1), TOPK, TOPK), ALU.add)
                    link(last)
                    top16(PH, cand, cand2, top, ci)
                    ciu = ci.bitcast(U32).rearrange("p h k -> p (h k)")
                    e.tensor_scalar(cab[:, 0, :].bitcast(U32), ciu, 4, None, ALU.logical_shift_right)
                    link(e.tensor_scalar(cab[:, 1, :].bitcast(U32), ciu, 15, None, ALU.bitwise_and))
                    link(e.tensor_copy(fab, cab.bitcast(U32)))
                    link(e.tensor_copy(gsum, top[:, :, 0]))
                    e.tensor_tensor(top, top, bc(gsum.unsqueeze(2), PH, TOPK), ALU.subtract).then_inc(expd, 1)
                    if t:
                        e.wait_ge(turned, t)
                    f4 = fidx.rearrange("p (h a) k -> p h a k", a=2)
                    for a in range(2):
                        for h in range(PH):
                            last = e.tensor_tensor(cand[:, h, :].rearrange("p (k j) -> p k j", j=TOPK),
                                                   bc(fab[:, a, h * TOPK:(h + 1) * TOPK].unsqueeze(2), TOPK, TOPK),
                                                   bc(iota[:, 0:TOPK].unsqueeze(1), TOPK, TOPK), ALU.is_equal)
                        link(last)
                        for h in range(PH):
                            last = e.tensor_tensor(cand2[:, h, :].rearrange("p (k j) -> p k j", j=TOPK),
                                                   cand[:, h, :].rearrange("p (k j) -> p k j", j=TOPK),
                                                   bc(f4[:, h, a, :].unsqueeze(1), TOPK, TOPK), ALU.mult)
                        link(last)
                        link(e.tensor_reduce(eg[:, a, :], cand2.rearrange("p h (k j) -> p (h k) j", j=TOPK), AX,
                                             ALU.add))
                    e.wait_ge(gated, t + 1)
                    link(e.tensor_reduce(gsum, top, AX, ALU.add))
                    link(e.reciprocal(gsum, gsum))
                    e.tensor_tensor(eg[:, 2, :].rearrange("p (h k) -> p h k", k=TOPK), top,
                                    bc(gsum.unsqueeze(2), PH, TOPK), ALU.mult).then_inc(ready, 1)
                    e.wait_ge(turned, t + 1)
                    e.tensor_copy(egT[:, :, t * P:(t + 1) * P], ps[:, 7, 0:3 * P].rearrange("p (a q) -> p a q", q=P))
            stage(pe=pe, act=act, dve=dve)
            return egT

        GB = 8
        NB = GT // GB

        def gate_stage(egT):
            stg, at = area(0, 2, KEYS, GT)
            oh, at = area(at + 3 * S, 2 * GB, 2, KEYS)
            one_hot, oh_used, copied = (sem("gm_" + n) for n in ("oh", "ohused", "copy"))
            written = [sem(f"gm_written{i}") for i in range(2)]

            def dve(e):
                with e.Fori(0, S // (2 * GB)) as i:
                    for j in range(2 * GB):
                        tok = i * (2 * GB) + j
                        if j % GB == 0:
                            e.wait_ge(oh_used, tok + GB)
                            e.tensor_tensor(oh[:, j:j + GB, 0, :], bc(iota[:].unsqueeze(1), GB, KEYS),
                                            bc(egT[:, 0, bass.ds(tok, GB)].unsqueeze(2), GB, KEYS), ALU.is_equal)
                        e.tensor_scalar(oh[:, j, 1, :], iota[:], egT[:, 1, bass.ds(tok, 1)],
                                        egT[:, 2, bass.ds(tok, 1)], ALU.is_equal, ALU.mult).then_inc(one_hot, 1)

            def pe(e):
                e.sem_inc(oh_used, 2 * GB)
                with e.Fori(0, S // (2 * GB)) as i:
                    for j in range(2 * GB):
                        if j % 4 == 0:
                            e.wait_ge(copied, i * 4 + j // 4 + 1)
                        e.wait_ge(one_hot, i * (2 * GB) + j + 1)
                        mm = e.matmul(ps[:, j // 4, (j % 4) * P:(j % 4 + 1) * P], oh[:, j, 0, :], oh[:, j, 1, :],
                                      start=True, stop=True)
                        mm.then_inc(oh_used, 1)

            def act(e):
                e.sem_inc(copied, 4)
                for b in range(2):
                    e.sem_inc(written[b], 16)
                quads = GT // 4
                with e.Fori(0, NG // 2) as i:
                    for b in range(2):
                        e.wait_ge(written[b], i * 16 + 16)
                        for q in range(quads):
                            e.wait_ge(oh_used, i * (2 * GT) + (b * GT + 4 * q + 4 + 2 * GB))
                            e.activation(stg[:, b, :, 4 * q:4 * q + 4],
                                         ps[:, q % 4, :].rearrange("p (t k) -> p k t", k=KEYS),
                                         ACT.Copy).then_inc(copied, 1)
                        e.wait_ge(copied, i * (2 * quads) + ((b + 1) * quads + 4))
                        e.dma_start(gates_dram[:, :, bass.ds(i * 2 + b, 1), :].rearrange("c p g n -> p (c g) n"),
                                    stg[:, b, :, :].rearrange("p (c k) t -> p c (k t)", k=E2C)
                                    ).then_inc(written[b], 16)
                for b in range(2):
                    e.wait_ge(written[b], 16 + 16 * (NG // 2))
            stage(pe=pe, act=act, dve=dve)

        FEED_G, FEED_TMP, FEED_W, FEED_ACC, FEED_H = 0, 4096, 6144, 14336, 18432

        def feed_stage(chunks, gated):
            J = N // P
            before = feed_chunks[0]
            feed_chunks[0] += chunks
            r = call("split")
            scored, acted, weighted, rounded, split, summed, added = (
                shared("feed_" + n) for n in ("scored", "acted", "weighted", "rounded", "split", "summed", "added"))
            w_rounded, h_rounded, h_split = (shared(n) for n in ("w_rounded", "h_rounded", "h_split"))
            s0, h0 = halves(4 * chunks, (summed, 8 * (before + chunks)))
            g, _ = area(FEED_G, 2, NG, E2C * GT)
            tmp, _ = area(FEED_TMP, J, S)
            w = arena_parts[:, FEED_W:FEED_W + 4 * J * S].rearrange("p (c h j t) -> p c h j t", c=2, h=2, j=J)
            acc = area(FEED_ACC, T, D)[0] if gated else x
            h_high = arena_parts[:, FEED_H:FEED_H + KC * S].rearrange("p (k t) -> p k t", k=KC)
            h = (h_high, hT_parts)
            if gated:
                g_in = [sem(f"feed_g{i}") for i in range(2)]

            def what(q):
                if q < 4:
                    return "u", q // 2, q % 2
                k = (q - 4) // 2
                return ("v", k // 2, q % 2) if k % 2 == 0 else ("u", 2 + k // 2, q % 2)

            def wait_products(e, q, m):
                kind, c, a = what(q)
                if kind == "u":
                    e.wait_ge(scored, m * 2 * J + J * (before + c) + 2 * a + 2)
                else:
                    e.wait_ge(summed, m * 16 + 8 * (before + c) + 4 * a + 4)

            def steps(do):
                for q in range(6):
                    do(q, *what(q), 0)
                with do.eng.Fori(0, (chunks - 2) // 2) as m:
                    for q in range(6, 14):
                        do(q, *what(q), m)
                for a in range(2):
                    do(4 * chunks - 2 + a, "v", chunks - 1, a, None)

            def pe(e):
                def do(q, kind, c, a, m):
                    m = 0 if m is None else m
                    e.wait_ge(slab_used, m * 8 + s0 + q + 1)
                    part = w_parts[:, q % 2]
                    if kind == "u":
                        u = part.rearrange("p h (k n) -> p h k n", k=KC)
                        for j in (2 * a, 2 * a + 1):
                            if c:
                                e.wait_ge(acted, m * 2 * J + J * (before + c - 1) + j + 1)
                            for k in range(KC):
                                if c == 0 and j == 0:
                                    e.wait_ge(h_split, r * KC + k + 1)
                                for n, (pw, ph) in enumerate(PASSES):
                                    mm = e.matmul(ps[:, j, :], u[:, pw, k, (j % 2) * P:(j % 2 + 1) * P],
                                                  h[ph][:, k, :], start=k == 0 and n == 0,
                                                  stop=k == KC - 1 and n == 2)
                            mm.then_inc(scored, 1)
                        return
                    v = part.rearrange("p h (j n) -> p h j n", j=J)
                    if a == 0:
                        e.wait_ge(split, m * 2 * J + J * (before + c + 1))
                    for t in range(T):
                        if c or a:
                            e.wait_ge(added, m * 16 + 8 * (before + c) + 4 * a + t - 3)
                        for j in range(J):
                            for n, (pw, pv) in enumerate(PASSES):
                                mm = e.matmul(ps[:, 4 + t, :], w[:, c % 2, pw, j, t * P:(t + 1) * P],
                                              v[:, pv, j, :], start=j == 0 and n == 0, stop=j == J - 1 and n == 2)
                        mm.then_inc(summed, 1)
                do.eng = e
                steps(do)

            def act(e):
                def high(q, m=0):
                    i = s0 + q
                    e.wait_ge(slab_in[i % RING], m * (16 * 8 // RING) + 16 * (i // RING + 1))
                    if q >= 2:
                        wait_products(e, q - 2, m)
                    e.activation(w_parts[:, q % 2, 0, :], half(i), ACT.Copy).then_inc(w_rounded, 1)

                def do(q, kind, c, a, m):
                    if kind == "u":
                        for j in (2 * a, 2 * a + 1):
                            e.wait_ge(scored, m * 2 * J + J * (before + c) + j + 1)
                            if c:
                                e.wait_ge(split, m * 2 * J + J * (before + c - 1) + j + 1)
                            e.activation(tmp[:, j, :], ps[:, j, :], ACT.Gelu if gated else ACT.Relu
                                         ).then_inc(acted, 1)
                        for j in (2 * a, 2 * a + 1):
                            e.wait_ge(weighted, m * 2 * J + J * (before + c) + j + 1)
                            if c >= 2:
                                e.wait_ge(summed, m * 16 + 8 * (before + c - 1))
                            e.activation(w[:, c % 2, 0, j, :], tmp[:, j, :], ACT.Copy).then_inc(rounded, 1)
                    if m is not None:
                        high(q + 2, m)
                high(0)
                for k in range(KC):
                    e.activation(h_high[:, k, :], hT[:, k, :], ACT.Copy).then_inc(h_rounded, 1)
                high(1)
                do.eng = e
                steps(do)

            def pool(e):
                for b in range(2):
                    e.dma_start(g[:, b, :, :], gates_dram[b]).then_inc(g_in[b], 16)
                with e.Fori(0, (chunks - 2) // 2) as m:
                    for b in range(2):
                        e.wait_ge(weighted, m * J * 2 + J * (before + b + 1))
                        e.dma_start(g[:, b, :, :], gates_dram[m * 2 + (b + 2)]).then_inc(g_in[b], 16)

            def dve(e):
                def low(q, m=0):
                    i = s0 + q
                    e.wait_ge(w_rounded, m * 8 + h0 + q + 1)
                    e.tensor_tensor(w_parts[:, q % 2, 1, :], half(i), w_parts[:, q % 2, 0, :].bitcast(F32),
                                    ALU.subtract).then_inc(slab_used, 1)

                def do(q, kind, c, a, m):
                    if kind == "u":
                        for j in (2 * a, 2 * a + 1):
                            e.wait_ge(acted, m * 2 * J + J * (before + c) + j + 1)
                            if gated:
                                if j == 0:
                                    e.wait_ge(g_in[c % 2], m * 16 + 16 * (c // 2 + 1))
                                tj = tmp[:, j, :].rearrange("p (g t) -> p g t", t=GT)
                                by = g[:, c % 2, :, j * GT:(j + 1) * GT]
                            else:
                                tj = by = tmp[:, j, :]
                            e.tensor_tensor(tj, tj, by, ALU.mult).then_inc(weighted, 1)
                        for j in (2 * a, 2 * a + 1):
                            e.wait_ge(rounded, m * 2 * J + J * (before + c) + j + 1)
                            e.tensor_tensor(w[:, c % 2, 1, j, :], tmp[:, j, :], w[:, c % 2, 0, j, :].bitcast(F32),
                                            ALU.subtract).then_inc(split, 1)
                    else:
                        for t in range(T):
                            mm = 0 if m is None else m
                            n = mm * 16 + 8 * (before + c) + 4 * a + t + 1
                            e.wait_ge(summed, n)
                            if c:
                                e.wait_ge(added, mm * 16 + 8 * (before + c - 1) + 4 * a + t + 1)
                            to = acc[:, t, a * N:(a + 1) * N]
                            if gated and c == 0:
                                e.tensor_copy(to, ps[:, 4 + t, :]).then_inc(added, 1)
                            else:
                                e.tensor_tensor(to, to, ps[:, 4 + t, :], ALU.add).then_inc(added, 1)
                    if m is not None:
                        low(q + 2, m)
                low(0)
                for k in range(KC):
                    e.wait_ge(h_rounded, r * KC + k + 1)
                    e.tensor_tensor(hT_parts[:, k, :], hT[:, k, :], h_high[:, k, :].bitcast(F32),
                                    ALU.subtract).then_inc(h_split, 1)
                low(1)
                do.eng = e
                steps(do)
            stage(pe=pe, act=act, dve=dve, **({"pool": pool} if gated else {}))
            return acc

        def close_stage(acc):
            frow, _ = area(8192 - D, D)
            sq, ss, rs = w_spare = area(4096, D)[0], small[:, 0:T], small[:, T:2 * T]
            squared, inverse, rooted, fed = (sem("cl_" + n) for n in ("sq", "inv", "root", "fed"))

            def act(e):
                e.dma_start(frow, A["final_g"].partition_broadcast(P)).then_inc(loaded, 16)
                for t in range(T):
                    e.wait_ge(fed, t + 1)
                    if t:
                        e.wait_ge(squared, t)
                    e.activation(sq, x[:, t, :], ACT.Square, accum_out=ss[:, t:t + 1]).then_inc(squared, 1)
                e.wait_ge(inverse, 1)
                e.activation(rs, rs, ACT.Sqrt).then_inc(rooted, 1)

            def dve(e):
                link = chain(e, "dve_chain")
                e.wait_ge(loaded, 112)
                for t in range(T):
                    link(e.tensor_tensor(acc[:, t, :], acc[:, t, :], gate2, ALU.mult))
                    e.tensor_tensor(x[:, t, :], x[:, t, :], acc[:, t, :], ALU.add).then_inc(fed, 1)
                e.wait_ge(squared, T)
                link(e.tensor_scalar(rs, ss, 1.0 / D, EPS, ALU.mult, ALU.add))
                e.reciprocal(rs, rs).then_inc(inverse, 1)
                e.wait_ge(rooted, 1)
                for t in range(T):
                    link(e.scalar_tensor_tensor(x[:, t, :], x[:, t, :], rs[:, t:t + 1], frow, ALU.mult, ALU.mult))
            stage(act=act, dve=dve)

        def attention_stage():
            ao, at = area(0, T, D)
            qT, at = area(at, KC, S)
            kT, at = area(at, KC, S)
            v, at = area(at, T, D)
            strip, at = area(at, 2, S)
            sc, at = area(at, 3, S)
            pt, at = area(at, 3, S)
            U = HEADS2 * T
            den, neg = small[:, 64:64 + U], small[:, 128:128 + U]
            done, freed = sem("qkv_done"), sem("qkv_freed")
            scored, read, maxed, expd, turned, copied, valued, taken_o, strip_ok = (
                sem("at_" + n) for n in ("scored", "read", "maxed", "exp", "turned", "copied", "valued", "taken", "strip"))
            strip_in = [sem(f"at_strip{i}") for i in range(2)]
            rel = A["rel"]
            proj = Projection(8, 4, 8, 0, done)

            def pool(e):
                for b in range(2):
                    e.memset(strip[0:64, b, 0:CHUNK], NEG).then_inc(strip_ok, 1)
                for h in range(HEADS2):
                    if h >= 2:
                        e.wait_ge(read, 4 * (h - 1))
                    for r0, n0 in ((0, CHUNK), (64, 0)):
                        e.dma_start(strip[r0:r0 + 64, h % 2, n0:],
                                    bass.AP(rel.tensor, h * rel.shape[1] + r0 + n0, [[1, 64], [1, S - n0]])
                                    ).then_inc(strip_in[h % 2], 16)

            def pe(e):
                for q in range(proj.count):
                    proj.products(e, q, lambda g: e.wait_ge(freed, g - 7) if g >= 8 else None)
                e.wait_ge(freed, 32)

                def values(u):
                    h, t = u // T, u % T
                    e.wait_ge(copied, u + 1)
                    if u % 8 == 0 and u >= 16:
                        e.wait_ge(taken_o, u // 8 - 1)
                    for kb in range(t + 1):
                        mm = e.matmul(ps[:, 4 + (u // 8) % 2, (u % 8) * HEAD:(u % 8 + 1) * HEAD],
                                      pt[:, u % 3, kb * P:(kb + 1) * P], v[:, kb, h * HEAD:(h + 1) * HEAD],
                                      start=kb == 0, stop=kb == t)
                    mm.then_inc(valued, 1)

                for u in range(U + 2):
                    if u < U:
                        h, t = u // T, u % T
                        b = 64 * (h % 2)
                        if u >= 2:
                            e.wait_ge(read, u - 1)
                        e.matmul(ps[:, u % 2, 0:(t + 1) * P], qT[b:b + 64, h // 2, t * P:(t + 1) * P],
                                 kT[b:b + 64, h // 2, 0:(t + 1) * P], start=True, stop=True).then_inc(scored, 1)
                    if 1 <= u <= U:
                        w = u - 1
                        e.wait_ge(expd, w + 1)
                        if w >= 2:
                            e.wait_ge(copied, w - 1)
                        for kb in range(w % T + 1):
                            mm = e.transpose(ps[:, 2 + w % 2, kb * P:(kb + 1) * P], sc[:, w % 3, kb * P:(kb + 1) * P],
                                             ident[:])
                        mm.then_inc(turned, 1)
                    if u >= 2:
                        values(u - 2)

            def act(e):
                proj.start_high(e)
                for q in range(2, proj.count):
                    proj.high(e, q)
                for u in range(U + 1):
                    if u < U:
                        w = (u % T + 1) * P
                        e.wait_ge(maxed, u + 1)
                        e.activation(sc[:, u % 3, 0:w], sc[:, u % 3, 0:w], ACT.Exp, bias=neg[:, u:u + 1],
                                     accum_out=den[:, u:u + 1]).then_inc(expd, 1)
                    if u >= 1:
                        a = u - 1
                        w = (a % T + 1) * P
                        e.wait_ge(turned, a + 1)
                        if a >= 3:
                            e.wait_ge(valued, a - 2)
                        e.activation(pt[:, a % 3, 0:w], ps[:, 2 + a % 2, 0:w], ACT.Copy).then_inc(copied, 1)

            def dve(e):
                link = chain(e, "dve_chain")
                proj.start_low(e)
                for g in range(32):
                    e.wait_ge(done, g + 1)
                    if g < 16:
                        e.tensor_copy(qT[:, g, :] if g < 8 else kT[:, g - 8, :], ps[:, g % 8, :]).then_inc(freed, 1)
                    else:
                        i = (g - 16) // 4
                        e.tensor_copy(v[:, g % 4, i * 2 * P:(i + 1) * 2 * P], ps[:, g % 8, 0:2 * P]).then_inc(freed, 1)
                    if proj.last(g) is not None:
                        proj.low(e, proj.last(g) + 2)
                e.wait_ge(strip_ok, 2)

                def backwards(h, w):
                    f = strip[:, h % 2, 0:w]
                    return bass.AP(f.tensor, f.offset + w - 1, [list(f.ap[0]), [-1, w]])

                def take(g):
                    e.wait_ge(valued, 8 * g + 8)
                    e.tensor_copy(ao.rearrange("p t (h d) -> p h t d", d=HEAD)[:, 2 * g:2 * g + 2, :, :],
                                  ps[:, 4 + g % 2, :].rearrange("p (h t d) -> p h t d", h=2, t=T)).then_inc(taken_o, 1)

                for u in range(U):
                    h, t = u // T, u % T
                    w = (t + 1) * P
                    e.wait_ge(scored, u + 1)
                    if t == 0:
                        e.wait_ge(strip_in[h % 2], 32 * (h // 2 + 1))
                    if u >= 3:
                        e.wait_ge(turned, u - 2)
                    e.scalar_tensor_tensor(sc[:, u % 3, 0:w], ps[:, u % 2, 0:w], HEAD ** -0.5,
                                           backwards(h, w), ALU.mult, ALU.add).then_inc(read, 1)
                    e.wait_ge(read, u + 1)
                    e.tensor_reduce(neg[:, u:u + 1], sc[:, u % 3, 0:w], AX, ALU.max, negate=True).then_inc(maxed, 1)
                    if u >= 12 and (u - 12) % 8 == 0:
                        take((u - 12) // 8)
                take(7)
                e.wait_ge(expd, U)
                link(e.reciprocal(den, den))
                for t in range(T):
                    a3 = ao[:, t, :].rearrange("p (h d) -> p h d", d=HEAD)
                    if t == 0:
                        e.wait_ge(taken_o, 8)
                    e.tensor_tensor(a3, a3, bc(den.rearrange("p (h t) -> p h t", t=T)[:, :, t].unsqueeze(2), HEADS2, HEAD),
                                    ALU.mult)
            stage(pe=pe, act=act, dve=dve, pool=pool)
            return ao

        def output_stage(tag, src, h_at):
            turned, done, added = (sem(f"{tag}_{n}") for n in ("turned", "done", "added"))
            proj = Projection(0, 4, 8, h_at, done)

            def pe(e):
                for c in range(KC):
                    for t in range(T):
                        mm = e.transpose(ps[:, c, t * P:(t + 1) * P], src[:, t, c * P:(c + 1) * P], ident[:])
                    mm.then_inc(turned, 1)
                for q in range(proj.count):
                    proj.products(e, q, lambda g: e.wait_ge(added, g - 7) if g >= 8 else None)

            def act(e):
                proj.start_high(e, ps, turned)
                for q in range(2, proj.count):
                    proj.high(e, q)

            def dve(e):
                proj.start_low(e, ps)
                for g in range(16):
                    cs = slice(g // 4 * 2 * P, (g // 4 + 1) * 2 * P)
                    e.wait_ge(done, g + 1)
                    e.tensor_tensor(x[:, g % 4, cs], x[:, g % 4, cs], ps[:, g % 8, 0:2 * P], ALU.add).then_inc(added, 1)
                    if g % 4 == 3:
                        proj.low(e, g // 4 + 2)
            stage(pe=pe, act=act, dve=dve)

        def dn_in_stage():
            qT, at = area(0, DNH, S)
            kT, at = area(at, DNH, S)
            k_, at = area(at, T, D)
            v, at = area(at, T, D)
            z, at = area(at, T, D)
            PAD = TAPS2 - 1
            zin, at = area(at, 2, S + PAD)
            y, at = area(at, 2, S)
            vt, at_vt = area(at, 2, S)
            assert at_vt <= ARENA
            ab = small[:, 192:192 + 64].rearrange("p (t c) -> p t c", c=2 * DNH)
            done, freed, conved, silued, vturned, vcopied = (
                sem("dp_" + n) for n in ("done", "freed", "conved", "silued", "vturned", "vcopied"))
            abdone, abread = sem("dp_abdone"), sem("dp_abread")
            proj = Projection(12, 4, 6, 2 * DNH * S, done)

            def pe(e):
                def turn_v(c):
                    e.wait_ge(silued, 16 + c + 1)
                    if c >= 2:
                        e.wait_ge(vcopied, c - 1)
                    for t in range(T):
                        mm = e.transpose(ps[:, 6 + c % 2, t * P:(t + 1) * P], vt[:, c % 2, t * P:(t + 1) * P], ident[:])
                    mm.then_inc(vturned, 1)
                w = col("dn_ab").rearrange("p (k c) -> p k c", c=2 * DNH)
                for t in range(T):
                    for k in range(KC):
                        mm = e.matmul(ps[:, 7, t * 16:(t + 1) * 16], hT[:, k, t * P:(t + 1) * P], w[:, k, :],
                                      start=k == 0, stop=k == KC - 1)
                mm.then_inc(abdone, 1)

                def before(g):
                    if 19 <= g < 27:
                        turn_v(g - 19)
                    if g >= 6:
                        e.wait_ge(freed, g - 5)
                for q in range(proj.count):
                    proj.products(e, q, before)

            def dst(g):
                return qT[:, g, :] if g < 8 else kT[:, g - 8, :] if g < 16 else vt[:, g % 2, :]

            def act(e):
                proj.start_high(e)

                def silu(g):
                    e.wait_ge(conved, g + 1)
                    if g >= 18:
                        e.wait_ge(vturned, g - 17)
                    e.activation(dst(g), y[:, g % 2, :], ACT.Silu).then_inc(silued, 1)
                for g in range(24):
                    e.wait_ge(done, g + 1)
                    if g >= 2:
                        e.wait_ge(conved, g - 1)
                    e.activation(zin[:, g % 2, PAD:], ps[:, g % 6, :], ACT.Copy).then_inc(freed, 1)
                    if g % 2:
                        proj.high(e, g // 2 + 2)
                    if g:
                        silu(g - 1)
                silu(23)
                for g in range(24, 40):
                    i = (g - 24) // 4
                    e.wait_ge(done, g + 1)
                    e.activation(z[:, g % 4, i * 2 * P:(i + 1) * 2 * P], ps[:, g % 6, 0:2 * P],
                                 ACT.Silu).then_inc(freed, 1)
                    if g % 4 == 3:
                        proj.high(e, proj.last(g) + 2)

            def dve(e):
                link = chain(e, "dve_chain")
                link(e.memset(zin[:, :, 0:PAD], 0.0))
                e.wait_ge(abdone, 1)
                e.tensor_copy(ab, ps[:, 7, 0:64].rearrange("p (t c) -> p t c", c=16)).then_inc(abread, 1)
                proj.start_low(e)
                cw = col("dn_conv_w")

                def copy_v(c):
                    e.wait_ge(vturned, c + 1)
                    e.tensor_copy(v[:, :, c * P:(c + 1) * P],
                                  ps[:, 6 + c % 2, :].rearrange("p (t q) -> p t q", q=P)).then_inc(vcopied, 1)
                for g in range(24):
                    e.wait_ge(freed, g + 1)
                    if g >= 2:
                        e.wait_ge(silued, g - 1)
                    zi, yo = zin[:, g % 2, :], y[:, g % 2, :]
                    link(e.tensor_scalar(yo, zi[:, 0:S], cw[:, g:g + 1], None, ALU.mult))
                    for tap in range(1, TAPS2):
                        ins = e.scalar_tensor_tensor(yo, zi[:, tap:tap + S], cw[:, 24 * tap + g:24 * tap + g + 1], yo,
                                                     ALU.mult, ALU.add)
                        if tap < TAPS2 - 1:
                            link(ins)
                    ins.then_inc(conved, 1)
                    if g % 2:
                        proj.low(e, g // 2 + 2)
                    if g >= 20:
                        copy_v(g - 20)
                for c in range(4, 8):
                    copy_v(c)
                for q in range(14, proj.count):
                    proj.low(e, q)
            stage(pe=pe, act=act, dve=dve)
            return qT, kT, k_, v, z, ab, at

        G_, BETA, EGC, REST, BEGC, EGL, GC = (small[:, 256 + 32 * i:288 + 32 * i] for i in range(7))
        EGL2 = small[:, 480:512]

        def dn_unit_stage(qT, kT, k_, v, z, ab, at):
            sqb, at = area(at - 2 * S - 2 * (S + 3), 2, S)
            squared, summed, inverse, rooted, selected, spread, unit, turned = (
                sem("du_" + n) for n in ("sq", "sum", "inv", "root", "selected", "spread", "unit", "turned"))
            V = 2 * DNH
            spare = hT[:].rearrange("p k t -> p (k t)")
            sel = spare[:, 0:V * V].rearrange("p (n m) -> p n m", m=V)
            back = spare[0:V, V * V:V * V + V * P].rearrange("p (n m) -> p n m", m=P)
            rs = spare[0:V, V * V + V * P:V * V + V * P + S]
            vectors = [kT[:, c, :] for c in range(DNH)] + [qT[:, c, :] for c in range(DNH)]
            ready, logs, sums, gsum, acted = (sem("du_" + n) for n in ("ready", "logs", "sums", "gsum", "acted"))
            tmp = small[:, 0:64]
            t8 = "p (t h) -> p t h"

            def act(e):
                for n, src in enumerate(vectors):
                    if n >= 2:
                        e.wait_ge(summed, n - 1)
                    e.activation(sqb[:, n % 2, :], src, ACT.Square).then_inc(squared, 1)
                e.wait_ge(inverse, 1)
                e.activation(rs, rs, ACT.Sqrt).then_inc(rooted, 1)
                e.wait_ge(ready, 1)
                e.activation(tmp[:, 0:32], tmp[:, 0:32], ACT.Exp, scale=-1.0)
                e.activation(small[:, 64:72], row("a_log"), ACT.Exp).then_inc(acted, 1)
                e.wait_ge(acted, 1)
                e.activation(tmp[:, 0:32], tmp[:, 0:32], ACT.Ln, bias=1.0)
                e.activation(BETA.rearrange(t8, h=DNH), ab[:, :, DNH:], ACT.Sigmoid).then_inc(acted, 1)
                e.wait_ge(sums, 1)
                for src in (EGC, REST, EGL, EGL2):
                    last = e.activation(src, src, ACT.Exp)
                last.then_inc(acted, 1)

            def pe(e):
                e.wait_ge(selected, 1)
                for n in range(V):
                    e.wait_ge(squared, n + 1)
                    e.matmul(ps[0:V, 0, :], sel[:, n, :], sqb[:, n % 2, :], start=n == 0, stop=n == V - 1
                             ).then_inc(summed, 1)
                e.wait_ge(selected, 2)
                e.wait_ge(rooted, 1)
                for n in range(V):
                    if n >= 3:
                        e.wait_ge(unit, n - 2)
                    e.matmul(ps[:, 1 + n % 3, :], back[:, n, :], rs, start=True, stop=True).then_inc(spread, 1)
                    c = n - 3
                    if 0 <= c < DNH:
                        e.wait_ge(unit, c + 1)
                        if c >= 2:
                            e.wait_ge(turned, c - 1)
                        for t in range(T):
                            mm = e.transpose(ps[:, 4 + c % 2, t * P:(t + 1) * P], kT[:, c, t * P:(t + 1) * P],
                                             ident[:])
                        mm.then_inc(gsum, 1)
                e.wait_ge(logs, 1)
                e.matmul(ps[0:64, 6, 0:32], blk_tri[0:64, :], G_[0:64, :], start=True, stop=True)
                e.matmul(ps[64:128, 6, 0:32], blk_tri[64:128, :], G_[64:128, :], start=True, stop=True)
                e.matmul(ps[:, 6, 32:64], group64[:], G_, start=True, stop=True)
                e.matmul(ps[:, 6, 64:96], ones[0:64, :], G_[0:64, :], start=True, stop=True)
                e.matmul(ps[:, 7, 0:32], ones[64:128, :], G_[64:128, :], start=True, stop=True).then_inc(gsum, 1)

            def dve(e):
                link = chain(e, "dve_chain")
                e.tensor_tensor(sel, bc(iota[:, 0:V].unsqueeze(2), V, V), bc(iota[:, 0:V].unsqueeze(1), V, V),
                                ALU.is_equal).then_inc(selected, 1)
                e.tensor_scalar(back[:, 0:DNH, :], bc(ident[0:V, 0:DNH].unsqueeze(2), DNH, P), 1.0, None, ALU.mult)
                e.tensor_scalar(back[:, DNH:, :], bc(ident[0:V, DNH:V].unsqueeze(2), DNH, P), DH ** -0.5, None,
                                ALU.mult).then_inc(selected, 1)
                a3 = tmp[:, 32:64].rearrange(t8, h=DNH)
                link(e.tensor_tensor(a3, ab[:, :, 0:DNH], bc(row("dt_bias").unsqueeze(1), T, DNH), ALU.add))
                link(e.scalar_tensor_tensor(tmp[:, 0:32], tmp[:, 32:64], -1.0, tmp[:, 32:64], ALU.mult, ALU.max))
                e.tensor_scalar(tmp[:, 32:64], tmp[:, 32:64], 0.0, None, ALU.max).then_inc(ready, 1)
                e.wait_ge(summed, V)
                link(e.tensor_scalar(rs, ps[0:V, 0, :], EPS, None, ALU.add))
                e.reciprocal(rs, rs).then_inc(inverse, 1)
                for n, src in enumerate(vectors):
                    e.wait_ge(spread, n + 1)
                    e.tensor_tensor(src, src, ps[:, 1 + n % 3, :], ALU.mult).then_inc(unit, 1)
                    c = n - 4
                    if 0 <= c < DNH:
                        e.wait_ge(gsum, c + 1)
                        e.tensor_copy(k_[:, :, c * P:(c + 1) * P],
                                      ps[:, 4 + c % 2, :].rearrange("p (t q) -> p t q", q=P)).then_inc(turned, 1)
                e.wait_ge(acted, 2)
                link(e.tensor_tensor(tmp[:, 0:32], tmp[:, 0:32], tmp[:, 32:64], ALU.add))
                link(e.tensor_scalar(tmp[:, 0:32], tmp[:, 0:32], -1.0, None, ALU.mult))
                e.tensor_tensor(G_.rearrange(t8, h=DNH), tmp[:, 0:32].rearrange(t8, h=DNH),
                                bc(small[:, 64:72].unsqueeze(1), T, DNH), ALU.mult).then_inc(logs, 1)
                e.wait_ge(gsum, DNH + 1)
                link(e.tensor_copy(GC, ps[:, 6, 0:32]))
                e.tensor_copy(EGC, GC)
                e.tensor_copy(EGL, ps[:, 6, 64:96])
                e.tensor_copy(EGL2, ps[:, 7, 0:32])
                link(e.tensor_tensor(REST, ps[:, 6, 32:64], GC, ALU.subtract))
                e.sem_inc(sums, 1)
                e.wait_ge(acted, 3)
                link(e.tensor_tensor(BEGC, BETA, EGC, ALU.mult))
            stage(pe=pe, act=act, dve=dve)

        def dn_solve_stage(qT, kT, k_, v, z, ab, at):
            base = at - 2 * (S + 3) - 2 * S
            B4 = T * CHUNK
            mats = [area(base + hh * 6 * B4, 6, T, CHUNK)[0] for hh in range(2)]
            wide = [[area(base + hh * 6 * B4 + 2 * B4 * i, T, DH)[0] for i in range(3)] for hh in range(2)]
            qkT = gates.rearrange("p a b -> p (a b)").rearrange("p (h t c) -> p h t c", h=DNH, t=T)
            wT = hT
            DEC, QK, L, LT, X, XT = range(6)
            NP, ND, NA = 3 + 2 * (LEVELS - 1), 6 + 2 * (LEVELS - 1), 3
            pe_s, dve_s, act_s = sem("ds_pe"), sem("ds_dve"), sem("ds_act")
            halves = ((0, slice(0, 64)), (64, slice(64, 128)))

            def count(per, pair, step, hh):
                return pair * 2 * per + 2 * step + hh + 1

            def bank(hh, b):
                return ps[:, 4 * hh + b, :]

            def part(hh, b, half):
                return bank(hh, b)[:, half * B4:(half + 1) * B4].rearrange("p (t c) -> p t c", t=T)

            def pe(e):
                def blocks(out, lhs, rhs):
                    for t in range(T):
                        for _, sl in halves:
                            mm = e.matmul(out[sl, t, :], lhs(t, sl), rhs(t, sl), start=True, stop=True)
                    return mm

                def step(pair, n, hh):
                    h = 2 * pair + hh
                    m = mats[hh]
                    def wait_d(d):
                        e.wait_ge(dve_s, count(ND, pair, d, hh))

                    def tok(t, sl):
                        return slice(t * P + sl.start, t * P + sl.stop)
                    if n == 0:
                        wait_d(0)
                        if pair:
                            e.wait_ge(act_s, count(NA, pair - 1, 2, hh))
                        blocks(part(hh, 0, 0), lambda t, sl: ones[sl, 0:64], lambda t, sl: m[sl, L, t, :])
                        blocks(part(hh, 0, 1), lambda t, sl: kT[:, h, tok(t, sl)], lambda t, sl: kT[:, h, tok(t, sl)])
                        mm = blocks(part(hh, 1, 0), lambda t, sl: qT[:, h, tok(t, sl)],
                                    lambda t, sl: kT[:, h, tok(t, sl)])
                    elif n == 1:
                        wait_d(2)
                        blocks(part(hh, 2, 0), lambda t, sl: m[sl, L, t, :], lambda t, sl: ident[sl, sl])
                        mm = blocks(part(hh, 2, 1), lambda t, sl: m[sl, QK, t, :], lambda t, sl: ident[sl, sl])
                    elif n < NP - 1 and n % 2 == 0:
                        wait_d(3 + (n - 2))
                        mm = blocks(part(hh, 3, 0), lambda t, sl: m[sl, LT, t, :], lambda t, sl: m[sl, X, t, :])
                    elif n < NP - 1:
                        wait_d(3 + (n - 2))
                        blocks(part(hh, 0, 0), lambda t, sl: m[sl, XT, t, :], lambda t, sl: m[sl, DEC, t, :])
                        mm = blocks(part(hh, 0, 1), lambda t, sl: m[sl, DEC, t, :], lambda t, sl: m[sl, XT, t, :])
                    else:
                        wait_d(ND - 2)
                        kbe, vb = wide[hh][0], wide[hh][1]
                        for t in range(T):
                            for par, sl in enumerate((slice(0, 64), slice(64, 128))):
                                e.matmul(bank(hh, 1)[sl, t * P:(t + 1) * P], m[sl, XT, t, :], vb[sl, t, :],
                                         start=True, stop=True)
                                mm = e.matmul(bank(hh, 2 + par)[:, t * CHUNK:(t + 1) * CHUNK], kbe[sl, t, :], m[sl, XT, t, :],
                                              start=True, stop=True)
                    mm.then_inc(pe_s, 1)

                for pair in range(DNH // 2):
                    for n in range(NP):
                        for hh in range(2):
                            step(pair, n, hh)

            def act(e):
                for pair in range(DNH // 2):
                    for n in range(NA):
                        for hh in range(2):
                            h = 2 * pair + hh
                            m = mats[hh]
                            if n == 0:
                                e.wait_ge(dve_s, count(ND, pair, 1, hh))
                                e.activation(m[:, DEC], m[:, DEC], ACT.Exp, scale=-1.0).then_inc(act_s, 1)
                            elif n == 1:
                                e.wait_ge(pe_s, count(NP, pair, 1, hh))
                                e.activation(m[:, LT], part(hh, 2, 0), ACT.Copy)
                                e.activation(qkT[:, h, :, :], part(hh, 2, 1), ACT.Copy).then_inc(act_s, 1)
                            else:
                                e.wait_ge(pe_s, count(NP, pair, NP - 1, hh))
                                src = ps[:, 4 * hh + 2:4 * hh + 4, 0:B4].rearrange("p a (t c) -> p t a c", c=CHUNK)
                                e.activation(wT[:, h, :].rearrange("p (t a c) -> p t a c", t=T, a=2), src,
                                             ACT.Copy).then_inc(act_s, 1)

            def dve(e):
                link = chain(e, "dve_chain")
                t8 = "p (t h) -> p t h"

                def per_row(a, h, w):
                    return bc(a.rearrange(t8, h=DNH)[:, :, h:h + 1], T, w)

                def mask(m):
                    return bc(m.unsqueeze(1), T, CHUNK)

                def step(pair, n, hh):
                    h = 2 * pair + hh
                    m = mats[hh]
                    head = slice(h * DH, (h + 1) * DH)

                    def wait_p(p):
                        e.wait_ge(pe_s, count(NP, pair, p, hh))
                    if n == 0:
                        ins = e.tensor_tensor(m[:, L], mask(blk_tri[:]), per_row(G_, h, CHUNK), ALU.mult)
                    elif n == 1:
                        wait_p(0)
                        link(e.tensor_tensor(m[:, DEC], part(hh, 0, 0), per_row(GC, h, CHUNK), ALU.subtract))
                        ins = e.tensor_scalar(m[:, DEC], m[:, DEC], 0.0, None, ALU.max)
                    elif n == 2:
                        e.wait_ge(act_s, count(NA, pair, 0, hh))
                        link(e.tensor_tensor(m[:, DEC], m[:, DEC], mask(blk_incl[:]), ALU.mult))
                        e.tensor_tensor(m[:, QK], part(hh, 1, 0), m[:, DEC], ALU.mult)
                        link(e.tensor_tensor(m[:, L], part(hh, 0, 1), m[:, DEC], ALU.mult))
                        link(e.tensor_tensor(m[:, L], m[:, L], per_row(BETA, h, CHUNK), ALU.mult))
                        ins = e.tensor_tensor(m[:, L], m[:, L], mask(blk_strict[:]), ALU.mult)
                    elif n == 3:
                        e.wait_ge(act_s, count(NA, pair, 1, hh))
                        e.scalar_tensor_tensor(m[:, X], m[:, L], -1.0, mask(blk_low[:, 0, :]), ALU.mult, ALU.mult)
                        link(e.scalar_tensor_tensor(m[:, XT], m[:, LT], -1.0, mask(blk_low0[:]), ALU.mult, ALU.mult))
                        e.tensor_tensor(m[:, X], m[:, X], mask(blk_id[:]), ALU.add)
                        ins = e.tensor_tensor(m[:, XT], m[:, XT], mask(blk_id[:]), ALU.add)
                    elif n < ND - 2 and n % 2 == 0:
                        wait_p(n - 2)
                        ins = e.tensor_tensor(m[:, DEC], part(hh, 3, 0), mask(blk_low[:, (n - 2) // 2, :]), ALU.mult)
                    elif n < ND - 2:
                        wait_p(n - 2)
                        e.tensor_tensor(m[:, X], m[:, X], part(hh, 0, 0), ALU.subtract)
                        ins = e.tensor_tensor(m[:, XT], m[:, XT], part(hh, 0, 1), ALU.subtract)
                    elif n == ND - 2:
                        kbe, vb = wide[hh][0], wide[hh][1]
                        e.tensor_tensor(vb, v[:, :, head], per_row(BETA, h, DH), ALU.mult)
                        link(e.tensor_tensor(kbe, k_[:, :, head], per_row(BEGC, h, DH), ALU.mult))
                        ins = e.tensor_tensor(k_[:, :, head], k_[:, :, head], per_row(REST, h, DH), ALU.mult)
                    else:
                        wait_p(NP - 1)
                        ins = e.tensor_copy(v[:, :, head], bank(hh, 1).rearrange("p (t c) -> p t c", t=T))
                    ins.then_inc(dve_s, 1)
                    e.wait_ge(dve_s, count(ND, pair, n, hh))

                for pair in range(DNH // 2):
                    for n in range(ND):
                        for hh in range(2):
                            step(pair, n, hh)
            stage(pe=pe, act=act, dve=dve)
            return qkT, wT

        def dn_scan_stage(qT, kT, k_, v, z, ab, at, qkT, wT):
            o = kT.rearrange("p h s -> p (h s)").rearrange("p (t d) -> p t d", t=T)
            base = at - 2 * (S + 3) - 2 * S
            state, p1 = area(base, DNH, DH)
            fresh, p1 = area(p1, DNH, DH)
            old, p1 = area(p1, DNH, DH)
            NCH = S // CHUNK
            begun, stated, freshed, second, decayed, outs, zero = (
                sem("dc_" + n) for n in ("begun", "state", "fresh", "second", "decayed", "out", "zero"))

            def row_of(c):
                return c // 2, slice(64 * (c % 2), 64 * (c % 2) + 64)

            def egl(c):
                return (EGL, EGL2)[c % 2].rearrange("p (t h) -> p t h", h=DNH)[:, c // 2, :]

            def pool(e):
                e.memset(state, 0.0).then_inc(zero, 1)
                for c in range(NCH):
                    if c == 0:
                        e.wait_ge(zero, 1)
                    else:
                        e.wait_ge(stated, c)
                    e.tensor_tensor(old, state, bc(egl(c).unsqueeze(2), DNH, DH), ALU.mult).then_inc(decayed, 1)

            def pe(e):
                for c in range(NCH):
                    t, sl = row_of(c)
                    cs = slice(c * CHUNK, (c + 1) * CHUNK)
                    if c == 0:
                        e.wait_ge(zero, 1)
                    else:
                        e.wait_ge(stated, c)
                        e.wait_ge(outs, c)
                    for h in range(DNH):
                        mm = e.matmul(ps[sl, h // 4, (h % 4) * DH:(h % 4 + 1) * DH], wT[:, h, cs], state[:, h, :],
                                      start=True, stop=True)
                    mm.then_inc(begun, 1)
                    for h in range(DNH):
                        mm = e.matmul(ps[sl, 2 + h // 4, (h % 4) * DH:(h % 4 + 1) * DH], qT[:, h, cs], state[:, h, :],
                                      start=True, stop=True)
                    e.wait_ge(freshed, c + 1)
                    for h in range(DNH):
                        mm = e.matmul(ps[:, 6 + h // 4, (h % 4) * DH:(h % 4 + 1) * DH],
                                      k_[sl, t, h * DH:(h + 1) * DH], fresh[sl, h, :], start=True, stop=True)
                    mm.then_inc(second, 1)
                    for h in range(DNH):
                        mm = e.matmul(ps[sl, 4 + h // 4, (h % 4) * DH:(h % 4 + 1) * DH], qkT[sl, h, t, :],
                                      fresh[sl, h, :], start=True, stop=True)
                    mm.then_inc(second, 1)

            def dve(e):
                link = chain(e, "dve_chain")
                e.wait_ge(zero, 1)
                for c in range(NCH):
                    t, sl = row_of(c)

                    def wide(a):
                        return a.rearrange("p b (h d) -> p (b h) d", d=DH)
                    e.wait_ge(begun, c + 1)
                    e.tensor_tensor(fresh[sl, :, :], v[sl, t, :].rearrange("p (h d) -> p h d", d=DH),
                                    wide(ps[sl, 0:2, :]), ALU.subtract).then_inc(freshed, 1)
                    e.wait_ge(second, 2 * c + 1)
                    e.wait_ge(decayed, c + 1)
                    e.tensor_tensor(state, old, wide(ps[:, 6:8, :]), ALU.add).then_inc(stated, 1)
                    e.wait_ge(second, 2 * c + 2)
                    ov = o[sl, t, :].rearrange("p (h d) -> p h d", d=DH)
                    eg = EGC.rearrange("p (t h) -> p t h", h=DNH)[sl, t, :]
                    link(e.tensor_tensor(ov, wide(ps[sl, 2:4, :]), bc(eg.unsqueeze(2), DNH, DH), ALU.mult))
                    e.tensor_tensor(ov, ov, wide(ps[sl, 4:6, :]), ALU.add).then_inc(outs, 1)
            stage(pe=pe, dve=dve, pool=pool)
            return o

        def dn_out_stage(o, z, at):
            base = at - 2 * (S + 3) - 2 * S
            sq, _ = area(base, 2, D)
            ss, rs = small[:, 0:32], small[:, 32:64]
            squared, summed, inverse, rooted = (sem("do_" + n) for n in ("sq", "sum", "inv", "root"))

            def act(e):
                for t in range(T):
                    if t >= 2:
                        e.wait_ge(summed, t - 1)
                    e.activation(sq[:, t % 2, :], o[:, t, :], ACT.Square).then_inc(squared, 1)
                e.wait_ge(inverse, 1)
                e.activation(rs, rs, ACT.Sqrt).then_inc(rooted, 1)

            def dve(e):
                link = chain(e, "dve_chain")
                for t in range(T):
                    e.wait_ge(squared, t + 1)
                    e.tensor_reduce(ss[:, t * DNH:(t + 1) * DNH], sq[:, t % 2, :].rearrange("p (h d) -> p h d", d=DH),
                                    AX, ALU.add).then_inc(summed, 1)
                e.wait_ge(summed, T)
                link(e.tensor_scalar(rs, ss, 1.0 / DH, EPS, ALU.mult, ALU.add))
                e.reciprocal(rs, rs).then_inc(inverse, 1)
                for t in range(T):
                    z3 = z[:, t, :].rearrange("p (h d) -> p h d", d=DH)
                    last = e.tensor_tensor(z3, z3, bc(row("head_norm").unsqueeze(1), DNH, DH), ALU.mult)
                link(last)
                e.wait_ge(rooted, 1)
                for t in range(T):
                    o3 = o[:, t, :].rearrange("p (h d) -> p h d", d=DH)
                    last = e.tensor_tensor(o3, o3, bc(rs[:, t * DNH:(t + 1) * DNH].unsqueeze(2), DNH, DH), ALU.mult)
                link(last)
                for t in range(T):
                    e.tensor_tensor(o[:, t, :], o[:, t, :], z[:, t, :], ALU.mult)
            stage(act=act, dve=dve)

        def final_stage():
            y, at = area(0, T, D)
            frow, at = area(at, D)
            ss, rs = small[:, 0:T], small[:, T:2 * T]
            squared, inverse, rooted, ready = (sem("fi_" + n) for n in ("sq", "inv", "root", "ready"))

            def act(e):
                e.dma_start(frow, A["final_norm"].partition_broadcast(P)).then_inc(loaded, 16)
                for t in range(T):
                    e.activation(y[:, t, :], x[:, t, :], ACT.Square, accum_out=ss[:, t:t + 1]).then_inc(squared, 1)
                e.wait_ge(inverse, 1)
                e.activation(rs, rs, ACT.Sqrt).then_inc(rooted, 1)
                for t in range(T):
                    e.wait_ge(ready, t + 1)
                    e.dma_start(out[t * P:(t + 1) * P, :], y[:, t, :]).then_inc(stored, 16)
                e.wait_ge(stored, 16 * T)

            def dve(e):
                link = chain(e, "dve_chain")
                e.wait_ge(loaded, 128)
                e.wait_ge(squared, T)
                link(e.tensor_scalar(rs, ss, 1.0 / D, EPS, ALU.mult, ALU.add))
                e.reciprocal(rs, rs).then_inc(inverse, 1)
                e.wait_ge(rooted, 1)
                for t in range(T):
                    e.scalar_tensor_tensor(y[:, t, :], x[:, t, :], rs[:, t:t + 1], frow, ALU.mult,
                                           ALU.mult).then_inc(ready, 1)
            stage(act=act, dve=dve)

        ada_stage()
        norm_stage("n1", mod1, ada[:, 0:KC])
        a = in_stage()
        mix_stage(*a)
        residual_stage("wo1", gate1, A["b_out"])
        norm_stage("n2", mod2, ada[:, 3 * KC:4 * KC])
        egT = route_stage()
        gate_stage(egT)
        acc = feed_stage(ECH, True)
        close_stage(acc)
        norm_stage("n3", col("attn_norm"))
        ao = attention_stage()
        output_stage("wo2", ao, T * D)
        norm_stage("n4", col("mlp_norm0"))
        feed_stage(MLP_CH, False)
        norm_stage("n5", col("dn_norm"))
        dn = dn_in_stage()
        dn_unit_stage(*dn)
        qk = dn_solve_stage(*dn)
        o = dn_scan_stage(*dn, *qk)
        dn_out_stage(o, dn[4], dn[6])
        output_stage("wo3", o, 0)
        norm_stage("n6", col("mlp_norm1"))
        feed_stage(MLP_CH, False)
        final_stage()

        block = ctx.enter_context(nc.Block())

        def between(e, n):
            e.drain().then_inc(stage_done, 1)
            e.wait_ge(stage_done, 4 * (n + 1))

        @block.sync
        def _(e):
            full, part = 0, 0
            for n, (at, count, _) in enumerate(loads):
                halved = loads[n][2] is not None
                if n and halved != (loads[n - 1][2] is not None):
                    e.wait_ge(slab_used, at)
                    if not halved:
                        e.wait_ge(*loads[n - 1][2])
                if halved:
                    for b in range(RING):
                        if not (n and loads[n - 1][2] is None):
                            e.wait_ge(slab_used, at + b - RING + 1)
                        e.dma_start(half(at + b), A["halves"][part + b]).then_inc(slab_in[(at + b) % RING], 16)
                    if count > RING:
                        with e.Fori(0, count // RING - 1) as m:
                            for b in range(RING):
                                e.wait_ge(slab_used, m * RING + (at + b + 1))
                                e.dma_start(half(at + b),
                                            A["halves"][bass.ds(m * RING + (part + RING + b), 1)].rearrange(
                                                "o p n -> p (o n)")).then_inc(slab_in[(at + b) % RING], 16)
                    part += count
                    continue
                for i in range(at, at + count):
                    if i >= RING:
                        e.wait_ge(slab_used, i - RING + 1)
                    e.dma_start(slab(i), A["stream"][full + i - at]).then_inc(slab_in[i % RING], 16)
                full += count

        @block.tensor
        def _(e):
            for n, s in enumerate(stages):
                if "pe" in s:
                    s["pe"](e)
                between(e, n)

        @block.scalar
        def _(e):
            for n, s in enumerate(stages):
                if "act" in s:
                    s["act"](e)
                between(e, n)

        @block.vector
        def _(e):
            for n, s in enumerate(stages):
                if "dve" in s:
                    s["dve"](e)
                between(e, n)

        @block.gpsimd
        def _(e):
            for n, s in enumerate(stages):
                if "pool" in s:
                    s["pool"](e)
                between(e, n)


def layout(inp):
    def colv(a):
        return np.asarray(a).reshape(-1, P).T

    def slabs(w, width=N):
        w = np.asarray(w)
        n = w.shape[1] // width
        return w.reshape(KC, P, n, width).transpose(2, 1, 0, 3).reshape(n, P, KC * width)

    g = {k: np.asarray(v) for k, v in inp.items()}
    heads = [h for c in range(4) for h in (c, c + 4)]
    perm = np.concatenate([np.arange(h * HEAD, (h + 1) * HEAD) for h in heads] + [np.arange(AW, g["w_in"].shape[1])])
    w_in, b_in = g["w_in"][:, perm], g["b_in"][perm]
    kv = np.zeros((1, P, SLAB), np.float32)
    kv[:, :, :KC * 256] = slabs(w_in[:, AW:AW + 256], 256)
    keys = np.stack([g["peer_keys1"], g["peer_keys2"]], 1).transpose(3, 0, 1, 2).reshape(P, 16 * KEYS)
    u = g["peer_u"].reshape(KEYS, ECH, 2, 2, KC, P).transpose(1, 2, 5, 4, 3, 0).reshape(ECH, 2, P, HALF)
    v = g["peer_v"].reshape(KEYS, ECH, E2C, 2, N).transpose(1, 3, 0, 2, 4).reshape(ECH, 2, P, HALF)

    def feed(u, v):
        order = [u[0]] + [h for c in range(1, len(u)) for h in (u[c], v[c - 1])] + [v[-1]]
        return np.concatenate(order)

    def mlp(i):
        up = slabs(g["mlp_w_up_2"][i], 2 * P).reshape(MLP_CH, 2, P, HALF)
        down = g["mlp_w_down_2"][i].reshape(MLP_CH, N // P, P, 2, N).transpose(0, 3, 2, 1, 4)
        return feed(up, down.reshape(MLP_CH, 2, P, HALF))

    dn = g["dn_w_in_2"][0]
    parts = [slabs(g["w_ada"]), slabs(w_in[:, :AW]), kv, slabs(w_in[:, AW + 256:]), slabs(g["w_out"]),
             slabs(g["w_query"])]
    halves = [feed(u, v), slabs(g["attn_w_qkv_2"][0], 2 * P), slabs(g["attn_w_o_2"][0], 2 * P), mlp(0),
              slabs(dn[:, :4 * D], 2 * P), slabs(g["dn_w_o_2"][0], 2 * P), mlp(1)]
    ab = dn[:, 4 * D:].reshape(KC, P, 2 * DNH).transpose(1, 0, 2).reshape(P, -1)
    cv = {"c": colv(g["c"]), "b_ada": colv(g["b_ada"]), "norm1_g": colv(g["norm1_g"]), "b_in": colv(b_in),
          "conv_w": colv(g["conv_w"]), "conv_out_g": colv(g["conv_out_g"]), "norm2_g": colv(g["norm2_g"]),
          "attn_norm": colv(g["attn_norm_2"]), "mlp_norm0": colv(g["mlp_norm_2"][0]),
          "mlp_norm1": colv(g["mlp_norm_2"][1]), "dn_norm": colv(g["dn_norm_2"]),
          "dn_conv_w": colv(g["dn_conv_w_2"]), "dn_ab": ab}
    rv = {"b_v": g["b_in"][AW + P:AW + 2 * P], "attn_out_g": g["attn_out_g"], "sinks": g["attn_sinks"],
          "head_norm": g["dn_head_norm_2"][0], "dt_bias": g["dn_dt_bias_2"][0], "a_log": g["dn_a_log_2"][0]}
    rb = g["attn_rel_bias_2"][0]
    rel = np.concatenate([rb[:, MAX_REL - P + 1:], np.repeat(rb[:, -1:], S - 1 - MAX_REL, 1)], 1)
    return {
        "keys": keys, "stream": np.concatenate(parts), "halves": np.concatenate([h.reshape(-1, P, HALF) for h in halves]),
        "cols": np.concatenate([cv[n] for n in COLS], 1),
        "rows": np.concatenate([rv[n] for n in ROWS]), "b_gate1": g["b_ada"][2 * D:3 * D],
        "b_gate2": g["b_ada"][5 * D:], "b_out": g["b_out"], "final_g": g["final_g"],
        "final_norm": g["final_norm_2"], "rel": rel, "x": g["x"].reshape(T, P, D).transpose(1, 0, 2),
    }


def kernel(**inputs):
    import concourse.bacc as bacc
    from concourse.bass_utils import run_bass_kernel_spmd

    nc = bacc.Bacc("TRN2", target_bir_lowering=False, num_devices=1)
    arrays = {name: np.ascontiguousarray(a) for name, a in layout(inputs).items()}
    handles = {name: nc.dram_tensor(name, a.shape, mybir.dt.from_np(a.dtype), kind="ExternalInput").ap()
               for name, a in arrays.items()}
    out = nc.dram_tensor("out", (S, D), F32, kind="ExternalOutput").ap()
    program(nc, handles, out)
    result = run_bass_kernel_spmd(nc, [arrays], core_ids=[0])
    return result.results[0]["out"].reshape(1, S, D)
```
